# Optimizing a Trainium2 kernel written in Bass

```python
import jax, jax.numpy as jnp
from jax import lax
import numpy as np

D_MODEL = 1024
BATCH = 1
SEQ = 2048
DEPTH = 1
DEC_BATCH = 8
DEC_SEQ = 1
PAST_LEN = 4096
PAGE_SIZE = 128

HEAD_DIM = 64
CONV_WIDTH = D_MODEL // 4
CONV_K = 3
FOX_WIDTH = D_MODEL // 2
FOX_HEADS = FOX_WIDTH // HEAD_DIM
MEM_WIDTH = D_MODEL // 4
MEM_HEADS = MEM_WIDTH // HEAD_DIM
MEM_LEN = 256
MIX_WIDTH = CONV_WIDTH + FOX_WIDTH + MEM_WIDTH
D_FF = -(-8 * D_MODEL // (3 * 256)) * 256
Q_BLOCK = 128
EPS = 1e-6
IN_SIZES = (CONV_WIDTH, CONV_WIDTH, CONV_WIDTH, FOX_WIDTH, FOX_WIDTH, FOX_WIDTH, FOX_HEADS, MEM_WIDTH)
IN_WIDTH = sum(IN_SIZES)

kernel_name = "hymba_conv_fox_memory_decode_step"

def _normalize(x):
    xf = x.astype(jnp.float32)
    return xf * lax.rsqrt(jnp.mean(xf * xf, axis=-1, keepdims=True) + EPS)

def rmsnorm(x, g):
    return (_normalize(x) * g.astype(jnp.float32)).astype(x.dtype)

def split_proj(h, w_in, b_f):
    p = h @ w_in
    offs = [int(o) for o in np.cumsum(IN_SIZES)[:-1]]
    b_c, c_c, h_c, q, k, v, f_logit, q_m = jnp.split(p, offs, axis=-1)
    B, T = h.shape[0], h.shape[1]
    q = q.reshape(B, T, FOX_HEADS, HEAD_DIM)
    k = k.reshape(B, T, FOX_HEADS, HEAD_DIM)
    v = v.reshape(B, T, FOX_HEADS, HEAD_DIM)
    q_m = q_m.reshape(B, T, MEM_HEADS, HEAD_DIM)
    logf = jax.nn.log_sigmoid((f_logit + b_f).astype(jnp.float32))
    return b_c, c_c, h_c, q, k, v, logf, q_m

def causal_conv(buf, conv_w, n_out):
    out = conv_w[0] * buf[:, 0:n_out]
    for i in range(1, CONV_K):
        out = out + conv_w[i] * buf[:, i:i + n_out]
    return out

def fox_prompt(q, k, v, logf):
    B, S, H, Dh = q.shape
    scale = Dh ** -0.5
    c = jnp.cumsum(logf, axis=1)
    ck = jnp.transpose(c, (0, 2, 1))
    n_blk = S // Q_BLOCK
    qb = q.reshape(B, n_blk, Q_BLOCK, H, Dh).transpose(1, 0, 2, 3, 4)
    cqb = ck.reshape(B, H, n_blk, Q_BLOCK).transpose(2, 0, 1, 3)
    kpos = jnp.arange(S)

    def block(args):
        qi, cqi, bi = args
        s = jnp.einsum('bqhd,bkhd->bhqk', qi, k).astype(jnp.float32) * scale
        s = s + cqi[..., :, None] - ck[:, :, None, :]
        qpos = bi * Q_BLOCK + jnp.arange(Q_BLOCK)
        mask = kpos[None, :] <= qpos[:, None]
        p = jax.nn.softmax(jnp.where(mask, s, -jnp.inf), axis=-1)
        return jnp.einsum('bhqk,bkhd->bqhd', p.astype(v.dtype), v)

    o = lax.map(block, (qb, cqb, jnp.arange(n_blk)))
    return o.transpose(1, 0, 2, 3, 4).reshape(B, S, H * Dh)

def fox_sample(q, k_new, v_new, logf_new, k_past, v_past, logf_past):
    B, T, H, Dh = q.shape
    P = k_past.shape[1]
    scale = Dh ** -0.5
    k_all = jnp.concatenate([k_past.astype(k_new.dtype), k_new], axis=1)
    v_all = jnp.concatenate([v_past.astype(v_new.dtype), v_new], axis=1)
    lf_all = jnp.concatenate([logf_past.astype(jnp.float32), logf_new], axis=1)
    c = jnp.transpose(jnp.cumsum(lf_all, axis=1), (0, 2, 1))
    cq = c[:, :, P:]
    s = jnp.einsum('bqhd,bkhd->bhqk', q, k_all).astype(jnp.float32) * scale
    s = s + cq[..., :, None] - c[:, :, None, :]
    kpos = jnp.arange(P + T)
    qpos = P + jnp.arange(T)
    mask = kpos[None, :] <= qpos[:, None]
    p = jax.nn.softmax(jnp.where(mask, s, -jnp.inf), axis=-1)
    o = jnp.einsum('bhqk,bkhd->bqhd', p.astype(v_all.dtype), v_all)
    return o.reshape(B, T, H * Dh)

def mem_attention(q_m, mem_k, mem_v):
    B, T = q_m.shape[0], q_m.shape[1]
    s = jnp.einsum('bqhd,bmhd->bhqm', q_m, mem_k.astype(q_m.dtype)).astype(jnp.float32) * (HEAD_DIM ** -0.5)
    p = jax.nn.softmax(s, axis=-1)
    o = jnp.einsum('bhqm,bmhd->bqhd', p.astype(q_m.dtype), mem_v.astype(q_m.dtype))
    return o.reshape(B, T, MEM_WIDTH)

def mem_kv(mem, mem_norm_g, w_mem_kv):
    kv = rmsnorm(mem, mem_norm_g) @ w_mem_kv
    mk, mv = jnp.split(kv, [MEM_WIDTH], axis=-1)
    B = mem.shape[0]
    return mk.reshape(B, MEM_LEN, MEM_HEADS, HEAD_DIM), mv.reshape(B, MEM_LEN, MEM_HEADS, HEAD_DIM)

def mix_out(y_conv, y_fox, y_mem, out_norm_g, w_out):
    y = jnp.concatenate([_normalize(y_conv), _normalize(y_fox), _normalize(y_mem)], axis=-1)
    y = (y * out_norm_g.astype(jnp.float32)).astype(y_conv.dtype)
    return y @ w_out

def swiglu(h, w_gate, w_up, w_down):
    return (jax.nn.silu(h @ w_gate) * (h @ w_up)) @ w_down

def setup_inputs(seed: int = 0) -> dict:
    key = jax.random.key(seed)
    ks = jax.random.split(key, 24)
    n_pages = PAST_LEN // PAGE_SIZE
    n_pool = (DEC_BATCH * n_pages * 5) // 4
    f32 = jnp.float32
    nrm = lambda k, shape, s=1.0: jax.random.normal(k, shape, f32) * s
    page_table = jax.random.permutation(ks[0], n_pool)[:DEC_BATCH * n_pages].reshape(DEC_BATCH, n_pages).astype(jnp.int32)
    return {
        "x_prompt": nrm(ks[1], (BATCH, SEQ, D_MODEL)),
        "x_sample": nrm(ks[2], (DEC_BATCH, DEC_SEQ, D_MODEL)),
        "mem_prompt": nrm(ks[3], (BATCH, MEM_LEN, D_MODEL)),
        "cache_k": nrm(ks[4], (DEPTH, n_pool, PAGE_SIZE, FOX_HEADS, HEAD_DIM)),
        "cache_v": nrm(ks[5], (DEPTH, n_pool, PAGE_SIZE, FOX_HEADS, HEAD_DIM)),
        "cache_logf": jax.nn.log_sigmoid(2.0 + nrm(ks[6], (DEPTH, n_pool, PAGE_SIZE, FOX_HEADS), 1.0)),
        "state_conv": nrm(ks[7], (DEPTH, DEC_BATCH, CONV_K - 1, CONV_WIDTH)),
        "cache_mem_k": nrm(ks[8], (DEPTH, DEC_BATCH, MEM_LEN, MEM_HEADS, HEAD_DIM)),
        "cache_mem_v": nrm(ks[9], (DEPTH, DEC_BATCH, MEM_LEN, MEM_HEADS, HEAD_DIM)),
        "page_table": page_table,
        "norm1_g": 1.0 + nrm(ks[10], (DEPTH, D_MODEL), 0.1),
        "w_in": nrm(ks[11], (DEPTH, D_MODEL, IN_WIDTH), D_MODEL ** -0.5),
        "b_f": 2.0 + nrm(ks[12], (DEPTH, FOX_HEADS), 0.5),
        "conv_w": nrm(ks[13], (DEPTH, CONV_K, CONV_WIDTH), CONV_K ** -0.5),
        "mem_norm_g": 1.0 + nrm(ks[14], (DEPTH, D_MODEL), 0.1),
        "w_mem_kv": nrm(ks[15], (DEPTH, D_MODEL, 2 * MEM_WIDTH), D_MODEL ** -0.5),
        "out_norm_g": 1.0 + nrm(ks[16], (DEPTH, MIX_WIDTH), 0.1),
        "w_out": nrm(ks[17], (DEPTH, MIX_WIDTH, D_MODEL), MIX_WIDTH ** -0.5),
        "norm2_g": 1.0 + nrm(ks[18], (DEPTH, D_MODEL), 0.1),
        "w_gate": nrm(ks[19], (DEPTH, D_MODEL, D_FF), D_MODEL ** -0.5),
        "w_up": nrm(ks[20], (DEPTH, D_MODEL, D_FF), D_MODEL ** -0.5),
        "w_down": nrm(ks[21], (DEPTH, D_FF, D_MODEL), D_FF ** -0.5),
        "final_norm_g": 1.0 + nrm(ks[22], (D_MODEL,), 0.1),
    }

def reference(x_prompt, x_sample, mem_prompt, cache_k, cache_v, cache_logf, state_conv, cache_mem_k, cache_mem_v,
              page_table, norm1_g, w_in, b_f, conv_w, mem_norm_g, w_mem_kv, out_norm_g, w_out, norm2_g,
              w_gate, w_up, w_down, final_norm_g):
    xp, xs = x_prompt, x_sample
    n_past = page_table.shape[1] * cache_k.shape[2]
    nk_p, nv_p, nlf_p, nconv_p, nmk_p, nmv_p = [], [], [], [], [], []
    nk_s, nv_s, nlf_s, nconv_s = [], [], [], []
    for l in range(DEPTH):
        hp = rmsnorm(xp, norm1_g[l])
        b_c, c_c, h_c, q, k, v, logf, q_m = split_proj(hp, w_in[l], b_f[l])
        u = c_c * h_c
        buf = jnp.pad(u, ((0, 0), (CONV_K - 1, 0), (0, 0)))
        y_conv = b_c * causal_conv(buf, conv_w[l], xp.shape[1])
        y_fox = fox_prompt(q, k, v, logf)
        mk, mv = mem_kv(mem_prompt, mem_norm_g[l], w_mem_kv[l])
        y_mem = mem_attention(q_m, mk, mv)
        xp = xp + mix_out(y_conv, y_fox, y_mem, out_norm_g[l], w_out[l])
        xp = xp + swiglu(rmsnorm(xp, norm2_g[l]), w_gate[l], w_up[l], w_down[l])
        nk_p.append(k); nv_p.append(v); nlf_p.append(logf)
        nconv_p.append(buf[:, -(CONV_K - 1):]); nmk_p.append(mk); nmv_p.append(mv)

        hs = rmsnorm(xs, norm1_g[l])
        b_c, c_c, h_c, q, k, v, logf, q_m = split_proj(hs, w_in[l], b_f[l])
        u = c_c * h_c
        buf = jnp.concatenate([state_conv[l].astype(u.dtype), u], axis=1)
        y_conv = b_c * causal_conv(buf, conv_w[l], xs.shape[1])
        k_past = cache_k[l, page_table].reshape(xs.shape[0], n_past, FOX_HEADS, HEAD_DIM)
        v_past = cache_v[l, page_table].reshape(xs.shape[0], n_past, FOX_HEADS, HEAD_DIM)
        lf_past = cache_logf[l, page_table].reshape(xs.shape[0], n_past, FOX_HEADS)
        y_fox = fox_sample(q, k, v, logf, k_past, v_past, lf_past)
        y_mem = mem_attention(q_m, cache_mem_k[l], cache_mem_v[l])
        xs = xs + mix_out(y_conv, y_fox, y_mem, out_norm_g[l], w_out[l])
        xs = xs + swiglu(rmsnorm(xs, norm2_g[l]), w_gate[l], w_up[l], w_down[l])
        nk_s.append(k); nv_s.append(v); nlf_s.append(logf); nconv_s.append(buf[:, -(CONV_K - 1):])

    y_prompt = rmsnorm(xp, final_norm_g)
    y_sample = rmsnorm(xs, final_norm_g)
    return (y_prompt, y_sample,
            jnp.stack(nk_p), jnp.stack(nv_p), jnp.stack(nlf_p), jnp.stack(nconv_p),
            jnp.stack(nmk_p), jnp.stack(nmv_p),
            jnp.stack(nk_s), jnp.stack(nv_s), jnp.stack(nlf_s), jnp.stack(nconv_s))


_drawn_inputs = setup_inputs


def setup_inputs(seed=0):
    import zlib

    import numpy as np

    out = dict(_drawn_inputs(seed))
    spreads = {}
    factors = {}
    for name, (base, spread) in spreads.items():
        noise = np.random.default_rng([zlib.crc32(name.encode()), seed]).standard_normal(out[name].shape)
        drawn = base * np.exp(spread * noise) if base else spread * noise
        out[name] = __import__('jax').numpy.asarray(drawn.astype(out[name].dtype))
    for name, factor in factors.items():
        out[name] = (out[name] * factor).astype(out[name].dtype)
    return out
```

```python
from collections import namedtuple
from contextlib import ExitStack, contextmanager

import concourse.bass as bass
from concourse import mybir

F32 = mybir.dt.float32
F32R = mybir.dt.float32r
I32 = mybir.dt.int32
U32 = mybir.dt.uint32
ALU = mybir.AluOpType
ACT = mybir.ActivationFunctionType
AX = mybir.AxisListType
RMAX = bass.bass_isa.ReduceOp.max
RADD = bass.bass_isa.ReduceOp.add
ds = bass.ds

P = 128
D = 1024
SEQ = 2048
HD = 64
CW = 256
FW = 512
MW = 256
FH = FW // HD
MH = MW // HD
MEM = 256
DB = 8
PAGES = 32
D_FF = 2816
DT = D // P
NT = SEQ // P
QCH = 4
FT = D_FF // P
EPS = 1e-6
SCALE = HD ** -0.5
NEG = -1.0e30
BIG = 3.0e38
BLK = 512
NBLK = 5
HALF = 8
PAD = 2
QCOL = 3 * CW
KCOL = QCOL + FW
VCOL = KCOL + FW
FCOL = VCOL + FW
MCOL = FCOL
PW = NBLK * BLK


def group(**things):
    return namedtuple("group", list(things))(**things)


class Steps:

    def __init__(self):
        self.score = self.turn = self.pv = self.page = self.scored = self.joined = 0
        self.uses = []


@contextmanager
def stage(nc, names):
    with ExitStack() as ctx:
        sems = [ctx.enter_context(nc.semaphore(n)) for n in names.split()]
        with nc.Block() as block:
            yield block, group(**dict(zip(names.split(), sems)))
        numbers = sorted(s.num for s in sems)
        starts = [n for n in numbers if n - 1 not in numbers]
        for n0 in starts:
            n1 = n0
            while n1 in numbers:
                n1 += 1
            nc.sync.sem_clear(range(n0, n1))
        nc.all_engine_barrier()


SERIAL = [0]


def alloc(ctx, nc):
    def own_name(name):
        SERIAL[0] += 1
        return f"{name}_{SERIAL[0]}"

    def sb(name, shape, dt=F32):
        return ctx.enter_context(nc.sbuf_tensor(own_name(name), shape, dt))

    def ps(name, shape, dt=F32):
        return ctx.enter_context(nc.psum_tensor(own_name(name), shape, dt))

    return sb, ps


def setup_constants(nc, c, io):
    with ExitStack() as ctx:
        sb, _ = alloc(ctx, nc)
        causal = sb("causal", [P, P])
        with stage(nc, "filled ready loaded") as (block, s):

            @block.gpsimd
            def _(pool):
                pool.memset(c.ident[:], 0.0).then_inc(s.filled, 1)
                pool.memset(causal[:], 0.0).then_inc(s.filled, 1)
                pool.memset(c.page_before[:], 1.0).then_inc(s.filled, 1)
                pool.memset(c.own_head[:], 1.0).then_inc(s.filled, 1)
                pool.memset(c.seq_of_page[:], 0.0).then_inc(s.filled, 1)
                pool.memset(c.ones[:], 1.0).then_inc(s.filled, 1)
                pool.memset(c.minus_half[:], -0.5).then_inc(s.filled, 1)
                pool.wait_ge(s.filled, 7)
                pool.affine_select(out=c.ident[:], in_=c.ident[:], compare_op=ALU.not_equal, fill=1.0, base=0,
                                   pattern=[[-1, P]], channel_multiplier=1).then_inc(s.ready, 1)
                pool.affine_select(out=causal[:], in_=causal[:], compare_op=ALU.is_ge, fill=NEG, base=0,
                                   pattern=[[-1, P]], channel_multiplier=1).then_inc(s.ready, 1)
                pool.affine_select(out=c.page_before[:], in_=c.page_before[:], compare_op=ALU.is_gt, fill=0.0,
                                   base=0, pattern=[[1, P]], channel_multiplier=-1).then_inc(s.ready, 1)
                pool.affine_select(out=c.own_head[:], in_=c.own_head[:], compare_op=ALU.is_ge, fill=0.0, base=0,
                                   pattern=[[1, FW]], channel_multiplier=-HD).then_inc(s.ready, 1)
                pool.wait_ge(s.ready, 4)
                pool.affine_select(out=c.own_head[:], in_=c.own_head[:], compare_op=ALU.is_ge, fill=0.0,
                                   base=HD - 1, pattern=[[-1, FW]], channel_multiplier=HD).then_inc(s.ready, 1)

            @block.vector
            def _(dve):
                dve.wait_ge(s.ready, 4)
                dve.tensor_copy(c.ident_r[:], c.ident[:])
                dve.tensor_copy(c.causal_r[:], causal[:])
                dve.tensor_copy(c.fold[0:HD, :], c.ident[0:HD, 0:HD])
                dve.tensor_copy(c.fold[HD:P, :], c.ident[HD:P, HD:P])
                for k in range(P // PAGES):
                    rows = slice(k * PAGES, (k + 1) * PAGES)
                    if k < P // PAGES - 1:
                        dve.memset(c.page_before[rows, (k + 1) * PAGES:], 0.0)
                    for g in range(2):
                        j = g * (P // PAGES) + k
                        dve.memset(c.seq_of_page[rows, g, j:j + 1], 1.0)

            @block.sync
            def _(sp):
                sp.dma_start(c.b_f[0:FH, :], io.b_f.rearrange("l h -> h l")).then_inc(s.loaded, 16)
                sp.dma_start(c.pages[0:1, :], io.page_table.rearrange("b n -> (b n)").unsqueeze(0)).then_inc(s.loaded, 16)
                for g in range(2):
                    half = io.page_table[4 * g:4 * g + 4, :].rearrange("b n -> (b n)").unsqueeze(1)
                    sp.dma_start(c.page_index[:, g:g + 1], half.bitcast(U32)).then_inc(s.loaded, 16)
                sp.wait_ge(s.loaded, 64)


def split_weights(nc, raw, hi, lo, src, rows=DT):
    with stage(nc, "loaded hi_done") as (block, s):

        @block.sync
        def _(sp):
            for dst, part in src:
                sp.dma_start(dst, part).then_inc(s.loaded, 16)

        @block.scalar
        def _(act):
            act.wait_ge(s.loaded, 16 * len(src))
            act.activation(hi, raw, ACT.Copy).then_inc(s.hi_done, 1)

        @block.vector
        def _(dve):
            dve.wait_ge(s.hi_done, 1)
            dve.tensor_tensor(lo, raw, hi.bitcast(F32), ALU.subtract)


def norm_transpose(nc, c, n, src, gain, hi, lo, rows=P, keep=None, gates=None):
    with ExitStack() as ctx:
        sb, psum = alloc(ctx, nc)
        x = keep if keep is not None else sb("x_in", [P, 2, D])
        slots = n if keep is not None else 2
        xn = sb("x_normed", [P, 2, D])
        junk = sb("squares", [P, D])
        ss = sb("sum_squares", [P, n])
        rstd = sb("rstd", [P, n])
        ps_t = psum("ps_transposed", [P, 2, D])
        ps_f = psum("ps_gates", [P, BLK])
        logits = sb("gate_logits", [P, n * P]) if gates else None
        with stage(nc, "zeroed load0 load1 squared var rstd normed turned hi_done lo_done gate gate_out gates_stored") as (block, s):
            loads = (s.load0, s.load1)
            gate_chunks = [(t0, min(BLK, n * P - t0)) for t0 in range(0, n * P, BLK)]

            @block.sync
            def _(sp):
                if rows < P:
                    sp.wait_ge(s.zeroed, 1)
                for k in range(n):
                    if k >= 2:
                        sp.wait_ge(s.normed, k - 1)
                    sp.dma_start(x[0:rows, k % slots, :], src(k)).then_inc(loads[k % 2], 16)
                if gates:
                    sp.wait_ge(s.gate_out, len(gate_chunks))
                    sp.dma_start(gates[2], logits[0:FH, :]).then_inc(s.gates_stored, 16)
                    sp.wait_ge(s.gates_stored, 16)

            @block.gpsimd
            def _(pool):
                if rows < P:
                    pool.memset(x[:, 0, :], 0.0).then_inc(s.zeroed, 1)
                for k in range(n):
                    pool.wait_ge(s.squared, k + 1)
                    pool.tensor_scalar(rstd[:, k:k + 1], ss[:, k:k + 1], 1.0 / D, EPS, ALU.mult, ALU.add).then_inc(s.var, 1)
                    pool.wait_ge(s.var, k + 1)
                    pool.tensor_tensor(rstd[:, k:k + 1], rstd[:, k:k + 1], c.minus_half[:], ALU.pow).then_inc(s.rstd, 1)

            @block.scalar
            def _(act):
                def square(k):
                    act.wait_ge(loads[k % 2], 16 * (k // 2 + 1))
                    if k >= 1:
                        act.wait_ge(s.squared, k)
                    act.activation(junk[:], x[:, k % slots, :], ACT.Square, accum_out=ss[:, k:k + 1]).then_inc(s.squared, 1)

                square(0)
                for k in range(n):
                    if k + 1 < n:
                        square(k + 1)
                    act.wait_ge(s.turned, k + 1)
                    act.activation(hi[:, :, k * P:(k + 1) * P], ps_t[:, k % 2, :].rearrange("p (d t) -> p d t", d=DT),
                                   ACT.Copy).then_inc(s.hi_done, 1)
                if gates:
                    for j, (t0, w) in enumerate(gate_chunks):
                        act.wait_ge(s.gate, j + 1)
                        act.activation(logits[0:FH, t0:t0 + w], ps_f[0:FH, 0:w], ACT.Identity,
                                       bias=c.b_f[0:FH, :]).then_inc(s.gate_out, 1)

            @block.vector
            def _(dve):
                def normalise(k):
                    dve.wait_ge(s.rstd, k + 1)
                    if k >= 2:
                        dve.wait_ge(s.turned, k - 1)
                    dve.scalar_tensor_tensor(out=xn[:, k % 2, :], in0=x[:, k % slots, :], scalar=rstd[:, k:k + 1],
                                             in1=gain, op0=ALU.mult, op1=ALU.mult).then_inc(s.normed, 1)

                normalise(0)
                for k in range(n):
                    if k + 1 < n:
                        normalise(k + 1)
                    dve.wait_ge(s.hi_done, k + 1)
                    dve.tensor_tensor(lo[:, :, k * P:(k + 1) * P], ps_t[:, k % 2, :].rearrange("p (d t) -> p d t", d=DT),
                                      hi[:, :, k * P:(k + 1) * P].bitcast(F32), ALU.subtract).then_inc(s.lo_done, 1)

            @block.tensor
            def _(pe):
                for k in range(n):
                    pe.wait_ge(s.normed, k + 1)
                    if k >= 2:
                        pe.wait_ge(s.lo_done, k - 1)
                    for d in range(DT):
                        turned = pe.transpose(ps_t[:, k % 2, d * P:(d + 1) * P], xn[:, k % 2, d * P:(d + 1) * P], c.ident[:])
                    turned.then_inc(s.turned, 1)
                if gates:
                    pe.wait_ge(s.lo_done, n)
                    for j, (t0, w) in enumerate(gate_chunks):
                        if j >= 1:
                            pe.wait_ge(s.gate_out, j)
                        for d in range(DT):
                            for m, (a, b) in enumerate(((gates[0], hi), (gates[0], lo), (gates[1], hi))):
                                mm = pe.matmul(ps_f[:, 0:w], a[:, d, :], b[:, d, t0:t0 + w],
                                               start=(d == 0 and m == 0), stop=(d == DT - 1 and m == 2))
                        mm.then_inc(s.gate, 1)


def project(nc, c, n, h_hi, h_lo, w, buf, dst, rows=P, following=(), keys=None):
    nxt = 1 - buf
    groups = PAGES // 4
    with ExitStack() as ctx:
        sb, psum = alloc(ctx, nc)
        out = sb("proj_out", [P, 2, BLK])
        ps_p = psum("ps_proj", [P, 2, BLK])
        if keys:
            page_k = sb("page_k", [P, 2, 4, FW])
            prod = sb("key_products", [P, 4, FW])
            q_row = sb("q_row", [P, FW])
        with stage(nc, "w_in w_hi made evacuated store0 store1 q_in keys0 keys1 prod_done keys_done") as (block, s):
            stores = (s.store0, s.store1)
            keys_in = (s.keys0, s.keys1)

            @block.sync
            def _(sp):
                def load_keys(g):
                    if not keys or g >= groups:
                        return
                    if g >= 2:
                        sp.wait_ge(s.prod_done, g - 1)
                    for j in range(4):
                        page = sp.value_load(c.pages[0:1, ds(keys.seq * PAGES + 4 * g + j, 1)], min_val=0, max_val=keys.last_page)
                        sp.dma_start(page_k[:, g % 2, j, :], keys.cache[ds(page, 1)].rearrange("n r c -> (n r) c")).then_inc(keys_in[g % 2], 16)

                if keys:
                    sp.dma_start(q_row[:], keys.query).then_inc(s.q_in, 16)
                load_keys(0)
                load_keys(1)
                for to, part in following:
                    sp.dma_start(to, part).then_inc(s.w_in, 16)
                for t in range(n):
                    load_keys(t + 2)
                    sp.wait_ge(s.evacuated, t + 1)
                    sp.dma_start(dst(t), out[0:rows, t % 2, :]).then_inc(stores[t % 2], 16)
                for k in range(min(n, 2)):
                    sp.wait_ge(stores[k], 16 * ((n - k + 1) // 2))

            @block.tensor
            def _(pe):
                for t in range(n):
                    if t >= 2:
                        pe.wait_ge(s.evacuated, t - 1)
                    for d in range(DT):
                        a_hi, a_lo = h_hi[:, d, t * P:(t + 1) * P], h_lo[:, d, t * P:(t + 1) * P]
                        b_hi, b_lo = w.hi[:, buf, d, :], w.lo[:, buf, d, :]
                        pe.matmul(ps_p[:, t % 2, :], a_hi, b_hi, start=(d == 0), stop=False)
                        pe.matmul(ps_p[:, t % 2, :], a_hi, b_lo, start=False, stop=False)
                        mm = pe.matmul(ps_p[:, t % 2, :], a_lo, b_hi, start=False, stop=(d == DT - 1))
                    mm.then_inc(s.made, 1)

            @block.scalar
            def _(act):
                def evacuate(t):
                    act.wait_ge(s.made, t + 1)
                    if t >= 2:
                        act.wait_ge(stores[t % 2], 16 * (t // 2))
                    act.activation(out[:, t % 2, :], ps_p[:, t % 2, :], ACT.Copy).then_inc(s.evacuated, 1)

                if n > 2:
                    evacuate(0)
                    evacuate(1)
                if following:
                    for j in range(4):
                        act.wait_ge(s.w_in, 16 * len(following))
                        act.activation(w.hi[:, nxt, 2 * j:2 * j + 2, :], w.raw[:, 2 * j:2 * j + 2, :], ACT.Copy).then_inc(s.w_hi, 1)
                for t in range(2 if n > 2 else 0, n):
                    evacuate(t)

            @block.vector
            def _(dve):
                if following:
                    for j in range(4):
                        dve.wait_ge(s.w_hi, j + 1)
                        dve.tensor_tensor(w.lo[:, nxt, 2 * j:2 * j + 2, :], w.raw[:, 2 * j:2 * j + 2, :],
                                          w.hi[:, nxt, 2 * j:2 * j + 2, :].bitcast(F32), ALU.subtract)
                if keys:
                    dve.wait_ge(s.q_in, 16)
                    for g in range(groups):
                        dve.wait_ge(keys_in[g % 2], 64 * (g // 2 + 1))
                        if g >= 1:
                            dve.wait_ge(s.keys_done, g)
                        dve.tensor_tensor(prod[:], page_k[:, g % 2, :, :], q_row[:].unsqueeze(1).to_broadcast([P, 4, FW]),
                                          ALU.mult).then_inc(s.prod_done, 1)
                        dve.wait_ge(s.prod_done, g + 1)
                        dve.tensor_reduce(keys.scores[:, ds(keys.seq * (PAGES * FH) + g * 4 * FH, 4 * FH)],
                                          prod[:].rearrange("p a (h d) -> p (a h) d", d=HD), AX.X, ALU.add).then_inc(s.keys_done, 1)


def forget_gates(nc, c, gates, io, scratch, dec):
    T = SEQ + P
    with ExitStack() as ctx:
        sb, psum = alloc(ctx, nc)
        low = sb("low", [P, T])
        soft = sb("soft", [P, T])
        lf = sb("logf", [P, T])
        ones = sb("ones_row", [P, SEQ])
        out = sb("logf_out", [P, NT, FH])
        ps = psum("ps_logf", [P, NT + 1, FH])
        with stage(nc, "low size exp ln lf cum turned out stored") as (block, s):

            @block.vector
            def _(dve):
                dve.memset(ones[0:FH, :], 1.0)
                dve.tensor_scalar(low[0:FH, :], gates[0:FH, :], 0.0, None, ALU.min).then_inc(s.low, 1)
                dve.wait_ge(s.ln, 1)
                dve.wait_ge(s.low, 1)
                dve.tensor_tensor(lf[0:FH, :], low[0:FH, :], soft[0:FH, :], ALU.subtract).then_inc(s.lf, 1)
                dve.wait_ge(s.lf, 1)
                dve.tensor_tensor_scan(low[0:FH, 0:SEQ], ones[0:FH, :], lf[0:FH, 0:SEQ], 0.0, ALU.mult, ALU.subtract).then_inc(s.cum, 1)
                dve.wait_ge(s.turned, 1)
                dve.tensor_copy(out[:], ps[:, 0:NT, :])
                dve.tensor_copy(dec.logf_new[0:DB, :], ps[0:DB, NT, :]).then_inc(s.out, 1)

            @block.scalar
            def _(act):
                act.activation(soft[0:FH, :], gates[0:FH, :], ACT.Abs).then_inc(s.size, 1)
                act.wait_ge(s.size, 1)
                act.activation(soft[0:FH, :], soft[0:FH, :], ACT.Exp, scale=-1.0).then_inc(s.exp, 1)
                act.wait_ge(s.exp, 1)
                act.activation(soft[0:FH, :], soft[0:FH, :], ACT.Ln, bias=1.0).then_inc(s.ln, 1)

            @block.tensor
            def _(pe):
                pe.wait_ge(s.lf, 1)
                for t in range(NT + 1):
                    turned = pe.transpose(ps[:, t, :], lf[0:FH, t * P:(t + 1) * P], c.ident[0:FH, 0:FH])
                turned.then_inc(s.turned, 1)

            @block.sync
            def _(sp):
                sp.wait_ge(s.cum, 1)
                sp.dma_start(scratch.neg_cum, low[0:FH, 0:SEQ]).then_inc(s.stored, 16)
                sp.wait_ge(s.out, 1)
                sp.dma_start(io.new_logf.rearrange("(t p) h -> p t h", p=P), out[:]).then_inc(s.stored, 16)
                sp.dma_start(io.new_logf_s, dec.logf_new[0:DB, :]).then_inc(s.stored, 16)
                sp.wait_ge(s.stored, 48)


def decode_softmax(nc, c, io, scratch, dec):
    G = 2
    NS = DB * FH
    NM = DB * MH
    with ExitStack() as ctx:
        sb, psum = alloc(ctx, nc)
        lfp = sb("page_logf", [P, G, P, FH])
        cum = sb("page_cum", [P, G, P, FH])
        ones = sb("ones_page", [P, P])
        cum_r = sb("row_cum", [P, DB, PAGES, FH])
        rows = sb("new_rows", [P, PW])
        small = sb("small", [P, 8, FH])
        wide = sb("wide", [P, DB, FH])
        mem_k = sb("mem_k", [P, DB, 2, MW])
        mem_q = sb("mem_q", [P, DB, MW])
        mx = sb("maxima", [P, NS + NM])
        top = sb("maxima_all", [P, NS + NM])
        sm = sb("sums", [P, NS + NM])
        total = sb("sums_all", [P, NS + NM])
        ps_t = psum("ps_cum", [P, 4, 4, P])
        ps_o = psum("ps_offset", [P, G, FH])
        ps_c = psum("ps_total", [P, FH])
        names = "loaded chain scanned offsets totals summed_cum turned row_major maxed all_max shifted weighed summed all_sum"
        with stage(nc, names) as (block, s):

            @block.gpsimd
            def _(pool):
                table = io.cache_logf.rearrange("l n r h -> (l n) (r h)")
                for g in range(G):
                    pool.indirect_dma_start(lfp[:, g, :, :].rearrange("p r h -> p (r h)"), None, table,
                                            bass.IndirectOffsetOnAxis(ap=c.page_index[:, g:g + 1], axis=0)).then_inc(c.gathered, 16)
                pool.wait_ge(s.maxed, 1)
                pool.partition_all_reduce(top[:], mx[:], P, RMAX).then_inc(s.all_max, 1)
                pool.wait_ge(s.summed, 1)
                pool.partition_all_reduce(total[:], sm[:], P, RADD).then_inc(s.all_sum, 1)

            @block.sync
            def _(sp):
                sp.dma_start(rows[0:DB, :], scratch.samp).then_inc(s.loaded, 16)
                sp.dma_start(mem_k[:], io.cache_mem_k.rearrange("l b (t p) h d -> p (l b) t (h d)", p=P)).then_inc(s.loaded, 16)
                for b in range(DB):
                    sp.dma_start(mem_q[:, b, :], scratch.samp[b:b + 1, MCOL:MCOL + MW].to_broadcast([P, MW])).then_inc(s.loaded, 16)

            @block.vector
            def _(dve):
                chain = [0]

                def link(ins):
                    chain[0] += 1
                    ins.then_inc(s.chain, 1)
                    dve.wait_ge(s.chain, chain[0])

                past = dec.scores[:].rearrange("p (b n h) -> p b n h", b=DB, n=PAGES)
                past_h = dec.scores[:].rearrange("p (b n h) -> p b h n", b=DB, n=PAGES)
                mem = dec.mem_scores[:].rearrange("p (b t h) -> p b t h", b=DB, t=2)
                mx_mem = mx[:, NS:].rearrange("p (b h) -> p b h", b=DB)
                own = c.ident[0:DB, 0:DB].unsqueeze(2).to_broadcast([DB, DB, FH])
                own_m = c.ident[0:DB, 0:DB].unsqueeze(2).to_broadcast([DB, DB, MH])

                def on_own(source, mask, heads, out):
                    link(dve.tensor_tensor(wide[0:DB, :, 0:heads], source.rearrange("p (b h) -> p b h", b=DB), mask, ALU.mult))
                    link(dve.tensor_reduce(out, wide[0:DB, :, 0:heads].rearrange("p b h -> p h b"), AX.X, ALU.add))

                link(dve.memset(ones[:], 1.0))
                dve.wait_ge(c.gathered, 16 * G)
                for g in range(G):
                    for h in range(FH):
                        scan = dve.tensor_tensor_scan(cum[:, g, :, h], ones[:], lfp[:, g, :, h], 0.0, ALU.mult, ALU.add)
                scan.then_inc(s.scanned, 1)
                dve.wait_ge(s.scanned, 1)
                dve.wait_ge(s.offsets, 1)
                dve.wait_ge(s.totals, 1)
                for g in range(G):
                    added = dve.tensor_tensor(cum[:, g], cum[:, g], ps_o[:, g, :].unsqueeze(1).to_broadcast([P, P, FH]), ALU.add)
                added.then_inc(s.summed_cum, 1)
                dve.wait_ge(s.loaded, 16 * (2 + DB))
                for b in range(DB):
                    last = dve.tensor_tensor(mem_k[:, b], mem_k[:, b], mem_q[:, b, :].unsqueeze(1).to_broadcast([P, 2, MW]), ALU.mult)
                link(last)
                link(dve.tensor_reduce(dec.mem_scores[:], mem_k[:].rearrange("p b t (h d) -> p (b t h) d", d=HD), AX.X, ALU.add))
                link(dve.tensor_scalar(dec.mem_scores[:], dec.mem_scores[:], SCALE, None, ALU.mult))
                dve.tensor_tensor(mx_mem, mem[:, :, 0, :], mem[:, :, 1, :], ALU.max)
                link(dve.tensor_tensor(rows[0:DB, QCOL:QCOL + FW], rows[0:DB, QCOL:QCOL + FW], rows[0:DB, KCOL:KCOL + FW], ALU.mult))
                dve.tensor_tensor(small[0:DB, 1, :], dec.logf_new[0:DB, :], ps_c[0:DB, :], ALU.add)
                link(dve.tensor_reduce(small[0:DB, 0, :], rows[0:DB, QCOL:QCOL + FW].rearrange("p (h d) -> p h d", d=HD), AX.X, ALU.add))
                dve.tensor_scalar(wide[0:DB], own, 1.0, -NEG, ALU.subtract, ALU.mult)
                link(dve.scalar_tensor_tensor(out=small[0:DB, 2, :], in0=small[0:DB, 0, :], scalar=SCALE, in1=small[0:DB, 1, :],
                                              op0=ALU.mult, op1=ALU.subtract))
                link(dve.tensor_tensor(wide[0:DB], wide[0:DB], small[0:DB, 2, :].unsqueeze(1).to_broadcast([DB, DB, FH]), ALU.add))
                dve.wait_ge(s.row_major, 4)
                link(dve.scalar_tensor_tensor(out=dec.scores[:], in0=dec.scores[:], scalar=SCALE,
                                              in1=cum_r[:].rearrange("p b n h -> p (b n h)"), op0=ALU.mult, op1=ALU.subtract))
                link(dve.tensor_reduce(mx[:, 0:NS], past_h, AX.X, ALU.max))
                dve.tensor_tensor(mx[0:DB, 0:NS], mx[0:DB, 0:NS], wide[0:DB].rearrange("p b h -> p (b h)"), ALU.max).then_inc(s.maxed, 1)
                dve.wait_ge(s.all_max, 1)
                for b in range(DB):
                    dve.tensor_tensor(past[:, b], past[:, b], top[:, b * FH:(b + 1) * FH].unsqueeze(1).to_broadcast([P, PAGES, FH]), ALU.subtract)
                    dve.tensor_tensor(mem[:, b], mem[:, b], top[:, NS + b * MH:NS + (b + 1) * MH].unsqueeze(1).to_broadcast([P, 2, MH]), ALU.subtract)
                on_own(top[0:DB, 0:NS], own, FH, small[0:DB, 3, :])
                dve.tensor_tensor(small[0:DB, 4, :], small[0:DB, 2, :], small[0:DB, 3, :], ALU.subtract).then_inc(s.shifted, 1)
                dve.wait_ge(s.weighed, 3)
                dve.tensor_reduce(sm[:, 0:NS], past_h, AX.X, ALU.add)
                dve.tensor_tensor(sm[:, NS:].rearrange("p (b h) -> p b h", b=DB), mem[:, :, 0, :], mem[:, :, 1, :], ALU.add).then_inc(s.summed, 1)
                dve.wait_ge(s.all_sum, 1)
                on_own(total[0:DB, 0:NS], own, FH, small[0:DB, 6, :])
                link(dve.tensor_tensor(small[0:DB, 6, :], small[0:DB, 6, :], dec.w_new[0:DB, :], ALU.add))
                dve.reciprocal(dec.r_fox[0:DB, :], small[0:DB, 6, :])
                on_own(total[0:DB, NS:], own_m, MH, small[0:DB, 7, 0:MH])
                dve.reciprocal(dec.r_mem[0:DB, :], small[0:DB, 7, 0:MH])

            @block.tensor
            def _(pe):
                pe.wait_ge(s.scanned, 1)
                for g in range(G):
                    mm = pe.matmul(ps_o[:, g, :], c.page_before[:], cum[:, g, P - 1, :], start=True, stop=True)
                mm.then_inc(s.offsets, 1)
                for g in range(G):
                    mm = pe.matmul(ps_c[0:DB, :], c.seq_of_page[:, g, :], cum[:, g, P - 1, :], start=(g == 0), stop=(g == 1))
                mm.then_inc(s.totals, 1)
                pe.wait_ge(s.summed_cum, 1)
                for k in range(4):
                    for j in range(4):
                        turned = pe.transpose(ps_t[:, k, j, :], cum[:, k // 2, :, 4 * (k % 2) + j], c.ident[:])
                    turned.then_inc(s.turned, 1)

            @block.scalar
            def _(act):
                for k in range(4):
                    act.wait_ge(s.turned, k + 1)
                    b0, h0 = 4 * (k // 2), 4 * (k % 2)
                    act.activation(cum_r[:, b0:b0 + 4, :, h0:h0 + 4].rearrange("p b n h -> p (b n) h"),
                                   ps_t[:, k, :, :].rearrange("p h m -> p m h"), ACT.Copy).then_inc(s.row_major, 1)
                act.wait_ge(s.shifted, 1)
                act.activation(dec.scores[:], dec.scores[:], ACT.Exp).then_inc(s.weighed, 1)
                act.activation(dec.mem_scores[:], dec.mem_scores[:], ACT.Exp).then_inc(s.weighed, 1)
                act.activation(dec.w_new[0:DB, :], small[0:DB, 4, :], ACT.Exp).then_inc(s.weighed, 1)


def decode_memory_values(nc, c, io, dec, out):
    with ExitStack() as ctx:
        sb, psum = alloc(ctx, nc)
        mem_v = sb("mem_v", [P, DB, 2, MW])
        own = sb("own_rows", [P, DB, MW])
        pick = sb("pick", [P, DB, DB])
        ps_m = psum("ps_m", [P, DB, MW])
        ps_s = psum("ps_s", [P, MW])
        with stage(nc, "loaded picked zeroed made masked summed") as (block, s):

            @block.sync
            def _(sp):
                sp.dma_start(mem_v[:], io.cache_mem_v.rearrange("l b (t p) h d -> p (l b) t (h d)", p=P)).then_inc(s.loaded, 16)

            @block.gpsimd
            def _(pool):
                pool.memset(pick[0:MH], 0.0).then_inc(s.zeroed, 1)
                pool.wait_ge(s.zeroed, 1)
                for b in range(DB):
                    pool.memset(pick[0:MH, b, b:b + 1], 1.0).then_inc(s.picked, 1)

            @block.tensor
            def _(pe):
                pe.wait_ge(s.loaded, 16)
                for b in range(DB):
                    for t in range(2):
                        mm = pe.matmul(ps_m[0:MH, b, :], dec.mem_scores[:, (2 * b + t) * MH:(2 * b + t + 1) * MH], mem_v[:, b, t, :],
                                       start=(t == 0), stop=(t == 1))
                mm.then_inc(s.made, 1)
                pe.wait_ge(s.picked, DB)
                pe.wait_ge(s.masked, 1)
                for b in range(DB):
                    mm = pe.matmul(ps_s[0:DB, :], pick[0:MH, b, :], own[0:MH, b, :], start=(b == 0), stop=(b == DB - 1))
                mm.then_inc(s.summed, 1)

            @block.vector
            def _(dve):
                dve.wait_ge(s.made, 1)
                dve.tensor_tensor(own[0:MH], ps_m[0:MH], c.own_head[0:MH, 0:MW].unsqueeze(1).to_broadcast([MH, DB, MW]), ALU.mult).then_inc(s.masked, 1)
                dve.wait_ge(s.summed, 1)
                dve.tensor_tensor(out[0:DB, :].rearrange("p (h d) -> p h d", d=HD), ps_s[0:DB, :].rearrange("p (h d) -> p h d", d=HD),
                                  dec.r_mem[0:DB, :].unsqueeze(2).to_broadcast([DB, MH, HD]), ALU.mult)


def load_head(eng, a, head, nk, sem):
    eng.dma_start(a.q[:, :, 0, :], head.q.rearrange("(t p) d -> p t d", p=P)).then_inc(sem, 16)
    eng.dma_start(a.k[:, 0:nk, 0, :], head.k.rearrange("(t p) d -> p t d", p=P)).then_inc(sem, 16)
    eng.dma_start(a.v[:, 0:nk, :], head.v.rearrange("(t p) d -> p t d", p=P)).then_inc(sem, 16)
    if head.neg_cum is None:
        return 48
    eng.dma_start(a.neg_cum[:], head.neg_cum.to_broadcast([P, SEQ])).then_inc(sem, 16)
    return 64


def attend(nc, c, a, nk, causal, following, dst, values=None):
    chunks = NT // QCH

    def key_tiles(ch):
        return QCH * (ch + 1) if causal else nk

    def pieces(i):
        w = (i + 1) * P if causal else nk * P
        return [(p0, min(w, p0 + 1024)) for p0 in range(0, w, 1024)]

    order = [("A", 0)]
    for ch in range(chunks):
        if ch + 1 < chunks:
            order.append(("A", ch + 1))
        order.append(("B", ch))
    n_k = (nk + 3) // 4
    with ExitStack() as ctx:
        sb, psum = alloc(ctx, nc)
        ps_s = psum("ps_scores", [P, 2, 1024])
        ps_t = psum("ps_turned", [P, 2, BLK])
        ps_o = psum("ps_out", [P, BLK])
        if values:
            ps_v = psum("ps_values", [P, FW])
        names = ("doubled turned hi lo v_hi v_lo scored min1 min2 probs t_turned t_hi t_split pv o_copied o_ready inverted o_out "
                 "stored loaded w_copied v0 v1 v2 v3 v_used v_masked v_row v_row_out")
        with stage(nc, names) as (block, s):
            v_in = (s.v0, s.v1, s.v2, s.v3)

            def turn_steps():
                return [("k", j) for j in range(n_k)] + [("q", j) for j in range(NT // 4)]

            @block.gpsimd
            def _(pool):
                pool.tensor_copy(a.k[:, 0:nk, 1, :], a.k[:, 0:nk, 0, :]).then_inc(s.doubled, 1)
                pool.tensor_copy(a.q[:, :, 1, :], a.q[:, :, 0, :]).then_inc(s.doubled, 1)
                if values:
                    pool.tensor_copy(values.weights[:], values.all_weights).then_inc(s.w_copied, 1)

            @block.sync
            def _(sp):
                if values:
                    for n in range(PAGES):
                        if n >= 4:
                            sp.wait_ge(s.v_used, n - 3)
                        page = sp.value_load(c.pages[0:1, ds(values.seq * PAGES + n, 1)], min_val=0, max_val=values.last_page)
                        sp.dma_start(values.page_v[:, n % 4, :], values.cache[ds(page, 1)].rearrange("n r c -> (n r) c")).then_inc(v_in[n % 4], 16)
                    sp.wait_ge(s.v_row_out, 1)
                    sp.dma_start(values.dst, values.row[0:1, :]).then_inc(s.stored, 16)
                sp.wait_ge(s.stored, 16 * (chunks + (1 if values else 0)))
                sp.wait_ge(s.loaded, 48 if following.neg_cum is None else 64)

            @block.tensor
            def _(pe):
                st = Steps()

                def take_bank():
                    if len(st.uses) >= 2:
                        pe.wait_ge(*st.uses[-2])
                    return ps_t[:, len(st.uses) % 2, :]

                def turn_in():
                    for u, (what, j) in enumerate(turn_steps()):
                        if u == 0:
                            pe.wait_ge(s.doubled, 2)
                        if u >= 2:
                            pe.wait_ge(s.lo, u - 1)
                        raw = a.k if what == "k" else a.q
                        tiles = range(4 * j, min(4 * j + 4, nk if what == "k" else NT))
                        for t in tiles:
                            turned = pe.transpose(ps_t[:, u % 2, (t - 4 * j) * P:(t - 4 * j + 1) * P],
                                                  raw[:, t, :, :].rearrange("p a d -> p (a d)"), c.ident[:])
                        turned.then_inc(s.turned, 1)
                    pe.wait_ge(s.lo, len(turn_steps()))

                def scores(ch):
                    for i in range(QCH * ch, QCH * ch + QCH):
                        for p0, p1 in pieces(i):
                            if st.score >= 2:
                                pe.wait_ge(s.min1, st.score - 1)
                            bank = ps_s[:, st.score % 2, :]
                            for b0 in range(p0, p1, BLK):
                                b1 = min(b0 + BLK, p1)
                                out = bank[:, b0 - p0:b1 - p0]
                                diag = causal and b1 == (i + 1) * P
                                pe.matmul(out, a.q_hi[:, i * P:(i + 1) * P], a.k_st[:, b0:b1], start=True, stop=False)
                                mm = pe.matmul(out, a.q_lo[:, i * P:(i + 1) * P], a.k_st[:, b0:b1], start=False, stop=not diag)
                                if diag:
                                    mm = pe.matmul(bank[:, b1 - P - p0:b1 - p0], c.ident_r[:], c.causal_r[:], start=False, stop=True)
                            mm.then_inc(s.scored, 1)
                            st.score += 1

                def value_page():
                    if not values or st.page >= PAGES:
                        return
                    n = st.page
                    if n == 0:
                        pe.wait_ge(s.w_copied, 1)
                    pe.wait_ge(v_in[n % 4], 16 * (n // 4 + 1))
                    pe.matmul(ps_v[0:FH, :], values.weights[:, n * FH:(n + 1) * FH], values.page_v[:, n % 4, :],
                              start=(n == 0), stop=(n == PAGES - 1)).then_inc(s.v_used, 1)
                    st.page += 1

                def weigh(ch):
                    last = key_tiles(ch) - 1
                    pe.wait_ge(s.probs, QCH * (ch + 1))

                    def turn(j):
                        r0 = max(0, j - QCH * ch) if causal else 0
                        bank = take_bank()
                        for r in range(r0, QCH):
                            turned = pe.transpose(bank[:, r * P:(r + 1) * P], a.probs[:, ch % 2, r, j * P:(j + 1) * P], c.ident[:])
                        turned.then_inc(s.t_turned, 1)
                        st.turn += 1
                        st.uses.append((s.t_split, st.turn))

                    turn(0)
                    for j in range(last + 1):
                        if j < last:
                            turn(j + 1)
                        value_page()
                        r0 = max(0, j - QCH * ch) if causal else 0
                        if j == 0 and ch >= 1:
                            pe.wait_ge(s.o_copied, ch)
                        out = ps_o[:, r0 * P:]
                        pe.wait_ge(s.t_split, st.pv + 1)
                        pe.matmul(out, a.v_st[:, j, :], a.p_hi[:, st.pv % 2, r0 * P:], start=(j == 0), stop=False)
                        pe.matmul(out, a.v_st[:, j, :], a.p_lo[:, st.pv % 2, r0 * P:], start=False, stop=(j == last)).then_inc(s.pv, 1)
                        st.pv += 1
                    pe.wait_ge(s.o_copied, ch + 1)
                    bank = take_bank()
                    for r in range(QCH):
                        mm = pe.matmul(bank[:, r * HD:(r + 1) * HD], a.o_t[:, ch % 2, r * P:(r + 1) * P], c.fold[:], start=True, stop=True)
                    mm.then_inc(s.o_ready, 1)
                    st.uses.append((s.o_out, ch + 1))

                turn_in()
                pe.wait_ge(s.v_lo, 1)
                for what, ch in order:
                    scores(ch) if what == "A" else weigh(ch)
                if values:
                    while st.page < PAGES:
                        value_page()
                    pe.wait_ge(s.v_masked, 1)
                    pe.matmul(take_bank()[0:1, :], c.ones[0:FH, :], values.own[0:FH, :], start=True, stop=True).then_inc(s.v_row, 1)

            @block.scalar
            def _(act):
                st = Steps()
                act.activation(a.v_st[:, 0:nk, 0:HD], a.v[:, 0:nk, :], ACT.Copy).then_inc(s.v_hi, 1)
                for u, (what, j) in enumerate(turn_steps()):
                    act.wait_ge(s.turned, u + 1)
                    if what == "k":
                        w = min(BLK, nk * P - j * BLK)
                        act.activation(a.k_st[:, j * BLK:j * BLK + w], ps_t[:, u % 2, 0:w], ACT.Copy).then_inc(s.hi, 1)
                    else:
                        act.activation(a.q_hi[:, j * BLK:(j + 1) * BLK], ps_t[:, u % 2, :], ACT.Copy, scale=SCALE).then_inc(s.hi, 1)

                def exps(ch):
                    for r in range(QCH):
                        i = QCH * ch + r
                        w = (i + 1) * P if causal else nk * P
                        st.scored += len(pieces(i))
                        if len(pieces(i)) == 1:
                            act.wait_ge(s.min1, st.scored)
                        else:
                            st.joined += 1
                            act.wait_ge(s.min2, st.joined)
                        act.activation(a.probs[:, ch % 2, r, 0:w], a.probs[:, ch % 2, r, 0:w], ACT.Exp, scale=-1.0, bias=a.low[:, i:i + 1],
                                       accum_out=a.sums[:, i:i + 1]).then_inc(s.probs, 1)

                def split(ch):
                    for j in range(key_tiles(ch)):
                        r0 = max(0, j - QCH * ch) if causal else 0
                        act.wait_ge(s.t_turned, st.pv + 1)
                        if st.pv >= 2:
                            act.wait_ge(s.pv, st.pv - 1)
                        act.activation(a.p_hi[:, st.pv % 2, r0 * P:], ps_t[:, st.turn % 2, r0 * P:], ACT.Copy).then_inc(s.t_hi, 1)
                        st.pv += 1
                        st.turn += 1
                    act.wait_ge(s.pv, st.pv)
                    if ch >= 2:
                        act.wait_ge(s.o_ready, ch - 1)
                    act.activation(a.o_t[:, ch % 2, :], ps_o[:], ACT.Copy).then_inc(s.o_copied, 1)
                    st.turn += 1

                def store(ch):
                    act.wait_ge(s.o_out, ch + 1)
                    act.dma_start(dst(ch), a.o_out[:, ch, :, :]).then_inc(s.stored, 16)

                for what, ch in order:
                    if what == "A":
                        exps(ch)
                        if ch >= 2:
                            store(ch - 2)
                    else:
                        split(ch)
                    if (what, ch) == ("A", chunks - 1):
                        act.wait_ge(s.v_lo, 1)
                        load_head(act, a, following, nk, s.loaded)
                store(chunks - 2)
                store(chunks - 1)
                if values:
                    act.wait_ge(s.v_row, 1)
                    act.activation(values.row[0:1, :], ps_t[0:1, st.turn % 2, :], ACT.Copy).then_inc(s.v_row_out, 1)

            @block.vector
            def _(dve):
                st = Steps()
                for u, (what, j) in enumerate(turn_steps()):
                    dve.wait_ge(s.hi, u + 1)
                    if what == "k":
                        w = min(BLK, nk * P - j * BLK)
                        upper = a.k_st[HD:P, j * BLK:j * BLK + w]
                        dve.tensor_tensor(upper, ps_t[HD:P, u % 2, 0:w], upper.bitcast(F32), ALU.subtract).then_inc(s.lo, 1)
                    else:
                        cols = slice(j * BLK, (j + 1) * BLK)
                        dve.scalar_tensor_tensor(out=a.q_lo[:, cols], in0=ps_t[:, u % 2, :], scalar=SCALE, in1=a.q_hi[:, cols].bitcast(F32),
                                                 op0=ALU.mult, op1=ALU.subtract).then_inc(s.lo, 1)
                dve.wait_ge(s.v_hi, 1)
                dve.tensor_tensor(a.v_st[:, 0:nk, HD:P], a.v[:, 0:nk, :], a.v_st[:, 0:nk, 0:HD].bitcast(F32), ALU.subtract).then_inc(s.v_lo, 1)

                def lows(ch):
                    for r in range(QCH):
                        i = QCH * ch + r
                        if r == 0 and ch >= 2:
                            dve.wait_ge(s.o_ready, ch - 1)
                        ps = pieces(i)
                        for m, (p0, p1) in enumerate(ps):
                            dve.wait_ge(s.scored, st.score + 1)
                            part = a.low[:, i:i + 1] if len(ps) == 1 else a.low2[:, m, i:i + 1]
                            scores = ps_s[:, st.score % 2, 0:p1 - p0]
                            bias = a.neg_cum[:, p0:p1] if causal else a.zeros[:, 0:p1 - p0]
                            dve.tensor_tensor_reduce(a.probs[:, ch % 2, r, p0:p1], scores, bias, -1.0, BIG, ALU.add, ALU.min,
                                                     part).then_inc(s.min1, 1)
                            st.score += 1
                        if len(ps) == 2:
                            dve.wait_ge(s.min1, st.score)
                            dve.tensor_tensor(a.low[:, i:i + 1], a.low2[:, 0, i:i + 1], a.low2[:, 1, i:i + 1], ALU.min).then_inc(s.min2, 1)

                def split(ch):
                    for j in range(key_tiles(ch)):
                        r0 = max(0, j - QCH * ch) if causal else 0
                        dve.wait_ge(s.t_hi, st.pv + 1)
                        dve.tensor_tensor(a.p_lo[:, st.pv % 2, r0 * P:], ps_t[:, st.turn % 2, r0 * P:], a.p_hi[:, st.pv % 2, r0 * P:].bitcast(F32),
                                          ALU.subtract).then_inc(s.t_split, 1)
                        st.pv += 1
                        st.turn += 1
                    part = slice(QCH * ch, QCH * ch + QCH)
                    dve.reciprocal(a.inv[:, part], a.sums[:, part]).then_inc(s.inverted, 1)
                    dve.wait_ge(s.inverted, ch + 1)
                    dve.wait_ge(s.o_ready, ch + 1)
                    dve.tensor_tensor(a.o_out[:, ch, :, :], ps_t[:, st.turn % 2, 0:QCH * HD].rearrange("p (r d) -> p r d", d=HD),
                                      a.inv[:, part].unsqueeze(2).to_broadcast([P, QCH, HD]), ALU.mult).then_inc(s.o_out, 1)
                    st.turn += 1

                for what, ch in order:
                    lows(ch) if what == "A" else split(ch)
                if values:
                    dve.wait_ge(s.v_used, PAGES)
                    dve.tensor_tensor(values.own[0:FH, :], ps_v[0:FH, :], c.own_head[0:FH, :], ALU.mult).then_inc(s.v_masked, 1)


def mix(nc, c, n, w, gain, assemble, x_src, dst, rows=P):
    with ExitStack() as ctx:
        sb, psum = alloc(ctx, nc)
        y = sb("y", [P, 2, D])
        yn = sb("y_normed", [P, D])
        y_hi = sb("y_hi", [P, 2, DT, P], F32R)
        y_lo = sb("y_lo", [P, 2, DT, P], F32R)
        x = sb("x_res", [P, 2, D])
        junk = sb("squares", [P, D])
        ss = sb("sum_squares", [P, n, 3])
        rstd = sb("rstd", [P, n, 3])
        ps_t = psum("ps_transposed", [P, 2, BLK])
        ps_y = psum("ps_y", [P, 2, D])
        groups = [(0, CW), (CW, FW), (CW + FW, MW)]
        with stage(nc, "fox0 fox1 parts0 parts1 xin0 xin1 conv conv_step squared var rstd normed turned hi_done lo_done made res store0 store1") as (block, s):
            parts = (s.parts0, s.parts1)
            fox = (s.fox0, s.fox1)
            xin = (s.xin0, s.xin1)
            stores = (s.store0, s.store1)

            @block.sync
            def _(sp):
                for k in range(n + 2):
                    if k < n:
                        assemble.load(sp, s, k, y, parts[k % 2], fox[k % 2])
                    if k >= 2:
                        sp.wait_ge(s.res, k - 1)
                        sp.dma_start(dst(k - 2), x[0:rows, k % 2, :]).then_inc(stores[k % 2], 16)
                    if k < n:
                        if k >= 2:
                            sp.wait_ge(stores[k % 2], 16 * (k // 2))
                        sp.dma_start(x[0:rows, k % 2, :], x_src(k)).then_inc(xin[k % 2], 16)
                for k in range(min(n, 2)):
                    sp.wait_ge(stores[k], 16 * ((n - k + 1) // 2))

            @block.gpsimd
            def _(pool):
                for k in range(n):
                    assemble.conv(pool, s, k, y, parts[k % 2])
                    pool.wait_ge(s.squared, k + 1)
                    for m, (g0, gw) in enumerate(groups):
                        scaled = pool.tensor_scalar(rstd[:, k, m:m + 1], ss[:, k, m:m + 1], 1.0 / gw, EPS, ALU.mult, ALU.add)
                    scaled.then_inc(s.var, 1)
                    pool.wait_ge(s.var, k + 1)
                    pool.tensor_tensor(rstd[:, k, :], rstd[:, k, :], c.minus_half[:].to_broadcast([P, 3]), ALU.pow).then_inc(s.rstd, 1)

            @block.scalar
            def _(act):
                def square(k):
                    act.wait_ge(s.conv, k + 1)
                    assemble.ready(act, s, k, fox[k % 2])
                    if k >= 1:
                        act.wait_ge(s.squared, k)
                    for m, (g0, gw) in enumerate(groups):
                        done = act.activation(junk[:, g0:g0 + gw], y[:, k % 2, g0:g0 + gw], ACT.Square, accum_out=ss[:, k, m:m + 1])
                    done.then_inc(s.squared, 1)

                square(0)
                for k in range(n):
                    if k + 1 < n:
                        square(k + 1)
                    for j in range(2):
                        u = 2 * k + j
                        act.wait_ge(s.turned, u + 1)
                        if k >= 2:
                            act.wait_ge(s.made, k - 1)
                        act.activation(y_hi[:, k % 2, 4 * j:4 * j + 4, :], ps_t[:, j, :].rearrange("p (d t) -> p d t", d=4), ACT.Copy).then_inc(s.hi_done, 1)

            @block.vector
            def _(dve):
                def normalise(k):
                    dve.wait_ge(s.rstd, k + 1)
                    if k >= 1:
                        dve.wait_ge(s.turned, 2 * k)
                    for m, (g0, gw) in enumerate(groups):
                        done = dve.scalar_tensor_tensor(out=yn[:, g0:g0 + gw], in0=y[:, k % 2, g0:g0 + gw], scalar=rstd[:, k, m:m + 1],
                                                        in1=gain[:, g0:g0 + gw], op0=ALU.mult, op1=ALU.mult)
                    done.then_inc(s.normed, 1)

                def split(k):
                    for j in range(2):
                        u = 2 * k + j
                        dve.wait_ge(s.hi_done, u + 1)
                        dve.tensor_tensor(y_lo[:, k % 2, 4 * j:4 * j + 4, :], ps_t[:, j, :].rearrange("p (d t) -> p d t", d=4),
                                          y_hi[:, k % 2, 4 * j:4 * j + 4, :].bitcast(F32), ALU.subtract).then_inc(s.lo_done, 1)

                def residual(k):
                    dve.wait_ge(s.made, k + 1)
                    dve.wait_ge(xin[k % 2], 16 * (k // 2 + 1))
                    dve.tensor_tensor(x[0:rows, k % 2, :], ps_y[0:rows, k % 2, :], x[0:rows, k % 2, :], ALU.add).then_inc(s.res, 1)

                for k in range(n):
                    normalise(k)
                    split(k)
                    if k >= 1:
                        residual(k - 1)
                residual(n - 1)

            @block.tensor
            def _(pe):
                def turn(k):
                    pe.wait_ge(s.normed, k + 1)
                    for j in range(2):
                        if k >= 1:
                            pe.wait_ge(s.lo_done, 2 * k - 1 + j)
                        for d in range(4):
                            turned = pe.transpose(ps_t[:, j, d * P:(d + 1) * P], yn[:, (4 * j + d) * P:(4 * j + d + 1) * P], c.ident[:])
                        turned.then_inc(s.turned, 1)

                turn(0)
                for k in range(n):
                    if k + 1 < n:
                        turn(k + 1)
                    pe.wait_ge(s.lo_done, 2 * k + 2)
                    if k >= 2:
                        pe.wait_ge(s.res, k - 1)
                    for e in range(2):
                        for d in range(DT):
                            out = ps_y[:, k % 2, e * BLK:(e + 1) * BLK]
                            cols = slice(e * BLK, (e + 1) * BLK)
                            pe.matmul(out, y_hi[:, k % 2, d, :], w.hi[:, d, cols], start=(d == 0), stop=False)
                            pe.matmul(out, y_hi[:, k % 2, d, :], w.lo[:, d, cols], start=False, stop=False)
                            mm = pe.matmul(out, y_lo[:, k % 2, d, :], w.hi[:, d, cols], start=False, stop=(d == DT - 1))
                    mm.then_inc(s.made, 1)


def ffn(nc, c, n, h_hi, h_lo, x1, io, gain_f, w, act_hi, act_lo, dst, rows=P):
    T = n * P
    R = 4
    items = [(kind, f) for f in range(FT) for kind in ("gate", "up")] + [("down", f) for f in range(FT)]
    with ExitStack() as ctx:
        sb, psum = alloc(ctx, nc)
        sil = sb("silu", [P, 2, T])
        prod = sb("silu_up", [P, T])
        ss = sb("sum_squares", [P, n])
        rstd = sb("rstd", [P, n])
        names = "w_in0 w_in1 w_in2 w_in3 w_hi w_lo w_used silu_done prod_done a_hi a_lo res squared var rstd normed stored"
        ps = psum("ps_ffn", [P, 8, BLK])
        with stage(nc, names) as (block, s):
            w_in = (s.w_in0, s.w_in1, s.w_in2, s.w_in3)

            @block.sync
            def _(sp):
                for i, (kind, f) in enumerate(items):
                    if i >= R:
                        sp.wait_ge(s.w_lo, i - R + 1)
                    if kind == "down":
                        src = io.w_down[f * P:(f + 1) * P, :]
                        to = w.raw[:, i % R, :]
                    else:
                        table = io.w_gate if kind == "gate" else io.w_up
                        src = table.rearrange("(d p) n -> p d n", p=P)[:, :, f * P:(f + 1) * P]
                        to = w.raw[:, i % R, :].rearrange("p (d n) -> p d n", d=DT)
                    sp.dma_start(to, src).then_inc(w_in[i % R], 16)
                for k in range(n):
                    sp.wait_ge(s.normed, k + 1)
                    sp.dma_start(dst(k), x1[0:rows, k, :]).then_inc(s.stored, 16)
                sp.wait_ge(s.stored, 16 * n)

            @block.gpsimd
            def _(pool):
                for k in range(n):
                    pool.wait_ge(s.squared, k + 1)
                    pool.tensor_scalar(rstd[:, k:k + 1], ss[:, k:k + 1], 1.0 / D, EPS, ALU.mult, ALU.add).then_inc(s.var, 1)
                    pool.wait_ge(s.var, k + 1)
                    pool.tensor_tensor(rstd[:, k:k + 1], rstd[:, k:k + 1], c.minus_half[:], ALU.pow).then_inc(s.rstd, 1)

            def split_hi(act, i):
                act.wait_ge(w_in[i % R], 16 * (i // R + 1))
                if i >= R:
                    act.wait_ge(s.w_used, i - R + 1)
                act.activation(w.hi[:, i % R, :], w.raw[:, i % R, :], ACT.Copy).then_inc(s.w_hi, 1)

            def split_lo(dve, i):
                dve.wait_ge(s.w_hi, i + 1)
                dve.tensor_tensor(w.lo[:, i % R, :], w.raw[:, i % R, :], w.hi[:, i % R, :].bitcast(F32), ALU.subtract).then_inc(s.w_lo, 1)

            AHEAD = R - 1

            @block.scalar
            def _(act):
                for i in range(AHEAD):
                    split_hi(act, i)
                for f in range(FT):
                    split_hi(act, 2 * f + AHEAD)
                    act.wait_ge(s.w_used, 2 * f + 1)
                    if f >= 2:
                        act.wait_ge(s.prod_done, f - 1)
                    act.activation(sil[:, f % 2, :], ps[:, f % 2, 0:T], ACT.Silu).then_inc(s.silu_done, 1)
                    split_hi(act, 2 * f + 1 + AHEAD)
                    act.wait_ge(s.prod_done, f + 1)
                    act.activation(act_hi[:, f, 0:T], prod[:], ACT.Copy).then_inc(s.a_hi, 1)
                for f in range(FT - AHEAD):
                    split_hi(act, 2 * FT + f + AHEAD)
                for k in range(n):
                    act.wait_ge(s.res, k + 1)
                    act.activation(w.junk[:], x1[:, k, :], ACT.Square, accum_out=ss[:, k:k + 1]).then_inc(s.squared, 1)
                    if k + 1 < n:
                        act.wait_ge(s.squared, k + 1)

            @block.vector
            def _(dve):
                for i in range(AHEAD):
                    split_lo(dve, i)
                for f in range(FT):
                    split_lo(dve, 2 * f + AHEAD)
                    split_lo(dve, 2 * f + 1 + AHEAD)
                    dve.wait_ge(s.silu_done, f + 1)
                    dve.wait_ge(s.w_used, 2 * f + 2)
                    if f >= 1:
                        dve.wait_ge(s.a_lo, f)
                    dve.tensor_tensor(prod[:], ps[:, 2 + f % 2, 0:T], sil[:, f % 2, :], ALU.mult).then_inc(s.prod_done, 1)
                    dve.wait_ge(s.a_hi, f + 1)
                    dve.tensor_tensor(act_lo[:, f, 0:T], prod[:], act_hi[:, f, 0:T].bitcast(F32), ALU.subtract).then_inc(s.a_lo, 1)
                for f in range(FT - AHEAD):
                    split_lo(dve, 2 * FT + f + AHEAD)
                dve.wait_ge(s.w_used, len(items))
                for k in range(n):
                    dve.tensor_tensor(x1[:, k, :], ps[:, 2 * k:2 * k + 2, :].rearrange("p a n -> p (a n)"), x1[:, k, :], ALU.add).then_inc(s.res, 1)
                for k in range(n):
                    dve.wait_ge(s.rstd, k + 1)
                    dve.scalar_tensor_tensor(out=x1[:, k, :], in0=x1[:, k, :], scalar=rstd[:, k:k + 1], in1=gain_f[:],
                                             op0=ALU.mult, op1=ALU.mult).then_inc(s.normed, 1)

            @block.tensor
            def _(pe):
                for i, (kind, f) in enumerate(items):
                    pe.wait_ge(s.w_lo, i + 1)
                    hi, lo = w.hi[:, i % R, :], w.lo[:, i % R, :]
                    if kind != "down":
                        if f >= 2:
                            pe.wait_ge(s.prod_done, f - 1)
                        out = ps[:, f % 2 + (0 if kind == "gate" else 2), 0:T]
                        for d in range(DT):
                            a_hi, a_lo = hi[:, d * P:(d + 1) * P], lo[:, d * P:(d + 1) * P]
                            pe.matmul(out, a_hi, h_hi[:, d, 0:T], start=(d == 0), stop=False)
                            pe.matmul(out, a_hi, h_lo[:, d, 0:T], start=False, stop=False)
                            mm = pe.matmul(out, a_lo, h_hi[:, d, 0:T], start=False, stop=(d == DT - 1))
                        mm.then_inc(s.w_used, 1)
                        continue
                    if f == 0:
                        pe.wait_ge(s.prod_done, FT)
                    pe.wait_ge(s.a_lo, min(FT, f + 1))
                    for k in range(n):
                        for e in range(2):
                            out = ps[:, 2 * k + e, :]
                            cols = slice(e * BLK, (e + 1) * BLK)
                            a_hi, a_lo = act_hi[:, f, k * P:(k + 1) * P], act_lo[:, f, k * P:(k + 1) * P]
                            pe.matmul(out, a_hi, hi[:, cols], start=(f == 0), stop=False)
                            pe.matmul(out, a_hi, lo[:, cols], start=False, stop=False)
                            mm = pe.matmul(out, a_lo, hi[:, cols], start=False, stop=(f == FT - 1))
                    mm.then_inc(s.w_used, 1)


class PromptTiles:

    def __init__(self, sb, conv_w, scratch, first):
        self.gate = sb("conv_gate", [P, 2, CW])
        self.ch = sb("conv_c_h", [P, 2, 3, 2 * CW])
        self.u = sb("conv_u", [P, 3, CW])
        self.sum = sb("conv_sum", [P, CW])
        self.w, self.scratch, self.first = conv_w, scratch, first

    def load(self, sp, s, k, y, parts, fox):
        row = (self.first + k) * P
        proj = self.scratch.proj
        if k >= 2:
            sp.wait_ge(s.normed, k - 1)
        sp.dma_start(self.gate[:, k % 2, :], proj[ds(row + PAD, P), 0:CW]).then_inc(parts, 16)
        for back in range(3):
            sp.dma_start(self.ch[:, k % 2, back, :], proj[ds(row + PAD - back, P), CW:3 * CW]).then_inc(parts, 16)
        sp.dma_start(y[:, k % 2, CW:CW + FW], self.scratch.fox[ds(row, P), :]).then_inc(fox, 16)
        sp.dma_start(y[:, k % 2, CW + FW:D], self.scratch.mem[ds(row, P), :]).then_inc(fox, 16)

    def ready(self, act, s, k, fox):
        act.wait_ge(fox, 32 * (k // 2 + 1))

    def conv(self, pool, s, k, y, parts):
        steps = 4 * k
        pool.wait_ge(parts, 64 * (k // 2 + 1))
        pool.tensor_tensor(self.u[:], self.ch[:, k % 2, :, 0:CW], self.ch[:, k % 2, :, CW:2 * CW], ALU.mult).then_inc(s.conv_step, 1)
        pool.wait_ge(s.conv_step, steps + 1)
        pool.tensor_tensor(self.u[:], self.u[:], self.w[:], ALU.mult).then_inc(s.conv_step, 1)
        pool.wait_ge(s.conv_step, steps + 2)
        pool.tensor_tensor(self.sum[:], self.u[:, 2, :], self.u[:, 1, :], ALU.add).then_inc(s.conv_step, 1)
        pool.wait_ge(s.conv_step, steps + 3)
        pool.tensor_tensor(self.sum[:], self.sum[:], self.u[:, 0, :], ALU.add).then_inc(s.conv_step, 1)
        pool.wait_ge(s.conv_step, steps + 4)
        pool.tensor_tensor(y[:, k % 2, 0:CW], self.sum[:], self.gate[:, k % 2, :], ALU.mult).then_inc(s.conv, 1)


class SampleTile:

    def __init__(self, src):
        self.src = src

    def load(self, sp, s, k, y, parts, fox):
        sp.wait_ge(s.conv, 1)
        sp.dma_start(y[0:DB, 0, :], self.src).then_inc(fox, 16)

    def ready(self, act, s, k, fox):
        act.wait_ge(fox, 16)

    def conv(self, pool, s, k, y, parts):
        pool.memset(y[:, 0, :], 0.0).then_inc(s.conv, 1)


def sample_outputs(nc, c, io, scratch, dec, conv_w, y):
    with ExitStack() as ctx:
        sb, _ = alloc(ctx, nc)
        rows = sb("rows", [P, PW])
        fox = sb("fox_rows", [P, FW])
        state = sb("state", [P, 3, CW])
        u = sb("weighted", [P, 3, CW])
        new = sb("new_value", [P, FW])
        last = sb("last_c_h", [P, 2 * CW])
        last_u = sb("last_u", [P, CW])
        with stage(nc, "loaded chain stored") as (block, s):

            @block.sync
            def _(sp):
                sp.dma_start(rows[0:DB, :], scratch.samp).then_inc(s.loaded, 16)
                sp.dma_start(fox[0:DB, :], scratch.samp_fox).then_inc(s.loaded, 16)
                sp.dma_start(state[0:DB, 0:2, :], io.state_conv.rearrange("l b k c -> (l b) k c")).then_inc(s.loaded, 16)
                sp.dma_start(last[0:PAD, :], scratch.proj[SEQ:SEQ + PAD, CW:3 * CW]).then_inc(s.loaded, 16)
                sp.wait_ge(s.chain, 8)
                sp.dma_start(io.new_conv_s.rearrange("b k c -> b k c"), state[0:DB, 1:3, :]).then_inc(s.stored, 16)
                sp.dma_start(io.new_conv, last_u[0:PAD, :]).then_inc(s.stored, 16)
                sp.dma_start(scratch.samp_y, y[0:DB, :]).then_inc(s.stored, 16)
                sp.wait_ge(s.stored, 48)

            @block.vector
            def _(dve):
                chain = [0]

                def link(ins):
                    chain[0] += 1
                    ins.then_inc(s.chain, 1)
                    dve.wait_ge(s.chain, chain[0])

                heads = [DB, FH, HD]
                dve.wait_ge(s.loaded, 64)
                dve.tensor_tensor(last_u[0:PAD, :], last[0:PAD, 0:CW], last[0:PAD, CW:], ALU.mult)
                link(dve.tensor_tensor(state[0:DB, 2, :], rows[0:DB, CW:2 * CW], rows[0:DB, 2 * CW:3 * CW], ALU.mult))
                for back in range(3):
                    done = dve.tensor_tensor(u[0:DB, back, :], state[0:DB, 2 - back, :], conv_w[0:DB, back, :], ALU.mult)
                link(done)
                link(dve.tensor_tensor(u[0:DB, 2, :], u[0:DB, 2, :], u[0:DB, 1, :], ALU.add))
                link(dve.tensor_tensor(u[0:DB, 2, :], u[0:DB, 2, :], u[0:DB, 0, :], ALU.add))
                link(dve.tensor_tensor(y[0:DB, 0:CW], u[0:DB, 2, :], rows[0:DB, 0:CW], ALU.mult))
                link(dve.tensor_tensor(new[0:DB, :].rearrange("p (h d) -> p h d", d=HD), rows[0:DB, VCOL:VCOL + FW].rearrange("p (h d) -> p h d", d=HD),
                                       dec.w_new[0:DB, :].unsqueeze(2).to_broadcast(heads), ALU.mult))
                link(dve.tensor_tensor(new[0:DB, :], new[0:DB, :], fox[0:DB, :], ALU.add))
                link(dve.tensor_tensor(y[0:DB, CW:CW + FW].rearrange("p (h d) -> p h d", d=HD), new[0:DB, :].rearrange("p (h d) -> p h d", d=HD),
                                       dec.r_fox[0:DB, :].unsqueeze(2).to_broadcast(heads), ALU.mult))


def load(nc, pairs):
    with stage(nc, "loaded") as (block, s):

        @block.sync
        def _(sp):
            for dst, src in pairs:
                sp.dma_start(dst, src).then_inc(s.loaded, 16)
            sp.wait_ge(s.loaded, 16 * len(pairs))


def decoder_step(nc, io):
    def dram(name, shape):
        return nc.dram_tensor(name, shape, F32, kind="Internal").ap()

    scratch = group(proj=io.proj, samp=io.samp, gates=dram("gate_logits", (FH, SEQ + P)), neg_cum=dram("neg_cum", (FH, SEQ)), fox=dram("fox", (SEQ, FW)),
                              mem=dram("mem", (SEQ, MW)), x1=dram("x1", (SEQ, D)), samp_fox=dram("samp_fox", (DB, FW)),
                              samp_y=dram("samp_y", (DB, D)), samp_x1=dram("samp_x1", (DB, D)))
    w_in = io.w_in.rearrange("(d p) n -> p d n", p=P)
    w_mem = io.w_mem_kv.rearrange("(d p) n -> p d n", p=P)
    last_page = io.cache_k.shape[1] - 1
    key_pages = io.cache_k.rearrange("l n r h d -> (l n) r (h d)")
    value_pages = io.cache_v.rearrange("l n r h d -> (l n) r (h d)")

    with ExitStack() as whole:
        sb, _ = alloc(whole, nc)
        c = group(ident=sb("ident", [P, P]), ident_r=sb("ident_r", [P, P], F32R), causal_r=sb("causal_r", [P, P], F32R),
                            page_before=sb("page_before", [P, P]), seq_of_page=sb("seq_of_page", [P, 2, DB]),
                            own_head=sb("own_head", [P, FW]), fold=sb("fold", [P, HD]), ones=sb("ones", [P, 1]),
                            minus_half=sb("minus_half", [P, 1]), b_f=sb("b_f", [P, 1]), pages=sb("pages", [1, DB * PAGES], I32),
                            page_index=sb("page_index", [P, 2], U32),
                  gathered=whole.enter_context(nc.semaphore("gathered")))
        early = whole.enter_context(ExitStack())
        early_sb, _ = alloc(early, nc)
        y_samp = early_sb("y_samp", [P, D])
        dec = group(scores=early_sb("scores", [P, DB * PAGES * FH]), mem_scores=early_sb("mem_scores", [P, DB * 2 * MH]),
                              logf_new=early_sb("logf_new", [P, FH]), w_new=early_sb("w_new", [P, FH]), r_fox=early_sb("r_fox", [P, FH]), r_mem=early_sb("r_mem", [P, MH]))
        setup_constants(nc, c, io)

        with ExitStack() as ctx:
            sb, _ = alloc(ctx, nc)
            h_hi = sb("h_hi", [P, DT, HALF * P], F32R)
            h_lo = sb("h_lo", [P, DT, HALF * P], F32R)
            w = group(raw=sb("w_raw", [P, DT, BLK]), hi=sb("w_hi", [P, 2, DT, BLK], F32R), lo=sb("w_lo", [P, 2, DT, BLK], F32R))
            wf_hi = sb("wf_hi", [P, DT, P], F32R)
            wf_lo = sb("wf_lo", [P, DT, P], F32R)
            with ExitStack() as inner:
                gain = inner.enter_context(nc.sbuf_tensor("gain_mem", [P, D], F32))
                zero = inner.enter_context(nc.sbuf_tensor("zero_rows", [PAD, 2 * CW], F32))
                with stage(nc, "loaded zeroed stored") as (block, s):

                    @block.gpsimd
                    def _(pool):
                        pool.memset(zero[:], 0.0).then_inc(s.zeroed, 1)

                    @block.sync
                    def _(sp):
                        sp.dma_start(gain[:], io.mem_norm_g.to_broadcast([P, D])).then_inc(s.loaded, 16)
                        sp.wait_ge(s.zeroed, 1)
                        sp.dma_start(scratch.proj[0:PAD, CW:3 * CW], zero[:]).then_inc(s.stored, 16)
                        sp.wait_ge(s.loaded, 16)
                        sp.wait_ge(s.stored, 16)
                split_weights(nc, w.raw[:], w.hi[:, 1, :, :], w.lo[:, 1, :, :], [(w.raw[:], w_mem)])
                norm_transpose(nc, c, 2, lambda k: io.mem_prompt[k * P:(k + 1) * P, :], gain[:], h_hi, h_lo)

            def block_columns(n):
                return [(w.raw[:, :, 0:CW], w_in[:, :, ds(n * BLK, CW)]),
                        (w.raw[:, :, CW:BLK], w_in[:, :, ds(n * BLK + CW + (n // (NBLK - 1)) * FH, CW)])]

            project(nc, c, 2, h_hi, h_lo, w, 1, lambda t: io.mem_kv[t * P:(t + 1) * P, :], following=block_columns(0))
            gain = sb("gain1", [P, D])
            load(nc, [(gain[:], io.norm1_g.to_broadcast([P, D]))])
            split_weights(nc, w.raw[:, :, 0:P], wf_hi[:], wf_lo[:], [(w.raw[:, :, 0:P], w_in[:, :, FCOL:FCOL + P])])
            norm_transpose(nc, c, 1, lambda k: io.x_sample[:, :], gain[:], h_hi, h_lo, rows=DB, gates=(wf_hi, wf_lo, scratch.gates[:, SEQ:]))
            with nc.Fori(0, NBLK) as n:
                project(nc, c, 1, h_hi, h_lo, w, n % 2, lambda t: scratch.samp[:, ds(n * BLK, BLK)], rows=DB,
                        following=block_columns((n + 1) % NBLK))
            for half in range(2):
                first = half * HALF
                norm_transpose(nc, c, HALF, lambda k: io.x_prompt[(first + k) * P:(first + k + 1) * P, :], gain[:], h_hi, h_lo,
                               gates=(wf_hi, wf_lo, scratch.gates[:, first * P:(first + HALF) * P]))
                for n0, n1 in ((0, NBLK),) if half == 0 else ((0, DB - NBLK), (DB - NBLK, NBLK)):
                    with nc.Fori(n0, n1) as n:
                        seq = n + half * NBLK
                        keys = None
                        if n0 == 0:
                            keys = group(seq=seq, scores=dec.scores, cache=key_pages, last_page=last_page,
                                                   query=scratch.samp[ds(seq, 1), QCOL:QCOL + FW].to_broadcast([P, FW]))
                        project(nc, c, HALF, h_hi, h_lo, w, (n + half + 1) % 2,
                                lambda t: scratch.proj[PAD + (first + t) * P:PAD + (first + t + 1) * P, ds(n * BLK, BLK)],
                                following=block_columns((n + 1) % NBLK), keys=keys)
        with ExitStack() as ctx:
            sb, _ = alloc(ctx, nc)
            gates = sb("gates2", [P, SEQ + P])
            load(nc, [(gates[0:FH, :], scratch.gates)])
            forget_gates(nc, c, gates, io, scratch, dec)
        decode_softmax(nc, c, io, scratch, dec)

        decode_memory_values(nc, c, io, dec, y_samp[:, CW + FW:D])
        with ExitStack() as ctx:
            sb, _ = alloc(ctx, nc)
            a = group(q=sb("q_raw", [P, NT, 2, HD]), k=sb("k_raw", [P, NT, 2, HD]), v=sb("v_raw", [P, NT, HD]),
                                neg_cum=sb("neg_cum_all", [P, SEQ]), k_st=sb("k_stacked", [P, SEQ], F32R),
                                q_hi=sb("q_hi", [P, SEQ], F32R), q_lo=sb("q_lo", [P, SEQ], F32R), v_st=sb("v_stacked", [P, NT, P], F32R),
                                probs=sb("probs", [P, 2, QCH, SEQ]), p_hi=sb("p_hi", [P, 2, BLK], F32R), p_lo=sb("p_lo", [P, 2, BLK], F32R),
                                o_t=sb("o_turned", [P, 2, BLK]), o_out=sb("o_out", [P, QCH, QCH, HD]), low=sb("low", [P, NT]),
                                low2=sb("low2", [P, 2, NT]), sums=sb("row_sums", [P, NT]), inv=sb("inverse", [P, NT]), zeros=sb("zeros", [P, MEM]))
            page_v = sb("page_v", [P, 4, FW])
            weights = sb("weights", [P, PAGES * FH])
            own = sb("own", [P, FW])
            row = sb("row", [P, FW])

            def fox_head(h):
                return group(q=scratch.proj[PAD:, ds(h * HD + QCOL, HD)], k=scratch.proj[PAD:, ds(h * HD + KCOL, HD)],
                                       v=scratch.proj[PAD:, ds(h * HD + VCOL, HD)], neg_cum=scratch.neg_cum[ds(h, 1), :])

            def mem_head(h):
                return group(q=scratch.proj[PAD:, ds(h * HD + MCOL, HD)], k=io.mem_kv[:, ds(h * HD, HD)],
                                       v=io.mem_kv[:, ds(h * HD + MW, HD)], neg_cum=None)

            def first_head(head, nk):
                with stage(nc, "loaded") as (block, s):

                    @block.sync
                    def _(sp):
                        sp.wait_ge(s.loaded, load_head(sp, a, head, nk, s.loaded))

                    @block.gpsimd
                    def _(pool):
                        pool.memset(a.zeros[:], 0.0)

            first_head(fox_head(0), NT)
            with nc.Fori(0, FH) as h:
                values = group(seq=h, cache=value_pages, last_page=last_page, page_v=page_v, weights=weights, own=own, row=row,
                                         all_weights=dec.scores[:, ds(h * (PAGES * FH), PAGES * FH)], dst=scratch.samp_fox[ds(h, 1), :])
                attend(nc, c, a, NT, True, fox_head((h + 1) % FH),
                       lambda ch: scratch.fox[ch * BLK:(ch + 1) * BLK, ds(h * HD, HD)].rearrange("(r p) d -> p r d", p=P), values)
            first_head(mem_head(0), 2)
            with nc.Fori(0, MH) as h:
                attend(nc, c, a, 2, False, mem_head((h + 1) % MH),
                       lambda ch: scratch.mem[ch * BLK:(ch + 1) * BLK, ds(h * HD, HD)].rearrange("(r p) d -> p r d", p=P))

        with ExitStack() as ctx:
            sb, _ = alloc(ctx, nc)
            w = group(hi=sb("wo_hi", [P, DT, D], F32R), lo=sb("wo_lo", [P, DT, D], F32R))
            gain = sb("gain_out", [P, D])
            conv_w = sb("conv_w", [P, 3, CW])
            load(nc, [(gain[:], io.out_norm_g.to_broadcast([P, D]))] +
                 [(conv_w[:, back, :], io.conv_w[2 - back:3 - back, :].to_broadcast([P, CW])) for back in range(3)])
            with ExitStack() as inner:
                raw = inner.enter_context(nc.sbuf_tensor("wo_raw", [P, DT, D], F32))
                split_weights(nc, raw[:], w.hi[:], w.lo[:], [(raw[:], io.w_out.rearrange("(d p) n -> p d n", p=P))])
            sample_outputs(nc, c, io, scratch, dec, conv_w, y_samp)
            mix(nc, c, 1, w, gain, SampleTile(scratch.samp_y), lambda k: io.x_sample, lambda k: scratch.samp_x1, rows=DB)
            with nc.Fori(0, NT // QCH) as ch:
                with ExitStack() as inner:
                    tiles = PromptTiles(alloc(inner, nc)[0], conv_w, scratch, ch * QCH)
                    mix(nc, c, QCH, w, gain, tiles, lambda k: io.x_prompt[ds((ch * QCH + k) * P, P), :],
                        lambda k: scratch.x1[ds((ch * QCH + k) * P, P), :])

        early.close()

        with ExitStack() as ctx:
            sb, _ = alloc(ctx, nc)
            T = QCH * P
            x1 = sb("x1_tiles", [P, QCH, D])
            h_hi = sb("h2_hi", [P, DT, T], F32R)
            h_lo = sb("h2_lo", [P, DT, T], F32R)
            gain2 = sb("gain2", [P, D])
            gain_f = sb("gain_f", [P, D])
            load(nc, [(gain2[:], io.norm2_g.to_broadcast([P, D])), (gain_f[:], io.final_norm_g.to_broadcast([P, D]))])

            def feed_forward(n, src, dst, rows):
                norm_transpose(nc, c, n, src, gain2[:], h_hi, h_lo, rows=rows, keep=x1)
                with ExitStack() as inner:
                    isb = alloc(inner, nc)[0]
                    w = group(raw=isb("w_items", [P, 4, D]), hi=isb("w_items_hi", [P, 4, D], F32R), lo=isb("w_items_lo", [P, 4, D], F32R),
                              junk=isb("squares_f", [P, D]))
                    act_hi = isb("act_hi", [P, FT, n * P], F32R)
                    act_lo = isb("act_lo", [P, FT, n * P], F32R)
                    ffn(nc, c, n, h_hi, h_lo, x1, io, gain_f, w, act_hi, act_lo, dst, rows)

            feed_forward(1, lambda k: scratch.samp_x1, lambda k: io.y_sample, DB)
            with nc.Fori(0, NT // QCH) as ch:
                feed_forward(QCH, lambda k: scratch.x1[ds((ch * QCH + k) * P, P), :], lambda k: io.y_prompt[ds((ch * QCH + k) * P, P), :], P)


_INS = ["x_prompt", "x_sample", "mem_prompt", "cache_k", "cache_v", "cache_logf", "state_conv", "cache_mem_k", "cache_mem_v",
        "page_table", "norm1_g", "w_in", "b_f", "conv_w", "mem_norm_g", "w_mem_kv", "out_norm_g", "w_out", "norm2_g",
        "w_gate", "w_up", "w_down", "final_norm_g"]
_OUTS = {"y_prompt": (SEQ, D), "y_sample": (DB, D), "proj": (PAD + SEQ, PW), "samp": (DB, PW), "mem_kv": (MEM, 2 * MW),
         "new_logf": (SEQ, FH), "new_logf_s": (DB, FH), "new_conv": (PAD, CW), "new_conv_s": (DB, PAD, CW)}
_FLAT = {"x_prompt": (SEQ, D), "x_sample": (DB, D), "mem_prompt": (MEM, D), "w_in": None, "conv_w": None, "w_mem_kv": None,
         "w_out": None, "w_gate": None, "w_up": None, "w_down": None, "final_norm_g": (1, D)}


def kernel(**inputs):
    import numpy as np
    import concourse.bacc as bacc
    from concourse.bass_utils import run_bass_kernel_spmd

    nc = bacc.Bacc("TRN2", target_bir_lowering=False, num_devices=1)
    arrays, io = {}, {}
    for name in _INS:
        a = np.ascontiguousarray(inputs[name])
        if name in _FLAT:
            a = a.reshape(_FLAT[name] or a.shape[1:])
        arrays[f"in_{name}"] = a
        io[name] = nc.dram_tensor(f"in_{name}", a.shape, mybir.dt.from_np(a.dtype), kind="ExternalInput").ap()
    for name, shape in _OUTS.items():
        io[name] = nc.dram_tensor(f"out_{name}", shape, F32, kind="ExternalOutput").ap()
    decoder_step(nc, group(**io))
    r = run_bass_kernel_spmd(nc, [arrays], core_ids=[0]).results[0]
    out = {name: r[f"out_{name}"] for name in _OUTS}
    proj, samp, mem_kv = out["proj"][PAD:], out["samp"], out["mem_kv"]
    heads = (1, 1, SEQ, FH, HD)
    sample_heads = (1, DB, 1, FH, HD)
    return (out["y_prompt"].reshape(1, SEQ, D), out["y_sample"].reshape(DB, 1, D),
            proj[:, KCOL:KCOL + FW].reshape(heads), proj[:, VCOL:VCOL + FW].reshape(heads),
            out["new_logf"].reshape(1, 1, SEQ, FH), out["new_conv"].reshape(1, 1, PAD, CW),
            mem_kv[:, 0:MW].reshape(1, 1, MEM, MH, HD), mem_kv[:, MW:].reshape(1, 1, MEM, MH, HD),
            samp[:, KCOL:KCOL + FW].reshape(sample_heads), samp[:, VCOL:VCOL + FW].reshape(sample_heads),
            out["new_logf_s"].reshape(1, DB, 1, FH), out["new_conv_s"].reshape(1, DB, PAD, CW))
```

```python
from collections import namedtuple
from contextlib import ExitStack, contextmanager

import concourse.bass as bass
from concourse import mybir

F32 = mybir.dt.float32
F32R = mybir.dt.float32r
I32 = mybir.dt.int32
U32 = mybir.dt.uint32
ALU = mybir.AluOpType
ACT = mybir.ActivationFunctionType
AX = mybir.AxisListType
RMAX = bass.bass_isa.ReduceOp.max
RADD = bass.bass_isa.ReduceOp.add
ds = bass.ds

P = 128
D = 1024
SEQ = 2048
HD = 64
CW = 256
FW = 512
MW = 256
FH = FW // HD
MH = MW // HD
MEM = 256
DB = 8
PAGES = 32
D_FF = 2816
DT = D // P
NT = SEQ // P
QCH = 4
FT = D_FF // P
FCH = 3
FULL = NT // FCH
RING = 3
SLOTS = 4
AHEAD = RING - 1
ITEMS = 3 * FT
EPS = 1e-6
SCALE = HD ** -0.5
NEG = -1.0e30
BIG = 3.0e38
BLK = 512
NBLK = 5
HALF = 8
PAD = 2
QCOL = 3 * CW
KCOL = QCOL + FW
VCOL = KCOL + FW
FCOL = VCOL + FW
MCOL = FCOL
PW = NBLK * BLK


def group(**things):
    return namedtuple("group", list(things))(**things)


class Steps:

    def __init__(self):
        self.score = self.turned = self.page = self.scored = self.joined = self.bank = 0
        self.uses = []


@contextmanager
def stage(nc, names):
    with ExitStack() as ctx:
        sems = [ctx.enter_context(nc.semaphore(n)) for n in names.split()]
        with nc.Block() as block:
            yield block, group(**dict(zip(names.split(), sems)))
        numbers = sorted(s.num for s in sems)
        starts = [n for n in numbers if n - 1 not in numbers]
        for n0 in starts:
            n1 = n0
            while n1 in numbers:
                n1 += 1
            nc.sync.sem_clear(range(n0, n1))
        nc.all_engine_barrier()


SERIAL = [0]


def alloc(ctx, nc):
    def own_name(name):
        SERIAL[0] += 1
        return f"{name}_{SERIAL[0]}"

    def sb(name, shape, dt=F32):
        return ctx.enter_context(nc.sbuf_tensor(own_name(name), shape, dt))

    def ps(name, shape, dt=F32):
        return ctx.enter_context(nc.psum_tensor(own_name(name), shape, dt))

    return sb, ps


def setup_constants(nc, c, io):
    with ExitStack() as ctx:
        sb, _ = alloc(ctx, nc)
        causal = sb("causal", [P, P])
        with stage(nc, "filled ready loaded") as (block, s):

            @block.gpsimd
            def _(pool):
                pool.memset(c.ident[:], 0.0).then_inc(s.filled, 1)
                pool.memset(causal[:], 0.0).then_inc(s.filled, 1)
                pool.memset(c.page_before[:], 1.0).then_inc(s.filled, 1)
                pool.memset(c.own_head[:], 1.0).then_inc(s.filled, 1)
                pool.memset(c.seq_of_page[:], 0.0).then_inc(s.filled, 1)
                pool.memset(c.ones[:], 1.0).then_inc(s.filled, 1)
                pool.memset(c.minus_half[:], -0.5).then_inc(s.filled, 1)
                pool.wait_ge(s.filled, 7)
                pool.affine_select(out=c.ident[:], in_=c.ident[:], compare_op=ALU.not_equal, fill=1.0, base=0,
                                   pattern=[[-1, P]], channel_multiplier=1).then_inc(s.ready, 1)
                pool.affine_select(out=causal[:], in_=causal[:], compare_op=ALU.is_ge, fill=NEG, base=0,
                                   pattern=[[-1, P]], channel_multiplier=1).then_inc(s.ready, 1)
                pool.affine_select(out=c.page_before[:], in_=c.page_before[:], compare_op=ALU.is_gt, fill=0.0,
                                   base=0, pattern=[[1, P]], channel_multiplier=-1).then_inc(s.ready, 1)
                pool.affine_select(out=c.own_head[:], in_=c.own_head[:], compare_op=ALU.is_ge, fill=0.0, base=0,
                                   pattern=[[1, FW]], channel_multiplier=-HD).then_inc(s.ready, 1)
                pool.wait_ge(s.ready, 4)
                pool.affine_select(out=c.own_head[:], in_=c.own_head[:], compare_op=ALU.is_ge, fill=0.0,
                                   base=HD - 1, pattern=[[-1, FW]], channel_multiplier=HD).then_inc(s.ready, 1)

            @block.vector
            def _(dve):
                dve.wait_ge(s.ready, 4)
                dve.tensor_copy(c.ident_r[:], c.ident[:])
                dve.tensor_copy(c.causal_r[:], causal[:])
                dve.tensor_copy(c.fold[0:HD, :], c.ident[0:HD, 0:HD])
                dve.tensor_copy(c.fold[HD:P, :], c.ident[HD:P, HD:P])
                for k in range(P // PAGES):
                    rows = slice(k * PAGES, (k + 1) * PAGES)
                    if k < P // PAGES - 1:
                        dve.memset(c.page_before[rows, (k + 1) * PAGES:], 0.0)
                    for g in range(2):
                        j = g * (P // PAGES) + k
                        dve.memset(c.seq_of_page[rows, g, j:j + 1], 1.0)

            @block.sync
            def _(sp):
                sp.dma_start(c.b_f[0:FH, :], io.b_f.rearrange("l h -> h l")).then_inc(s.loaded, 16)
                sp.dma_start(c.pages[0:1, :], io.page_table.rearrange("b n -> (b n)").unsqueeze(0)).then_inc(s.loaded, 16)
                for g in range(2):
                    half = io.page_table[4 * g:4 * g + 4, :].rearrange("b n -> (b n)").unsqueeze(1)
                    sp.dma_start(c.page_index[:, g:g + 1], half.bitcast(U32)).then_inc(s.loaded, 16)
                sp.wait_ge(s.loaded, 64)


def split_weights(nc, parts):
    with stage(nc, "loaded0 loaded1 loaded2 loaded3 hi_done") as (block, s):
        loaded = (s.loaded0, s.loaded1, s.loaded2, s.loaded3)

        @block.sync
        def _(sp):
            for j, (_, _, _, src) in enumerate(parts):
                for dst, part in src:
                    sp.dma_start(dst, part).then_inc(loaded[j], 16)

        @block.scalar
        def _(act):
            for j, (raw, hi, _, src) in enumerate(parts):
                act.wait_ge(loaded[j], 16 * len(src))
                act.activation(hi, raw, ACT.Copy).then_inc(s.hi_done, 1)

        @block.vector
        def _(dve):
            for j, (raw, hi, lo, _) in enumerate(parts):
                dve.wait_ge(s.hi_done, j + 1)
                dve.tensor_tensor(lo, raw, hi.bitcast(F32), ALU.subtract)


def weight_parts(raw, hi, lo, src):
    rows = [slice(d, d + 2) for d in range(0, DT, 2)]
    return [(raw[:, r], hi[:, r], lo[:, r], [(raw[:, r], src[:, r])]) for r in rows]


def norm_transpose(nc, c, n, src, gain, hi, lo, rows=P, keep=None, gates=None):
    with ExitStack() as ctx:
        sb, psum = alloc(ctx, nc)
        x = keep if keep is not None else sb("x_in", [P, 3, D])
        slots = n if keep is not None else 3
        xn = sb("x_normed", [P, 3, D])
        ss = sb("sum_squares", [P, n])
        rstd = sb("rstd", [P, n])
        ps_t = psum("ps_transposed", [P, 2, D])
        ps_f = psum("ps_gates", [P, BLK])
        logits = sb("gate_logits", [P, n * P]) if gates else None
        with stage(nc, "zeroed load0 load1 load2 squared var rstd normed turned hi_done lo_done gate gate_out gates_stored") as (block, s):
            loads = (s.load0, s.load1, s.load2)
            gate_chunks = [(t0, min(BLK, n * P - t0)) for t0 in range(0, n * P, BLK)]

            @block.sync
            def _(sp):
                if rows < P:
                    sp.wait_ge(s.zeroed, 1)
                for k in range(n):
                    if k >= 3:
                        sp.wait_ge(s.normed, k - 2)
                    sp.dma_start(x[0:rows, k % slots, :], src(k)).then_inc(loads[k % 3], 16)
                if gates:
                    sp.wait_ge(s.gate_out, len(gate_chunks))
                    sp.dma_start(gates[2], logits[0:FH, :]).then_inc(s.gates_stored, 16)
                    sp.wait_ge(s.gates_stored, 16)

            @block.gpsimd
            def _(pool):
                if rows < P:
                    pool.memset(x[:, 0, :], 0.0).then_inc(s.zeroed, 1)
                for k in range(n):
                    pool.wait_ge(s.squared, k + 1)
                    pool.tensor_scalar(rstd[:, k:k + 1], ss[:, k:k + 1], 1.0 / D, EPS, ALU.mult, ALU.add).then_inc(s.var, 1)
                    pool.wait_ge(s.var, k + 1)
                    pool.tensor_tensor(rstd[:, k:k + 1], rstd[:, k:k + 1], c.minus_half[:], ALU.pow).then_inc(s.rstd, 1)

            @block.scalar
            def _(act):
                def square(k):
                    act.wait_ge(loads[k % 3], 16 * (k // 3 + 1))
                    if k >= 3:
                        act.wait_ge(s.turned, k - 2)
                    act.activation(xn[:, k % 3, :], x[:, k % slots, :], ACT.Square, accum_out=ss[:, k:k + 1]).then_inc(s.squared, 1)

                def gate_logits(j):
                    t0, w = gate_chunks[j]
                    act.wait_ge(s.gate, j + 1)
                    act.activation(logits[0:FH, t0:t0 + w], ps_f[0:FH, 0:w], ACT.Identity, bias=c.b_f[0:FH, :]).then_inc(s.gate_out, 1)

                for k in range(min(n, 2)):
                    square(k)
                for k in range(n):
                    if k + 2 < n:
                        square(k + 2)
                    act.wait_ge(s.turned, k + 1)
                    act.activation(hi[:, :, k * P:(k + 1) * P], ps_t[:, k % 2, :].rearrange("p (d t) -> p d t", d=DT),
                                   ACT.Copy).then_inc(s.hi_done, 1)
                    if gates and k == 6:
                        gate_logits(0)
                if gates:
                    gate_logits(len(gate_chunks) - 1)

            @block.vector
            def _(dve):
                def normalise(k):
                    dve.wait_ge(s.rstd, k + 1)
                    dve.scalar_tensor_tensor(out=xn[:, k % 3, :], in0=x[:, k % slots, :], scalar=rstd[:, k:k + 1],
                                             in1=gain, op0=ALU.mult, op1=ALU.mult).then_inc(s.normed, 1)

                normalise(0)
                for k in range(n):
                    if k + 1 < n:
                        normalise(k + 1)
                    dve.wait_ge(s.hi_done, k + 1)
                    dve.tensor_tensor(lo[:, :, k * P:(k + 1) * P], ps_t[:, k % 2, :].rearrange("p (d t) -> p d t", d=DT),
                                      hi[:, :, k * P:(k + 1) * P].bitcast(F32), ALU.subtract).then_inc(s.lo_done, 1)

            @block.tensor
            def _(pe):
                def gate_products(j):
                    t0, w = gate_chunks[j]
                    pe.wait_ge(s.lo_done, (t0 + w) // P)
                    if j >= 1:
                        pe.wait_ge(s.gate_out, j)
                    for d in range(DT):
                        for m, (a, b) in enumerate(((gates[0], hi), (gates[0], lo), (gates[1], hi))):
                            mm = pe.matmul(ps_f[:, 0:w], a[:, d, :], b[:, d, t0:t0 + w],
                                           start=(d == 0 and m == 0), stop=(d == DT - 1 and m == 2))
                    mm.then_inc(s.gate, 1)

                for k in range(n):
                    pe.wait_ge(s.normed, k + 1)
                    if k >= 2:
                        pe.wait_ge(s.lo_done, k - 1)
                    for d in range(DT):
                        turned = pe.transpose(ps_t[:, k % 2, d * P:(d + 1) * P], xn[:, k % 3, d * P:(d + 1) * P], c.ident[:])
                    turned.then_inc(s.turned, 1)
                    if gates and k == 5:
                        gate_products(0)
                if gates:
                    gate_products(len(gate_chunks) - 1)


def project(nc, c, n, h_hi, h_lo, w, buf, dst, following, rows=P, keys=None):
    nxt = 1 - buf
    groups = PAGES // 4
    pairs = DT // 2
    bufs = 3
    with ExitStack() as ctx:
        sb, psum = alloc(ctx, nc)
        out = sb("proj_out", [P, 2, BLK])
        ps_p = psum("ps_proj", [P, 4, BLK])
        if keys:
            page_k = sb("page_k", [P, bufs, 4, FW])
            q_row = sb("q_row", [P, FW])
        with stage(nc, "w_in0 w_in1 w_in2 w_in3 w_hi made evacuated store0 store1 q_in keys0 keys1 keys2 prod_done keys_done") as (block, s):
            w_in = (s.w_in0, s.w_in1, s.w_in2, s.w_in3)
            stores = (s.store0, s.store1)
            keys_in = (s.keys0, s.keys1, s.keys2)

            @block.sync
            def _(sp):
                def load_keys(g):
                    if g >= bufs:
                        sp.wait_ge(s.keys_done, g - bufs + 1)
                    for j in range(4):
                        page = sp.value_load(c.pages[0:1, ds(keys.seq * PAGES + 4 * g + j, 1)], min_val=0, max_val=keys.last_page)
                        sp.dma_start(page_k[:, g % bufs, j, :], keys.cache[ds(page, 1)].rearrange("n r c -> (n r) c")).then_inc(keys_in[g % bufs], 16)

                if keys:
                    sp.dma_start(q_row[:], keys.query).then_inc(s.q_in, 16)
                    load_keys(0)
                    load_keys(1)
                    load_keys(2)
                for j in range(pairs):
                    for to, part in following(j):
                        sp.dma_start(to, part).then_inc(w_in[j], 16)
                if keys:
                    for g in range(3, groups):
                        load_keys(g)
                for k in range(min(n, 2)):
                    sp.wait_ge(stores[k], 16 * ((n - k + 1) // 2))

            @block.tensor
            def _(pe):
                for t in range(n):
                    if t >= 4:
                        pe.wait_ge(s.evacuated, t - 3)
                    for d in range(DT):
                        a_hi, a_lo = h_hi[:, d, t * P:(t + 1) * P], h_lo[:, d, t * P:(t + 1) * P]
                        b_hi, b_lo = w.hi[:, buf, d, :], w.lo[:, buf, d, :]
                        pe.matmul(ps_p[:, t % 4, :], a_hi, b_hi, start=(d == 0), stop=False)
                        pe.matmul(ps_p[:, t % 4, :], a_hi, b_lo, start=False, stop=False)
                        mm = pe.matmul(ps_p[:, t % 4, :], a_lo, b_hi, start=False, stop=(d == DT - 1))
                    mm.then_inc(s.made, 1)

            @block.scalar
            def _(act):
                def evacuate(t):
                    act.wait_ge(s.made, t + 1)
                    if t >= 2:
                        act.wait_ge(stores[t % 2], 16 * (t // 2))
                    act.activation(out[:, t % 2, :], ps_p[:, t % 4, :], ACT.Copy).then_inc(s.evacuated, 1)
                    act.wait_ge(s.evacuated, t + 1)
                    act.dma_start(dst(t), out[0:rows, t % 2, :]).then_inc(stores[t % 2], 16)

                def split_hi(j):
                    act.wait_ge(w_in[j], 16 * len(following(j)))
                    act.activation(w.hi[:, nxt, 2 * j:2 * j + 2, :], w.raw[:, 2 * j:2 * j + 2, :], ACT.Copy).then_inc(s.w_hi, 1)

                todo = list(range(pairs))
                if n <= 2:
                    while todo:
                        split_hi(todo.pop(0))
                for t in range(n):
                    evacuate(t)
                    if t >= 1 and todo:
                        split_hi(todo.pop(0))

            def split_lo(eng, j):
                eng.wait_ge(s.w_hi, j + 1)
                eng.tensor_tensor(w.lo[:, nxt, 2 * j:2 * j + 2, :], w.raw[:, 2 * j:2 * j + 2, :],
                                  w.hi[:, nxt, 2 * j:2 * j + 2, :].bitcast(F32), ALU.subtract)

            @block.gpsimd
            def _(pool):
                if keys:
                    for j in range(pairs):
                        split_lo(pool, j)

            @block.vector
            def _(dve):
                if keys:
                    dve.wait_ge(s.q_in, 16)
                    for g in range(groups):
                        part = page_k[:, g % bufs, :, :]
                        dve.wait_ge(keys_in[g % bufs], 64 * (g // bufs + 1))
                        dve.tensor_tensor(part, part, q_row[:].unsqueeze(1).to_broadcast([P, 4, FW]), ALU.mult).then_inc(s.prod_done, 1)
                        dve.wait_ge(s.prod_done, g + 1)
                        dve.tensor_reduce(keys.scores[:, ds(keys.seq * (PAGES * FH) + g * 4 * FH, 4 * FH)],
                                          part.rearrange("p a (h d) -> p (a h) d", d=HD), AX.X, ALU.add).then_inc(s.keys_done, 1)
                else:
                    for j in range(pairs):
                        split_lo(dve, j)


def forget_gates(nc, c, gates, io, scratch, dec):
    T = SEQ + P
    with ExitStack() as ctx:
        sb, psum = alloc(ctx, nc)
        low = sb("low", [P, T])
        soft = sb("soft", [P, T])
        lf = sb("logf", [P, T])
        ones = sb("ones_row", [P, SEQ])
        out = sb("logf_out", [P, NT, FH])
        ps = psum("ps_logf", [P, NT + 1, FH])
        with stage(nc, "low size exp ln lf cum turned out stored") as (block, s):

            @block.vector
            def _(dve):
                dve.memset(ones[0:FH, :], 1.0)
                dve.tensor_scalar(low[0:FH, :], gates[0:FH, :], 0.0, None, ALU.min).then_inc(s.low, 1)
                dve.wait_ge(s.ln, 1)
                dve.wait_ge(s.low, 1)
                dve.tensor_tensor(lf[0:FH, :], low[0:FH, :], soft[0:FH, :], ALU.subtract).then_inc(s.lf, 1)
                dve.wait_ge(s.lf, 1)
                dve.tensor_tensor_scan(low[0:FH, 0:SEQ], ones[0:FH, :], lf[0:FH, 0:SEQ], 0.0, ALU.mult, ALU.subtract).then_inc(s.cum, 1)
                dve.wait_ge(s.turned, 1)
                dve.tensor_copy(out[:], ps[:, 0:NT, :])
                dve.tensor_copy(dec.logf_new[0:DB, :], ps[0:DB, NT, :]).then_inc(s.out, 1)

            @block.scalar
            def _(act):
                act.activation(soft[0:FH, :], gates[0:FH, :], ACT.Abs).then_inc(s.size, 1)
                act.wait_ge(s.size, 1)
                act.activation(soft[0:FH, :], soft[0:FH, :], ACT.Exp, scale=-1.0).then_inc(s.exp, 1)
                act.wait_ge(s.exp, 1)
                act.activation(soft[0:FH, :], soft[0:FH, :], ACT.Ln, bias=1.0).then_inc(s.ln, 1)

            @block.tensor
            def _(pe):
                pe.wait_ge(s.lf, 1)
                for t in range(NT + 1):
                    turned = pe.transpose(ps[:, t, :], lf[0:FH, t * P:(t + 1) * P], c.ident[0:FH, 0:FH])
                turned.then_inc(s.turned, 1)

            @block.sync
            def _(sp):
                sp.wait_ge(s.cum, 1)
                sp.dma_start(scratch.neg_cum, low[0:FH, 0:SEQ]).then_inc(s.stored, 16)
                sp.wait_ge(s.out, 1)
                sp.dma_start(io.new_logf.rearrange("(t p) h -> p t h", p=P), out[:]).then_inc(s.stored, 16)
                sp.dma_start(io.new_logf_s, dec.logf_new[0:DB, :]).then_inc(s.stored, 16)
                sp.wait_ge(s.stored, 48)


def decode_softmax(nc, c, io, scratch, dec):
    G = 2
    NS = DB * FH
    NM = DB * MH
    with ExitStack() as ctx:
        sb, psum = alloc(ctx, nc)
        lfp = sb("page_logf", [P, G, P, FH])
        cum = sb("page_cum", [P, G, P, FH])
        ones = sb("ones_page", [P, P])
        cum_r = sb("row_cum", [P, DB, PAGES, FH])
        rows = sb("new_rows", [P, PW])
        small = sb("small", [P, 8, FH])
        wide = sb("wide", [P, DB, FH])
        mem_k = sb("mem_k", [P, DB, 2, MW])
        mem_q = sb("mem_q", [P, DB, MW])
        mx = sb("maxima", [P, NS + NM])
        top = sb("maxima_all", [P, NS + NM])
        sm = sb("sums", [P, NS + NM])
        total = sb("sums_all", [P, NS + NM])
        ps_t = psum("ps_cum", [P, 4, 4, P])
        ps_o = psum("ps_offset", [P, G, FH])
        ps_c = psum("ps_total", [P, FH])
        names = "loaded chain scanned offsets totals summed_cum turned row_major maxed all_max shifted weighed summed all_sum"
        with stage(nc, names) as (block, s):

            @block.gpsimd
            def _(pool):
                table = io.cache_logf.rearrange("l n r h -> (l n) (r h)")
                for g in range(G):
                    pool.indirect_dma_start(lfp[:, g, :, :].rearrange("p r h -> p (r h)"), None, table,
                                            bass.IndirectOffsetOnAxis(ap=c.page_index[:, g:g + 1], axis=0)).then_inc(c.gathered, 16)
                pool.wait_ge(s.maxed, 1)
                pool.partition_all_reduce(top[:], mx[:], P, RMAX).then_inc(s.all_max, 1)
                pool.wait_ge(s.summed, 1)
                pool.partition_all_reduce(total[:], sm[:], P, RADD).then_inc(s.all_sum, 1)

            @block.sync
            def _(sp):
                sp.dma_start(rows[0:DB, :], scratch.samp).then_inc(s.loaded, 16)
                sp.dma_start(mem_k[:], io.cache_mem_k.rearrange("l b (t p) h d -> p (l b) t (h d)", p=P)).then_inc(s.loaded, 16)
                for b in range(DB):
                    sp.dma_start(mem_q[:, b, :], scratch.samp[b:b + 1, MCOL:MCOL + MW].to_broadcast([P, MW])).then_inc(s.loaded, 16)

            @block.vector
            def _(dve):
                chain = [0]

                def link(ins):
                    chain[0] += 1
                    ins.then_inc(s.chain, 1)
                    dve.wait_ge(s.chain, chain[0])

                past = dec.scores[:].rearrange("p (b n h) -> p b n h", b=DB, n=PAGES)
                past_h = dec.scores[:].rearrange("p (b n h) -> p b h n", b=DB, n=PAGES)
                mem = dec.mem_scores[:].rearrange("p (b t h) -> p b t h", b=DB, t=2)
                mx_mem = mx[:, NS:].rearrange("p (b h) -> p b h", b=DB)
                own = c.ident[0:DB, 0:DB].unsqueeze(2).to_broadcast([DB, DB, FH])
                own_m = c.ident[0:DB, 0:DB].unsqueeze(2).to_broadcast([DB, DB, MH])

                def on_own(source, mask, heads, out):
                    link(dve.tensor_tensor(wide[0:DB, :, 0:heads], source.rearrange("p (b h) -> p b h", b=DB), mask, ALU.mult))
                    link(dve.tensor_reduce(out, wide[0:DB, :, 0:heads].rearrange("p b h -> p h b"), AX.X, ALU.add))

                link(dve.memset(ones[:], 1.0))
                dve.wait_ge(c.gathered, 16 * G)
                for g in range(G):
                    for h in range(FH):
                        scan = dve.tensor_tensor_scan(cum[:, g, :, h], ones[:], lfp[:, g, :, h], 0.0, ALU.mult, ALU.add)
                scan.then_inc(s.scanned, 1)
                dve.wait_ge(s.scanned, 1)
                dve.wait_ge(s.offsets, 1)
                dve.wait_ge(s.totals, 1)
                for g in range(G):
                    added = dve.tensor_tensor(cum[:, g], cum[:, g], ps_o[:, g, :].unsqueeze(1).to_broadcast([P, P, FH]), ALU.add)
                added.then_inc(s.summed_cum, 1)
                dve.wait_ge(s.loaded, 16 * (2 + DB))
                for b in range(DB):
                    last = dve.tensor_tensor(mem_k[:, b], mem_k[:, b], mem_q[:, b, :].unsqueeze(1).to_broadcast([P, 2, MW]), ALU.mult)
                link(last)
                link(dve.tensor_reduce(dec.mem_scores[:], mem_k[:].rearrange("p b t (h d) -> p (b t h) d", d=HD), AX.X, ALU.add))
                link(dve.tensor_scalar(dec.mem_scores[:], dec.mem_scores[:], SCALE, None, ALU.mult))
                dve.tensor_tensor(mx_mem, mem[:, :, 0, :], mem[:, :, 1, :], ALU.max)
                link(dve.tensor_tensor(rows[0:DB, QCOL:QCOL + FW], rows[0:DB, QCOL:QCOL + FW], rows[0:DB, KCOL:KCOL + FW], ALU.mult))
                dve.tensor_tensor(small[0:DB, 1, :], dec.logf_new[0:DB, :], ps_c[0:DB, :], ALU.add)
                link(dve.tensor_reduce(small[0:DB, 0, :], rows[0:DB, QCOL:QCOL + FW].rearrange("p (h d) -> p h d", d=HD), AX.X, ALU.add))
                dve.tensor_scalar(wide[0:DB], own, 1.0, -NEG, ALU.subtract, ALU.mult)
                link(dve.scalar_tensor_tensor(out=small[0:DB, 2, :], in0=small[0:DB, 0, :], scalar=SCALE, in1=small[0:DB, 1, :],
                                              op0=ALU.mult, op1=ALU.subtract))
                link(dve.tensor_tensor(wide[0:DB], wide[0:DB], small[0:DB, 2, :].unsqueeze(1).to_broadcast([DB, DB, FH]), ALU.add))
                dve.wait_ge(s.row_major, 4)
                link(dve.scalar_tensor_tensor(out=dec.scores[:], in0=dec.scores[:], scalar=SCALE,
                                              in1=cum_r[:].rearrange("p b n h -> p (b n h)"), op0=ALU.mult, op1=ALU.subtract))
                link(dve.tensor_reduce(mx[:, 0:NS], past_h, AX.X, ALU.max))
                dve.tensor_tensor(mx[0:DB, 0:NS], mx[0:DB, 0:NS], wide[0:DB].rearrange("p b h -> p (b h)"), ALU.max).then_inc(s.maxed, 1)
                dve.wait_ge(s.all_max, 1)
                for b in range(DB):
                    dve.tensor_tensor(past[:, b], past[:, b], top[:, b * FH:(b + 1) * FH].unsqueeze(1).to_broadcast([P, PAGES, FH]), ALU.subtract)
                    dve.tensor_tensor(mem[:, b], mem[:, b], top[:, NS + b * MH:NS + (b + 1) * MH].unsqueeze(1).to_broadcast([P, 2, MH]), ALU.subtract)
                on_own(top[0:DB, 0:NS], own, FH, small[0:DB, 3, :])
                dve.tensor_tensor(small[0:DB, 4, :], small[0:DB, 2, :], small[0:DB, 3, :], ALU.subtract).then_inc(s.shifted, 1)
                dve.wait_ge(s.weighed, 3)
                dve.tensor_reduce(sm[:, 0:NS], past_h, AX.X, ALU.add)
                dve.tensor_tensor(sm[:, NS:].rearrange("p (b h) -> p b h", b=DB), mem[:, :, 0, :], mem[:, :, 1, :], ALU.add).then_inc(s.summed, 1)
                dve.wait_ge(s.all_sum, 1)
                on_own(total[0:DB, 0:NS], own, FH, small[0:DB, 6, :])
                link(dve.tensor_tensor(small[0:DB, 6, :], small[0:DB, 6, :], dec.w_new[0:DB, :], ALU.add))
                dve.reciprocal(dec.r_fox[0:DB, :], small[0:DB, 6, :])
                on_own(total[0:DB, NS:], own_m, MH, small[0:DB, 7, 0:MH])
                dve.reciprocal(dec.r_mem[0:DB, :], small[0:DB, 7, 0:MH])

            @block.tensor
            def _(pe):
                pe.wait_ge(s.scanned, 1)
                for g in range(G):
                    mm = pe.matmul(ps_o[:, g, :], c.page_before[:], cum[:, g, P - 1, :], start=True, stop=True)
                mm.then_inc(s.offsets, 1)
                for g in range(G):
                    mm = pe.matmul(ps_c[0:DB, :], c.seq_of_page[:, g, :], cum[:, g, P - 1, :], start=(g == 0), stop=(g == 1))
                mm.then_inc(s.totals, 1)
                pe.wait_ge(s.summed_cum, 1)
                for k in range(4):
                    for j in range(4):
                        turned = pe.transpose(ps_t[:, k, j, :], cum[:, k // 2, :, 4 * (k % 2) + j], c.ident[:])
                    turned.then_inc(s.turned, 1)

            @block.scalar
            def _(act):
                for k in range(4):
                    act.wait_ge(s.turned, k + 1)
                    b0, h0 = 4 * (k // 2), 4 * (k % 2)
                    act.activation(cum_r[:, b0:b0 + 4, :, h0:h0 + 4].rearrange("p b n h -> p (b n) h"),
                                   ps_t[:, k, :, :].rearrange("p h m -> p m h"), ACT.Copy).then_inc(s.row_major, 1)
                act.wait_ge(s.shifted, 1)
                act.activation(dec.scores[:], dec.scores[:], ACT.Exp).then_inc(s.weighed, 1)
                act.activation(dec.mem_scores[:], dec.mem_scores[:], ACT.Exp).then_inc(s.weighed, 1)
                act.activation(dec.w_new[0:DB, :], small[0:DB, 4, :], ACT.Exp).then_inc(s.weighed, 1)


def decode_memory_values(nc, c, io, dec, out):
    with ExitStack() as ctx:
        sb, psum = alloc(ctx, nc)
        mem_v = sb("mem_v", [P, DB, 2, MW])
        own = sb("own_rows", [P, DB, MW])
        pick = sb("pick", [P, DB, DB])
        ps_m = psum("ps_m", [P, DB, MW])
        ps_s = psum("ps_s", [P, MW])
        with stage(nc, "loaded picked zeroed made masked summed") as (block, s):

            @block.sync
            def _(sp):
                sp.dma_start(mem_v[:], io.cache_mem_v.rearrange("l b (t p) h d -> p (l b) t (h d)", p=P)).then_inc(s.loaded, 16)

            @block.gpsimd
            def _(pool):
                pool.memset(pick[0:MH], 0.0).then_inc(s.zeroed, 1)
                pool.wait_ge(s.zeroed, 1)
                for b in range(DB):
                    pool.memset(pick[0:MH, b, b:b + 1], 1.0).then_inc(s.picked, 1)

            @block.tensor
            def _(pe):
                pe.wait_ge(s.loaded, 16)
                for b in range(DB):
                    for t in range(2):
                        mm = pe.matmul(ps_m[0:MH, b, :], dec.mem_scores[:, (2 * b + t) * MH:(2 * b + t + 1) * MH], mem_v[:, b, t, :],
                                       start=(t == 0), stop=(t == 1))
                mm.then_inc(s.made, 1)
                pe.wait_ge(s.picked, DB)
                pe.wait_ge(s.masked, 1)
                for b in range(DB):
                    mm = pe.matmul(ps_s[0:DB, :], pick[0:MH, b, :], own[0:MH, b, :], start=(b == 0), stop=(b == DB - 1))
                mm.then_inc(s.summed, 1)

            @block.vector
            def _(dve):
                dve.wait_ge(s.made, 1)
                dve.tensor_tensor(own[0:MH], ps_m[0:MH], c.own_head[0:MH, 0:MW].unsqueeze(1).to_broadcast([MH, DB, MW]), ALU.mult).then_inc(s.masked, 1)
                dve.wait_ge(s.summed, 1)
                dve.tensor_tensor(out[0:DB, :].rearrange("p (h d) -> p h d", d=HD), ps_s[0:DB, :].rearrange("p (h d) -> p h d", d=HD),
                                  dec.r_mem[0:DB, :].unsqueeze(2).to_broadcast([DB, MH, HD]), ALU.mult)


def load_head(eng, a, head, nk, sem):
    eng.dma_start(a.q[:, :, 0, :], head.q.rearrange("(t p) d -> p t d", p=P)).then_inc(sem, 16)
    eng.dma_start(a.k[:, 0:nk, 0, :], head.k.rearrange("(t p) d -> p t d", p=P)).then_inc(sem, 16)
    eng.dma_start(a.v[:, 0:nk, :], head.v.rearrange("(t p) d -> p t d", p=P)).then_inc(sem, 16)


def load_decay(eng, a, head, sem):
    if head.neg_cum is not None:
        eng.dma_start(a.neg_cum[:], head.neg_cum.to_broadcast([P, SEQ])).then_inc(sem, 16)


def double_head(pool, a, nk):
    pool.tensor_copy(a.k[:, 0:nk, 1, :], a.k[:, 0:nk, 0, :])
    pool.tensor_copy(a.q[:, :, 1, :], a.q[:, :, 0, :])


def attention_order(nk, causal, pages):
    chunks = NT // QCH
    n_k = (nk + 3) // 4
    steps = [(ch, j) for ch in range(chunks) for j in range(QCH * (ch + 1) if causal else nk)]
    ins = [("in", what, j) for j in range(NT // 4) for what in "kq" if what == "q" or j < n_k]
    order, pending = [], []
    left = [pages]

    def score(i):
        w = (i + 1) * P if causal else nk * P
        return [("score", i, m, p0, min(w, p0 + 1024), p0 + 1024 >= w) for m, p0 in enumerate(range(0, w, 1024))]

    def past(count):
        for _ in range(min(count, left[0])):
            left[0] -= 1
            order.append(("page",))

    def slot(items, page=False, value=()):
        order.extend(items)
        past(1 if page else 0)
        order.extend(value)
        order.extend(("exp", i) for i in pending)
        pending[:] = [e[1] for e in items if e[0] == "score" and e[5]]

    rows = [score(i) for i in range(NT)]
    lead = QCH + 2 if causal else 2 * QCH
    slot([ins.pop(0)], page=True)
    slot([ins.pop(0)], page=True)
    for i in range(0, lead, 2):
        slot(rows[i] + ins[0:1], page=i < 4)
        ins = ins[1:]
        slot(rows[i + 1] + ([] if i else [("split_v",)]), page=i == 0)
    done = lead

    def turn(n):
        ch, j = steps[n]
        if j == 0:
            order.extend(("exp", i) for i in pending if i < QCH * (ch + 1))
            pending[:] = [i for i in pending if i >= QCH * (ch + 1)]
        return ("turn", n, ch, j)

    past(3)
    order.append(turn(0))
    folding = None
    for ch in range(chunks):
        own = [n for n, (c, _) in enumerate(steps) if c == ch]
        ahead = min(NT, QCH * (ch + (2 if causal else 3)))
        todo = [piece for row in rows[done:ahead] for piece in row]
        total, done = len(todo), max(done, ahead)
        span = (2, 5, 8, 1)[ch] if causal else len(own)
        for j, n in enumerate(own):
            items = []
            if n + 1 < len(steps):
                if n == own[-1]:
                    past(1)
                items.append(turn(n + 1))
            if ins:
                items.append(ins.pop(0))
            while todo and total - len(todo) < -(-total * (j + 1) // span):
                items.append(todo.pop(0))
            slot(items, page=ch == chunks - 1 or j >= len(own) - (2, 3, 4)[ch], value=[("value", n, ch, j)])
            if j == 0 and folding is not None:
                order.append(("fold", folding))
            if j == 1 and folding is not None:
                order.append(("store", folding))
            if ch == 1 and j == 0:
                order.append(("load_head",))
            if ch == chunks - 1 and j == 0:
                order.append(("load_decay",))
        order.append(("copy", ch))
        folding = ch
    if pages:
        order.append(("row",))
    order.extend([("fold", folding), ("store", folding)])
    return order


def attend(nc, c, a, nk, causal, following, dst, values=None):
    chunks = NT // QCH
    n_k = (nk + 3) // 4
    order = attention_order(nk, causal, PAGES if values else 0)

    def first_row(ch, j):
        return max(0, j - QCH * ch) if causal else 0

    def last_key(ch):
        return (QCH * (ch + 1) if causal else nk) - 1

    def probs(ch, r, p0, p1):
        at = 0 if causal else (ch // 2) * nk * P
        return a.probs[:, ch % 2, r, at + p0:at + p1]

    def turned_in(i):
        return sum(min(i // 4 + 1, n) for n in (n_k, NT // 4))

    with ExitStack() as ctx:
        sb, psum = alloc(ctx, nc)
        ps_s = psum("ps_scores", [P, 2, 1024])
        ps_t = psum("ps_turned", [P, 2, BLK])
        ps_o = psum("ps_out", [P, BLK])
        if values:
            ps_v = psum("ps_values", [P, FW])
        names = ("turned hi lo v_hi v_lo scored min1 min2 probs t_turned t_hi t_split pv o_copied o_ready inverted o_out "
                 "stored loaded decay w_copied v0 v1 v2 v3 v_used v_masked v_row v_row_out")
        with stage(nc, names) as (block, s):
            v_in = (s.v0, s.v1, s.v2, s.v3)

            @block.sync
            def _(sp):
                if values:
                    for n in range(PAGES):
                        if n >= 4:
                            sp.wait_ge(s.v_used, n - 3)
                        page = sp.value_load(c.pages[0:1, ds(values.seq * PAGES + n, 1)], min_val=0, max_val=values.last_page)
                        sp.dma_start(values.page_v[:, n % 4, :], values.cache[ds(page, 1)].rearrange("n r c -> (n r) c")).then_inc(v_in[n % 4], 16)
                    sp.wait_ge(s.v_row_out, 1)
                    sp.dma_start(values.dst, values.row[0:1, :]).then_inc(s.stored, 16)
                sp.wait_ge(s.stored, 16 * (chunks + (1 if values else 0)))
                if following.neg_cum is not None:
                    sp.wait_ge(s.decay, 16)

            @block.gpsimd
            def _(pool):
                pool.wait_ge(s.loaded, 48)
                double_head(pool, a, nk)

            @block.tensor
            def _(pe):
                st = Steps()

                def take_bank():
                    if len(st.uses) >= 2:
                        pe.wait_ge(*st.uses[-2])
                    return ps_t[:, len(st.uses) % 2, :]

                for what, *at in order:
                    if what == "in":
                        side, j = at
                        bank = take_bank()
                        raw = a.k if side == "k" else a.q
                        for t in range(4 * j, min(4 * j + 4, nk if side == "k" else NT)):
                            turned = pe.transpose(bank[:, (t - 4 * j) * P:(t - 4 * j + 1) * P],
                                                  raw[:, t, :, :].rearrange("p a d -> p (a d)"), c.ident[:])
                        turned.then_inc(s.turned, 1)
                        st.turned += 1
                        st.uses.append((s.lo, st.turned))
                    elif what == "score":
                        i, m, p0, p1, _ = at
                        if m == 0:
                            pe.wait_ge(s.lo, turned_in(i))
                        if st.score >= 2:
                            pe.wait_ge(s.min1, st.score - 1)
                        bank = ps_s[:, st.score % 2, :]
                        for b0 in range(p0, p1, BLK):
                            b1 = min(b0 + BLK, p1)
                            out = bank[:, b0 - p0:b1 - p0]
                            diag = causal and b1 == (i + 1) * P
                            pe.matmul(out, a.q_hi[:, i * P:(i + 1) * P], a.k_st[:, b0:b1], start=True, stop=False)
                            mm = pe.matmul(out, a.q_lo[:, i * P:(i + 1) * P], a.k_st[:, b0:b1], start=False, stop=not diag)
                            if diag:
                                mm = pe.matmul(bank[:, b1 - P - p0:b1 - p0], c.ident_r[:], c.causal_r[:], start=False, stop=True)
                        mm.then_inc(s.scored, 1)
                        st.score += 1
                    elif what == "turn":
                        n, ch, j = at
                        if j == 0:
                            pe.wait_ge(s.probs, QCH * (ch + 1))
                        bank = take_bank()
                        for r in range(first_row(ch, j), QCH):
                            turned = pe.transpose(bank[:, r * P:(r + 1) * P], probs(ch, r, j * P, (j + 1) * P), c.ident[:])
                        turned.then_inc(s.t_turned, 1)
                        st.uses.append((s.t_split, n + 1))
                    elif what == "value":
                        n, ch, j = at
                        r0 = first_row(ch, j)
                        if n == 0:
                            pe.wait_ge(s.v_lo, 1)
                        if j == 0 and ch >= 1:
                            pe.wait_ge(s.o_copied, ch)
                        out = ps_o[:, r0 * P:]
                        pe.wait_ge(s.t_split, n + 1)
                        pe.matmul(out, a.v_st[:, j, :], a.p_hi[:, n % 2, r0 * P:], start=(j == 0), stop=False)
                        pe.matmul(out, a.v_st[:, j, :], a.p_lo[:, n % 2, r0 * P:], start=False, stop=(j == last_key(ch))).then_inc(s.pv, 1)
                    elif what == "fold":
                        ch, = at
                        pe.wait_ge(s.o_copied, ch + 1)
                        bank = take_bank()
                        for r in range(QCH):
                            mm = pe.matmul(bank[:, r * HD:(r + 1) * HD], a.o_t[:, ch % 2, r * P:(r + 1) * P], c.fold[:], start=True, stop=True)
                        mm.then_inc(s.o_ready, 1)
                        st.uses.append((s.o_out, ch + 1))
                    elif what == "page":
                        n = st.page
                        if n == 0:
                            pe.wait_ge(s.w_copied, 1)
                        pe.wait_ge(v_in[n % 4], 16 * (n // 4 + 1))
                        pe.matmul(ps_v[0:FH, :], values.weights[:, n * FH:(n + 1) * FH], values.page_v[:, n % 4, :],
                                  start=(n == 0), stop=(n == PAGES - 1)).then_inc(s.v_used, 1)
                        st.page += 1
                    elif what == "row":
                        bank = take_bank()
                        pe.wait_ge(s.v_masked, 1)
                        pe.matmul(bank[0:1, :], c.ones[0:FH, :], values.own[0:FH, :], start=True, stop=True).then_inc(s.v_row, 1)
                        st.uses.append((s.v_row_out, 1))

            @block.scalar
            def _(act):
                st = Steps()
                for what, *at in order:
                    if what == "in":
                        side, j = at
                        act.wait_ge(s.turned, st.turned + 1)
                        if side == "k":
                            w = min(BLK, nk * P - j * BLK)
                            act.activation(a.k_st[:, j * BLK:j * BLK + w], ps_t[:, st.bank % 2, 0:w], ACT.Copy).then_inc(s.hi, 1)
                        else:
                            act.activation(a.q_hi[:, j * BLK:(j + 1) * BLK], ps_t[:, st.bank % 2, :], ACT.Copy, scale=SCALE).then_inc(s.hi, 1)
                        st.turned += 1
                        st.bank += 1
                    elif what == "split_v":
                        act.activation(a.v_st[:, 0:nk, 0:HD], a.v[:, 0:nk, :], ACT.Copy).then_inc(s.v_hi, 1)
                    elif what == "exp":
                        i, = at
                        w = (i + 1) * P if causal else nk * P
                        n_pieces = -(-w // 1024)
                        st.scored += n_pieces
                        if n_pieces == 1:
                            act.wait_ge(s.min1, st.scored)
                        else:
                            st.joined += 1
                            act.wait_ge(s.min2, st.joined)
                        part = probs(i // QCH, i % QCH, 0, w)
                        act.activation(part, part, ACT.Exp, scale=-1.0, bias=a.low[:, i:i + 1], accum_out=a.sums[:, i:i + 1]).then_inc(s.probs, 1)
                    elif what == "turn":
                        n, ch, j = at
                        r0 = first_row(ch, j)
                        act.wait_ge(s.t_turned, n + 1)
                        if n >= 2:
                            act.wait_ge(s.pv, n - 1)
                        act.activation(a.p_hi[:, n % 2, r0 * P:], ps_t[:, st.bank % 2, r0 * P:], ACT.Copy).then_inc(s.t_hi, 1)
                        st.bank += 1
                    elif what == "copy":
                        ch, = at
                        act.wait_ge(s.pv, sum(last_key(k) + 1 for k in range(ch + 1)))
                        if ch >= 2:
                            act.wait_ge(s.o_ready, ch - 1)
                        act.activation(a.o_t[:, ch % 2, :], ps_o[:], ACT.Copy).then_inc(s.o_copied, 1)
                    elif what == "fold":
                        st.bank += 1
                    elif what == "store":
                        ch, = at
                        act.wait_ge(s.o_out, ch + 1)
                        act.dma_start(dst(ch), a.o_out[:, ch, :, :]).then_inc(s.stored, 16)
                    elif what == "load_head":
                        act.wait_ge(s.turned, n_k + NT // 4)
                        act.wait_ge(s.v_lo, 1)
                        load_head(act, a, following, nk, s.loaded)
                    elif what == "load_decay":
                        load_decay(act, a, following, s.decay)
                    elif what == "row":
                        act.wait_ge(s.v_row, 1)
                        act.activation(values.row[0:1, :], ps_t[0:1, st.bank % 2, :], ACT.Copy).then_inc(s.v_row_out, 1)
                        st.bank += 1

            @block.vector
            def _(dve):
                st = Steps()
                if values:
                    dve.tensor_copy(values.weights[:], values.all_weights).then_inc(s.w_copied, 1)
                for what, *at in order:
                    if what == "in":
                        side, j = at
                        dve.wait_ge(s.hi, st.turned + 1)
                        if side == "k":
                            w = min(BLK, nk * P - j * BLK)
                            upper = a.k_st[HD:P, j * BLK:j * BLK + w]
                            dve.tensor_tensor(upper, ps_t[HD:P, st.bank % 2, 0:w], upper.bitcast(F32), ALU.subtract).then_inc(s.lo, 1)
                        else:
                            cols = slice(j * BLK, (j + 1) * BLK)
                            dve.scalar_tensor_tensor(out=a.q_lo[:, cols], in0=ps_t[:, st.bank % 2, :], scalar=SCALE, in1=a.q_hi[:, cols].bitcast(F32),
                                                     op0=ALU.mult, op1=ALU.subtract).then_inc(s.lo, 1)
                        st.turned += 1
                        st.bank += 1
                    elif what == "split_v":
                        dve.wait_ge(s.v_hi, 1)
                        dve.tensor_tensor(a.v_st[:, 0:nk, HD:P], a.v[:, 0:nk, :], a.v_st[:, 0:nk, 0:HD].bitcast(F32), ALU.subtract).then_inc(s.v_lo, 1)
                    elif what == "score":
                        i, m, p0, p1, complete = at
                        ch, r = i // QCH, i % QCH
                        if causal and r == 0 and m == 0 and ch >= 2:
                            dve.wait_ge(s.t_turned, sum(last_key(k) + 1 for k in range(ch - 1)))
                        dve.wait_ge(s.scored, st.score + 1)
                        part = a.low[:, i:i + 1] if complete and m == 0 else a.low2[:, m, i:i + 1]
                        bias = a.neg_cum[:, p0:p1] if causal else a.zeros[:, 0:p1 - p0]
                        dve.tensor_tensor_reduce(probs(ch, r, p0, p1), ps_s[:, st.score % 2, 0:p1 - p0], bias, -1.0, BIG, ALU.add, ALU.min,
                                                 part).then_inc(s.min1, 1)
                        st.score += 1
                        if complete and m == 1:
                            dve.wait_ge(s.min1, st.score)
                            dve.tensor_tensor(a.low[:, i:i + 1], a.low2[:, 0, i:i + 1], a.low2[:, 1, i:i + 1], ALU.min).then_inc(s.min2, 1)
                    elif what == "turn":
                        n, ch, j = at
                        r0 = first_row(ch, j)
                        dve.wait_ge(s.t_hi, n + 1)
                        dve.tensor_tensor(a.p_lo[:, n % 2, r0 * P:], ps_t[:, st.bank % 2, r0 * P:], a.p_hi[:, n % 2, r0 * P:].bitcast(F32),
                                          ALU.subtract).then_inc(s.t_split, 1)
                        st.bank += 1
                    elif what == "fold":
                        ch, = at
                        part = slice(QCH * ch, QCH * ch + QCH)
                        dve.reciprocal(a.inv[:, part], a.sums[:, part]).then_inc(s.inverted, 1)
                        dve.wait_ge(s.inverted, ch + 1)
                        dve.wait_ge(s.o_ready, ch + 1)
                        dve.tensor_tensor(a.o_out[:, ch, :, :], ps_t[:, st.bank % 2, 0:QCH * HD].rearrange("p (r d) -> p r d", d=HD),
                                          a.inv[:, part].unsqueeze(2).to_broadcast([P, QCH, HD]), ALU.mult).then_inc(s.o_out, 1)
                        st.bank += 1
                    elif what == "row":
                        dve.wait_ge(s.v_used, PAGES)
                        dve.tensor_tensor(values.own[0:FH, :], ps_v[0:FH, :], c.own_head[0:FH, :], ALU.mult).then_inc(s.v_masked, 1)
                        st.bank += 1


def mix(nc, c, n, w, gain, assemble, x_src, dst, rows=P):
    with ExitStack() as ctx:
        sb, psum = alloc(ctx, nc)
        y = sb("y", [P, min(n, SLOTS), D])
        yn = sb("y_normed", [P, D])
        y_hi = sb("y_hi", [P, 2, DT, P], F32R)
        y_lo = sb("y_lo", [P, 2, DT, P], F32R)
        x = sb("x_res", [P, min(n, SLOTS), D])
        junk = sb("squares", [P, D])
        ss = sb("sum_squares", [P, n, 3])
        rstd = sb("rstd", [P, n, 3])
        ps_t = psum("ps_transposed", [P, 2, BLK])
        ps_y = psum("ps_y", [P, 2, D])
        groups = [(0, CW), (CW, FW), (CW + FW, MW)]
        with stage(nc, "fox0 fox1 fox2 fox3 parts0 parts1 parts2 parts3 xin0 xin1 xin2 xin3 conv conv_step squared var rstd normed turned hi_done lo_done made res store0 store1 store2 store3") as (block, s):
            parts = (s.parts0, s.parts1, s.parts2, s.parts3)
            fox = (s.fox0, s.fox1, s.fox2, s.fox3)
            xin = (s.xin0, s.xin1, s.xin2, s.xin3)
            stores = (s.store0, s.store1, s.store2, s.store3)

            @block.sync
            def _(sp):
                for k in range(n + SLOTS - 1):
                    if k < n:
                        assemble.load(sp, s, k, y, parts[k % SLOTS], fox[k % SLOTS])
                        if k >= SLOTS:
                            sp.wait_ge(stores[k % SLOTS], 16 * (k // SLOTS))
                        sp.dma_start(x[0:rows, k % SLOTS, :], x_src(k)).then_inc(xin[k % SLOTS], 16)
                    done = k - (SLOTS - 1)
                    if done >= 0:
                        sp.wait_ge(s.res, done + 1)
                        sp.dma_start(dst(done), x[0:rows, done % SLOTS, :]).then_inc(stores[done % SLOTS], 16)
                for k in range(min(n, SLOTS)):
                    sp.wait_ge(stores[k], 16 * ((n - k + SLOTS - 1) // SLOTS))

            @block.gpsimd
            def _(pool):
                for k in range(n):
                    assemble.conv(pool, s, k, y, parts[k % SLOTS])
                    pool.wait_ge(s.squared, k + 1)
                    for m, (g0, gw) in enumerate(groups):
                        scaled = pool.tensor_scalar(rstd[:, k, m:m + 1], ss[:, k, m:m + 1], 1.0 / gw, EPS, ALU.mult, ALU.add)
                    scaled.then_inc(s.var, 1)
                    pool.wait_ge(s.var, k + 1)
                    pool.tensor_tensor(rstd[:, k, :], rstd[:, k, :], c.minus_half[:].to_broadcast([P, 3]), ALU.pow).then_inc(s.rstd, 1)

            @block.scalar
            def _(act):
                def square(k):
                    act.wait_ge(s.conv, k + 1)
                    assemble.ready(act, s, k, fox[k % SLOTS])
                    if k >= 1:
                        act.wait_ge(s.squared, k)
                    for m, (g0, gw) in enumerate(groups):
                        done = act.activation(junk[:, g0:g0 + gw], y[:, k % SLOTS, g0:g0 + gw], ACT.Square, accum_out=ss[:, k, m:m + 1])
                    done.then_inc(s.squared, 1)

                square(0)
                for k in range(n):
                    for j in range(2):
                        u = 2 * k + j
                        act.wait_ge(s.turned, u + 1)
                        if k >= 2:
                            act.wait_ge(s.made, k - 1)
                        act.activation(y_hi[:, k % 2, 4 * j:4 * j + 4, :], ps_t[:, j, :].rearrange("p (d t) -> p d t", d=4), ACT.Copy).then_inc(s.hi_done, 1)
                    if k + 1 < n:
                        square(k + 1)

            @block.vector
            def _(dve):
                def normalise(k):
                    dve.wait_ge(s.rstd, k + 1)
                    if k >= 1:
                        dve.wait_ge(s.turned, 2 * k)
                    for m, (g0, gw) in enumerate(groups):
                        done = dve.scalar_tensor_tensor(out=yn[:, g0:g0 + gw], in0=y[:, k % SLOTS, g0:g0 + gw], scalar=rstd[:, k, m:m + 1],
                                                        in1=gain[:, g0:g0 + gw], op0=ALU.mult, op1=ALU.mult)
                    done.then_inc(s.normed, 1)

                def split(k):
                    for j in range(2):
                        u = 2 * k + j
                        dve.wait_ge(s.hi_done, u + 1)
                        dve.tensor_tensor(y_lo[:, k % 2, 4 * j:4 * j + 4, :], ps_t[:, j, :].rearrange("p (d t) -> p d t", d=4),
                                          y_hi[:, k % 2, 4 * j:4 * j + 4, :].bitcast(F32), ALU.subtract).then_inc(s.lo_done, 1)

                def residual(k):
                    dve.wait_ge(s.made, k + 1)
                    dve.wait_ge(xin[k % SLOTS], 16 * (k // SLOTS + 1))
                    dve.tensor_tensor(x[0:rows, k % SLOTS, :], ps_y[0:rows, k % 2, :], x[0:rows, k % SLOTS, :], ALU.add).then_inc(s.res, 1)

                normalise(0)
                for k in range(n):
                    split(k)
                    if k + 1 < n:
                        normalise(k + 1)
                    if k >= 1:
                        residual(k - 1)
                residual(n - 1)

            @block.tensor
            def _(pe):
                def turn(k):
                    pe.wait_ge(s.normed, k + 1)
                    for j in range(2):
                        if k >= 1:
                            pe.wait_ge(s.lo_done, 2 * k - 1 + j)
                        for d in range(4):
                            turned = pe.transpose(ps_t[:, j, d * P:(d + 1) * P], yn[:, (4 * j + d) * P:(4 * j + d + 1) * P], c.ident[:])
                        turned.then_inc(s.turned, 1)

                turn(0)
                for k in range(n):
                    pe.wait_ge(s.lo_done, 2 * k + 2)
                    if k >= 2:
                        pe.wait_ge(s.res, k - 1)
                    for e in range(2):
                        if e == 1 and k + 1 < n:
                            turn(k + 1)
                        for d in range(DT):
                            out = ps_y[:, k % 2, e * BLK:(e + 1) * BLK]
                            cols = slice(e * BLK, (e + 1) * BLK)
                            pe.matmul(out, y_hi[:, k % 2, d, :], w.hi[:, d, cols], start=(d == 0), stop=False)
                            pe.matmul(out, y_hi[:, k % 2, d, :], w.lo[:, d, cols], start=False, stop=False)
                            mm = pe.matmul(out, y_lo[:, k % 2, d, :], w.hi[:, d, cols], start=False, stop=(d == DT - 1))
                    mm.then_inc(s.made, 1)


def weight_source(io, i):
    if i >= 2 * FT:
        return io.w_down[(i - 2 * FT) * P:(i - 2 * FT + 1) * P, :]
    table = io.w_up if i % 2 else io.w_gate
    return table.rearrange("(d p) n -> p d n", p=P)[:, :, (i // 2) * P:(i // 2 + 1) * P]


def weight_slot(w, i):
    slot = w.raw[:, i % RING, :]
    return slot if i >= 2 * FT else slot.rearrange("p (d n) -> p d n", d=DT)


def ffn(nc, c, n, b, w, ps, io, before=None, following=None):
    T = n * P
    splits = ITEMS if following else ITEMS - AHEAD
    def squared_at(k):
        return 3 + 5 * k

    def turned_at(k, j):
        return squared_at(k) + 2 + j

    names = ("w_in0 w_in1 w_in2 w_hi w_lo w_used silu_done prod_done a_hi a_lo res squared var rstd normed stored "
             "n_loaded0 n_loaded1 n_loaded2 n_squared n_var n_rstd n_normed n_turned n_hi n_lo")
    with stage(nc, names) as (block, s):
        w_in = (s.w_in0, s.w_in1, s.w_in2)
        n_loaded = (s.n_loaded0, s.n_loaded1, s.n_loaded2)

        @block.sync
        def _(sp):
            for k in range(splits):
                i = (k + AHEAD) % ITEMS
                if before and k == 12:
                    for t in range(before.n):
                        sp.wait_ge(s.normed, t + 1)
                        sp.dma_start(before.dst(t), before.x[:, t, :]).then_inc(s.stored, 16)
                if following and k == 2 * FT:
                    if before:
                        sp.wait_ge(s.stored, 16 * before.n)
                    for t in range(following.n):
                        sp.dma_start(following.x[0:following.rows(t), t, :], following.src(t)).then_inc(n_loaded[t], 16)
                if k >= RING:
                    sp.wait_ge(s.w_lo, k - RING + 1)
                sp.dma_start(weight_slot(w, i), weight_source(io, i)).then_inc(w_in[(k + AHEAD) % RING], 16)
            if before and not following:
                sp.wait_ge(s.stored, 16 * before.n)

        @block.gpsimd
        def _(pool):
            if before:
                for k in range(before.n):
                    pool.wait_ge(s.squared, k + 1)
                    pool.tensor_scalar(b.rstd[:, k:k + 1], b.ss[:, k:k + 1], 1.0 / D, EPS, ALU.mult, ALU.add).then_inc(s.var, 1)
                    pool.wait_ge(s.var, k + 1)
                    pool.tensor_tensor(b.rstd[:, k:k + 1], b.rstd[:, k:k + 1], c.minus_half[:], ALU.pow).then_inc(s.rstd, 1)
            if following:
                for k in range(following.n):
                    pool.wait_ge(s.n_squared, k + 1)
                    pool.tensor_scalar(b.n_rstd[:, k:k + 1], b.n_ss[:, k:k + 1], 1.0 / D, EPS, ALU.mult, ALU.add).then_inc(s.n_var, 1)
                    pool.wait_ge(s.n_var, k + 1)
                    pool.tensor_tensor(b.n_rstd[:, k:k + 1], b.n_rstd[:, k:k + 1], c.minus_half[:], ALU.pow).then_inc(s.n_rstd, 1)

        @block.scalar
        def _(act):
            def split_hi(k):
                if k >= splits:
                    return
                i = k + AHEAD
                act.wait_ge(w_in[i % RING], 16 * (k // RING + 1))
                if i >= RING:
                    act.wait_ge(s.w_used, i - RING + 1)
                act.activation(w.hi[:, i % RING, :], w.raw[:, i % RING, :], ACT.Copy).then_inc(s.w_hi, 1)

            for f in range(FT):
                split_hi(2 * f)
                act.wait_ge(s.w_used, 2 * f + 1)
                if f >= 2:
                    act.wait_ge(s.prod_done, f - 1)
                act.activation(b.sil[:, f % 2, 0:T], ps[:, gate_bank(f), 0:T], ACT.Silu).then_inc(s.silu_done, 1)
                split_hi(2 * f + 1)
                act.wait_ge(s.prod_done, f + 1)
                act.activation(b.act_hi[:, f, 0:T], b.prod[:, 0:T], ACT.Copy).then_inc(s.a_hi, 1)
                if before and 1 <= f <= before.n:
                    act.wait_ge(s.res, before.n)
                    if f > 1:
                        act.wait_ge(s.squared, f - 1)
                    act.activation(b.xn[:, 0, :], before.x[:, f - 1, :], ACT.Square, accum_out=b.ss[:, f - 1:f]).then_inc(s.squared, 1)
            for f in range(FT):
                split_hi(2 * FT + f)
                if following:
                    for k in range(following.n):
                        if f == squared_at(k):
                            act.wait_ge(n_loaded[k], 16)
                            if k >= 2:
                                act.wait_ge(s.n_turned, 2 * (k - 1))
                            act.activation(b.xn[:, k % 2, :], following.x[:, k, :], ACT.Square, accum_out=b.n_ss[:, k:k + 1]).then_inc(s.n_squared, 1)
                        for j in range(2):
                            if f == turned_at(k, j):
                                act.wait_ge(s.n_turned, 2 * k + j + 1)
                                act.activation(b.h_hi[:, 4 * j:4 * j + 4, k * P:(k + 1) * P], ps[:, 6 + j, :].rearrange("p (d t) -> p d t", d=4),
                                               ACT.Copy).then_inc(s.n_hi, 1)

        @block.vector
        def _(dve):
            def split_lo(k):
                if k >= splits:
                    return
                i = k + AHEAD
                dve.wait_ge(s.w_hi, k + 1)
                dve.tensor_tensor(w.lo[:, i % RING, :], w.raw[:, i % RING, :], w.hi[:, i % RING, :].bitcast(F32), ALU.subtract).then_inc(s.w_lo, 1)

            if before:
                for k in (2, 0, 1):
                    dve.tensor_tensor(before.x[:, k, :], ps[:, 2 * k:2 * k + 2, :].rearrange("p a n -> p (a n)"), before.x[:, k, :],
                                      ALU.add).then_inc(s.res, 1)
            for f in range(FT):
                split_lo(2 * f)
                split_lo(2 * f + 1)
                dve.wait_ge(s.silu_done, f + 1)
                dve.wait_ge(s.w_used, 2 * f + 2)
                if f >= 1:
                    dve.wait_ge(s.a_lo, f)
                dve.tensor_tensor(b.prod[:, 0:T], ps[:, gate_bank(f) + 1, 0:T], b.sil[:, f % 2, 0:T], ALU.mult).then_inc(s.prod_done, 1)
                dve.wait_ge(s.a_hi, f + 1)
                dve.tensor_tensor(b.act_lo[:, f, 0:T], b.prod[:, 0:T], b.act_hi[:, f, 0:T].bitcast(F32), ALU.subtract).then_inc(s.a_lo, 1)
                if before and 2 <= f < 2 + before.n:
                    k = f - 2
                    dve.wait_ge(s.rstd, k + 1)
                    dve.scalar_tensor_tensor(out=before.x[:, k, :], in0=before.x[:, k, :], scalar=b.rstd[:, k:k + 1], in1=b.gain_f[:],
                                             op0=ALU.mult, op1=ALU.mult).then_inc(s.normed, 1)
            for f in range(FT):
                split_lo(2 * FT + f)
                if following:
                    for k in range(following.n):
                        if f == squared_at(k) + 1:
                            dve.wait_ge(s.n_rstd, k + 1)
                            dve.scalar_tensor_tensor(out=b.xn[:, k % 2, :], in0=following.x[:, k, :], scalar=b.n_rstd[:, k:k + 1], in1=b.gain2[:],
                                                     op0=ALU.mult, op1=ALU.mult).then_inc(s.n_normed, 1)
                        for j in range(2):
                            if f == turned_at(k, j):
                                dve.wait_ge(s.n_hi, 2 * k + j + 1)
                                part = b.h_hi[:, 4 * j:4 * j + 4, k * P:(k + 1) * P]
                                dve.tensor_tensor(b.h_lo[:, 4 * j:4 * j + 4, k * P:(k + 1) * P], ps[:, 6 + j, :].rearrange("p (d t) -> p d t", d=4),
                                                  part.bitcast(F32), ALU.subtract).then_inc(s.n_lo, 1)

        @block.tensor
        def _(pe):
            def item(i):
                if i >= AHEAD:
                    pe.wait_ge(s.w_lo, i - AHEAD + 1)
                return w.hi[:, i % RING, :], w.lo[:, i % RING, :]

            for f in range(FT):
                if f == 1 and before:
                    pe.wait_ge(s.res, 1)
                if f >= 2:
                    pe.wait_ge(s.prod_done, f - 1)
                for u in range(2):
                    hi, lo = item(2 * f + u)
                    out = ps[:, gate_bank(f) + u, 0:T]
                    for d in range(DT):
                        a_hi, a_lo = hi[:, d * P:(d + 1) * P], lo[:, d * P:(d + 1) * P]
                        pe.matmul(out, a_hi, b.h_hi[:, d, 0:T], start=(d == 0), stop=False)
                        pe.matmul(out, a_hi, b.h_lo[:, d, 0:T], start=False, stop=False)
                        mm = pe.matmul(out, a_lo, b.h_hi[:, d, 0:T], start=False, stop=(d == DT - 1))
                    mm.then_inc(s.w_used, 1)
            for f in range(FT):
                if following:
                    for k in range(following.n):
                        for j in range(2):
                            if f == turned_at(k, j):
                                pe.wait_ge(s.n_normed, k + 1)
                                if k >= 1:
                                    pe.wait_ge(s.n_lo, 2 * (k - 1) + j + 1)
                                for d in range(4):
                                    turned = pe.transpose(ps[:, 6 + j, d * P:(d + 1) * P], b.xn[:, k % 2, (4 * j + d) * P:(4 * j + d + 1) * P], c.ident[:])
                                turned.then_inc(s.n_turned, 1)
                if f == 0 and before:
                    pe.wait_ge(s.res, before.n)
                hi, lo = item(2 * FT + f)
                pe.wait_ge(s.a_lo, f + 1)
                for k in range(n):
                    if f == 0 and k == 2:
                        pe.wait_ge(s.prod_done, FT)
                    for e in range(2):
                        out = ps[:, 2 * k + e, :]
                        cols = slice(e * BLK, (e + 1) * BLK)
                        a_hi, a_lo = b.act_hi[:, f, k * P:(k + 1) * P], b.act_lo[:, f, k * P:(k + 1) * P]
                        pe.matmul(out, a_hi, hi[:, cols], start=(f == 0), stop=False)
                        pe.matmul(out, a_hi, lo[:, cols], start=False, stop=False)
                        mm = pe.matmul(out, a_lo, hi[:, cols], start=False, stop=(f == FT - 1))
                mm.then_inc(s.w_used, 1)


def gate_bank(f):
    return 6 if f % 2 == 0 else 4


def finish(nc, c, b, ps, last):
    with stage(nc, "res squared var rstd normed stored") as (block, s):

        @block.vector
        def _(dve):
            for k in range(last.n):
                dve.tensor_tensor(last.x[:, k, :], ps[:, 2 * k:2 * k + 2, :].rearrange("p a n -> p (a n)"), last.x[:, k, :],
                                  ALU.add).then_inc(s.res, 1)
            for k in range(last.n):
                dve.wait_ge(s.rstd, k + 1)
                dve.scalar_tensor_tensor(out=last.x[:, k, :], in0=last.x[:, k, :], scalar=b.rstd[:, k:k + 1], in1=b.gain_f[:],
                                         op0=ALU.mult, op1=ALU.mult).then_inc(s.normed, 1)

        @block.scalar
        def _(act):
            for k in range(last.n):
                act.wait_ge(s.res, k + 1)
                act.activation(b.xn[:, k, :], last.x[:, k, :], ACT.Square, accum_out=b.ss[:, k:k + 1]).then_inc(s.squared, 1)

        @block.gpsimd
        def _(pool):
            for k in range(last.n):
                pool.wait_ge(s.squared, k + 1)
                pool.tensor_scalar(b.rstd[:, k:k + 1], b.ss[:, k:k + 1], 1.0 / D, EPS, ALU.mult, ALU.add).then_inc(s.var, 1)
                pool.wait_ge(s.var, k + 1)
                pool.tensor_tensor(b.rstd[:, k:k + 1], b.rstd[:, k:k + 1], c.minus_half[:], ALU.pow).then_inc(s.rstd, 1)

        @block.sync
        def _(sp):
            for k in range(last.n):
                sp.wait_ge(s.normed, k + 1)
                sp.dma_start(last.dst(k), last.x[0:last.rows(k), k, :]).then_inc(s.stored, 16)
            sp.wait_ge(s.stored, 16 * last.n)


class PromptTiles:

    def __init__(self, sb, conv_w, scratch, first):
        self.gate = sb("conv_gate", [P, SLOTS, CW])
        self.ch = sb("conv_c_h", [P, SLOTS, 3, 2 * CW])
        self.u = sb("conv_u", [P, 3, CW])
        self.sum = sb("conv_sum", [P, CW])
        self.w, self.scratch, self.first = conv_w, scratch, first

    def load(self, sp, s, k, y, parts, fox):
        row = (self.first + k) * P
        proj = self.scratch.proj
        if k >= SLOTS:
            sp.wait_ge(s.normed, k - SLOTS + 1)
        sp.dma_start(self.gate[:, k % SLOTS, :], proj[ds(row + PAD, P), 0:CW]).then_inc(parts, 16)
        for back in range(3):
            sp.dma_start(self.ch[:, k % SLOTS, back, :], proj[ds(row + PAD - back, P), CW:3 * CW]).then_inc(parts, 16)
        sp.dma_start(y[:, k % SLOTS, CW:CW + FW], self.scratch.fox[ds(row, P), :]).then_inc(fox, 16)
        sp.dma_start(y[:, k % SLOTS, CW + FW:D], self.scratch.mem[ds(row, P), :]).then_inc(fox, 16)

    def ready(self, act, s, k, fox):
        act.wait_ge(fox, 32 * (k // SLOTS + 1))

    def conv(self, pool, s, k, y, parts):
        steps = 4 * k
        pool.wait_ge(parts, 64 * (k // SLOTS + 1))
        pool.tensor_tensor(self.u[:], self.ch[:, k % SLOTS, :, 0:CW], self.ch[:, k % SLOTS, :, CW:2 * CW], ALU.mult).then_inc(s.conv_step, 1)
        pool.wait_ge(s.conv_step, steps + 1)
        pool.tensor_tensor(self.u[:], self.u[:], self.w[:], ALU.mult).then_inc(s.conv_step, 1)
        pool.wait_ge(s.conv_step, steps + 2)
        pool.tensor_tensor(self.sum[:], self.u[:, 2, :], self.u[:, 1, :], ALU.add).then_inc(s.conv_step, 1)
        pool.wait_ge(s.conv_step, steps + 3)
        pool.tensor_tensor(self.sum[:], self.sum[:], self.u[:, 0, :], ALU.add).then_inc(s.conv_step, 1)
        pool.wait_ge(s.conv_step, steps + 4)
        pool.tensor_tensor(y[:, k % SLOTS, 0:CW], self.sum[:], self.gate[:, k % SLOTS, :], ALU.mult).then_inc(s.conv, 1)


class SampleTile:

    def __init__(self, src):
        self.src = src

    def load(self, sp, s, k, y, parts, fox):
        sp.wait_ge(s.conv, 1)
        sp.dma_start(y[0:DB, 0, :], self.src).then_inc(fox, 16)

    def ready(self, act, s, k, fox):
        act.wait_ge(fox, 16)

    def conv(self, pool, s, k, y, parts):
        pool.memset(y[:, 0, :], 0.0).then_inc(s.conv, 1)


def sample_outputs(nc, c, io, scratch, dec, conv_w, y):
    with ExitStack() as ctx:
        sb, _ = alloc(ctx, nc)
        rows = sb("rows", [P, PW])
        fox = sb("fox_rows", [P, FW])
        state = sb("state", [P, 3, CW])
        u = sb("weighted", [P, 3, CW])
        new = sb("new_value", [P, FW])
        last = sb("last_c_h", [P, 2 * CW])
        last_u = sb("last_u", [P, CW])
        with stage(nc, "loaded chain stored") as (block, s):

            @block.sync
            def _(sp):
                sp.dma_start(rows[0:DB, :], scratch.samp).then_inc(s.loaded, 16)
                sp.dma_start(fox[0:DB, :], scratch.samp_fox).then_inc(s.loaded, 16)
                sp.dma_start(state[0:DB, 0:2, :], io.state_conv.rearrange("l b k c -> (l b) k c")).then_inc(s.loaded, 16)
                sp.dma_start(last[0:PAD, :], scratch.proj[SEQ:SEQ + PAD, CW:3 * CW]).then_inc(s.loaded, 16)
                sp.wait_ge(s.chain, 8)
                sp.dma_start(io.new_conv_s.rearrange("b k c -> b k c"), state[0:DB, 1:3, :]).then_inc(s.stored, 16)
                sp.dma_start(io.new_conv, last_u[0:PAD, :]).then_inc(s.stored, 16)
                sp.dma_start(scratch.samp_y, y[0:DB, :]).then_inc(s.stored, 16)
                sp.wait_ge(s.stored, 48)

            @block.vector
            def _(dve):
                chain = [0]

                def link(ins):
                    chain[0] += 1
                    ins.then_inc(s.chain, 1)
                    dve.wait_ge(s.chain, chain[0])

                heads = [DB, FH, HD]
                dve.wait_ge(s.loaded, 64)
                dve.tensor_tensor(last_u[0:PAD, :], last[0:PAD, 0:CW], last[0:PAD, CW:], ALU.mult)
                link(dve.tensor_tensor(state[0:DB, 2, :], rows[0:DB, CW:2 * CW], rows[0:DB, 2 * CW:3 * CW], ALU.mult))
                for back in range(3):
                    done = dve.tensor_tensor(u[0:DB, back, :], state[0:DB, 2 - back, :], conv_w[0:DB, back, :], ALU.mult)
                link(done)
                link(dve.tensor_tensor(u[0:DB, 2, :], u[0:DB, 2, :], u[0:DB, 1, :], ALU.add))
                link(dve.tensor_tensor(u[0:DB, 2, :], u[0:DB, 2, :], u[0:DB, 0, :], ALU.add))
                link(dve.tensor_tensor(y[0:DB, 0:CW], u[0:DB, 2, :], rows[0:DB, 0:CW], ALU.mult))
                link(dve.tensor_tensor(new[0:DB, :].rearrange("p (h d) -> p h d", d=HD), rows[0:DB, VCOL:VCOL + FW].rearrange("p (h d) -> p h d", d=HD),
                                       dec.w_new[0:DB, :].unsqueeze(2).to_broadcast(heads), ALU.mult))
                link(dve.tensor_tensor(new[0:DB, :], new[0:DB, :], fox[0:DB, :], ALU.add))
                link(dve.tensor_tensor(y[0:DB, CW:CW + FW].rearrange("p (h d) -> p h d", d=HD), new[0:DB, :].rearrange("p (h d) -> p h d", d=HD),
                                       dec.r_fox[0:DB, :].unsqueeze(2).to_broadcast(heads), ALU.mult))


def load(nc, pairs):
    with stage(nc, "loaded") as (block, s):

        @block.sync
        def _(sp):
            for dst, src in pairs:
                sp.dma_start(dst, src).then_inc(s.loaded, 16)
            sp.wait_ge(s.loaded, 16 * len(pairs))


def decoder_step(nc, io):
    def dram(name, shape):
        return nc.dram_tensor(name, shape, F32, kind="Internal").ap()

    scratch = group(proj=io.proj, samp=io.samp, gates=dram("gate_logits", (FH, SEQ + P)), neg_cum=dram("neg_cum", (FH, SEQ)), fox=dram("fox", (SEQ, FW)),
                              mem=dram("mem", (SEQ, MW)), x1=dram("x1", (SEQ, D)), samp_fox=dram("samp_fox", (DB, FW)),
                              samp_y=dram("samp_y", (DB, D)), samp_x1=dram("samp_x1", (DB, D)))
    w_in = io.w_in.rearrange("(d p) n -> p d n", p=P)
    w_mem = io.w_mem_kv.rearrange("(d p) n -> p d n", p=P)
    last_page = io.cache_k.shape[1] - 1
    key_pages = io.cache_k.rearrange("l n r h d -> (l n) r (h d)")
    value_pages = io.cache_v.rearrange("l n r h d -> (l n) r (h d)")

    with ExitStack() as whole:
        sb, _ = alloc(whole, nc)
        c = group(ident=sb("ident", [P, P]), ident_r=sb("ident_r", [P, P], F32R), causal_r=sb("causal_r", [P, P], F32R),
                            page_before=sb("page_before", [P, P]), seq_of_page=sb("seq_of_page", [P, 2, DB]),
                            own_head=sb("own_head", [P, FW]), fold=sb("fold", [P, HD]), ones=sb("ones", [P, 1]),
                            minus_half=sb("minus_half", [P, 1]), b_f=sb("b_f", [P, 1]), pages=sb("pages", [1, DB * PAGES], I32),
                            page_index=sb("page_index", [P, 2], U32),
                  gathered=whole.enter_context(nc.semaphore("gathered")))
        early = whole.enter_context(ExitStack())
        early_sb, _ = alloc(early, nc)
        y_samp = early_sb("y_samp", [P, D])
        dec = group(scores=early_sb("scores", [P, DB * PAGES * FH]), mem_scores=early_sb("mem_scores", [P, DB * 2 * MH]),
                              logf_new=early_sb("logf_new", [P, FH]), w_new=early_sb("w_new", [P, FH]), r_fox=early_sb("r_fox", [P, FH]), r_mem=early_sb("r_mem", [P, MH]))
        setup_constants(nc, c, io)

        with ExitStack() as ctx:
            sb, _ = alloc(ctx, nc)
            h_hi = sb("h_hi", [P, DT, HALF * P], F32R)
            h_lo = sb("h_lo", [P, DT, HALF * P], F32R)
            w = group(raw=sb("w_raw", [P, DT, BLK]), hi=sb("w_hi", [P, 2, DT, BLK], F32R), lo=sb("w_lo", [P, 2, DT, BLK], F32R))
            wf_hi = sb("wf_hi", [P, DT, P], F32R)
            wf_lo = sb("wf_lo", [P, DT, P], F32R)
            with ExitStack() as inner:
                gain = inner.enter_context(nc.sbuf_tensor("gain_mem", [P, D], F32))
                zero = inner.enter_context(nc.sbuf_tensor("zero_rows", [PAD, 2 * CW], F32))
                with stage(nc, "loaded zeroed stored") as (block, s):

                    @block.gpsimd
                    def _(pool):
                        pool.memset(zero[:], 0.0).then_inc(s.zeroed, 1)

                    @block.sync
                    def _(sp):
                        sp.dma_start(gain[:], io.mem_norm_g.to_broadcast([P, D])).then_inc(s.loaded, 16)
                        sp.wait_ge(s.zeroed, 1)
                        sp.dma_start(scratch.proj[0:PAD, CW:3 * CW], zero[:]).then_inc(s.stored, 16)
                        sp.wait_ge(s.loaded, 16)
                        sp.wait_ge(s.stored, 16)
                split_weights(nc, weight_parts(w.raw[:], w.hi[:, 1], w.lo[:, 1], w_mem))
                norm_transpose(nc, c, 2, lambda k: io.mem_prompt[k * P:(k + 1) * P, :], gain[:], h_hi, h_lo)

            def block_columns(n):
                return lambda j: [(w.raw[:, 2 * j:2 * j + 2, 0:CW], w_in[:, 2 * j:2 * j + 2, ds(n * BLK, CW)]),
                                  (w.raw[:, 2 * j:2 * j + 2, CW:BLK], w_in[:, 2 * j:2 * j + 2, ds(n * BLK + CW + (n // (NBLK - 1)) * FH, CW)])]

            project(nc, c, 2, h_hi, h_lo, w, 1, lambda t: io.mem_kv[t * P:(t + 1) * P, :], block_columns(0))
            gain = sb("gain1", [P, D])
            load(nc, [(gain[:], io.norm1_g.to_broadcast([P, D]))])
            split_weights(nc, weight_parts(w.raw[:, :, 0:P], wf_hi[:], wf_lo[:], w_in[:, :, FCOL:FCOL + P]))
            norm_transpose(nc, c, 1, lambda k: io.x_sample[:, :], gain[:], h_hi, h_lo, rows=DB, gates=(wf_hi, wf_lo, scratch.gates[:, SEQ:]))
            with nc.Fori(0, NBLK) as n:
                project(nc, c, 1, h_hi, h_lo, w, n % 2, lambda t: scratch.samp[:, ds(n * BLK, BLK)],
                        block_columns((n + 1) % NBLK), rows=DB)
            for half in range(2):
                first = half * HALF
                norm_transpose(nc, c, HALF, lambda k: io.x_prompt[(first + k) * P:(first + k + 1) * P, :], gain[:], h_hi, h_lo,
                               gates=(wf_hi, wf_lo, scratch.gates[:, first * P:(first + HALF) * P]))
                for n0, n1 in ((0, NBLK),) if half == 0 else ((0, DB - NBLK), (DB - NBLK, NBLK)):
                    with nc.Fori(n0, n1) as n:
                        seq = n + half * NBLK
                        keys = None
                        if n0 == 0:
                            keys = group(seq=seq, scores=dec.scores, cache=key_pages, last_page=last_page,
                                                   query=scratch.samp[ds(seq, 1), QCOL:QCOL + FW].to_broadcast([P, FW]))
                        project(nc, c, HALF, h_hi, h_lo, w, (n + half + 1) % 2,
                                lambda t: scratch.proj[PAD + (first + t) * P:PAD + (first + t + 1) * P, ds(n * BLK, BLK)],
                                block_columns((n + 1) % NBLK), keys=keys)
        with ExitStack() as ctx:
            sb, _ = alloc(ctx, nc)
            gates = sb("gates2", [P, SEQ + P])
            load(nc, [(gates[0:FH, :], scratch.gates)])
            forget_gates(nc, c, gates, io, scratch, dec)
        decode_softmax(nc, c, io, scratch, dec)

        decode_memory_values(nc, c, io, dec, y_samp[:, CW + FW:D])
        with ExitStack() as ctx:
            sb, _ = alloc(ctx, nc)
            a = group(q=sb("q_raw", [P, NT, 2, HD]), k=sb("k_raw", [P, NT, 2, HD]), v=sb("v_raw", [P, NT, HD]),
                                neg_cum=sb("neg_cum_all", [P, SEQ]), k_st=sb("k_stacked", [P, SEQ], F32R),
                                q_hi=sb("q_hi", [P, SEQ], F32R), q_lo=sb("q_lo", [P, SEQ], F32R), v_st=sb("v_stacked", [P, NT, P], F32R),
                                probs=sb("probs", [P, 2, QCH, SEQ]), p_hi=sb("p_hi", [P, 2, BLK], F32R), p_lo=sb("p_lo", [P, 2, BLK], F32R),
                                o_t=sb("o_turned", [P, 2, BLK]), o_out=sb("o_out", [P, QCH, QCH, HD]), low=sb("low", [P, NT]),
                                low2=sb("low2", [P, 2, NT]), sums=sb("row_sums", [P, NT]), inv=sb("inverse", [P, NT]), zeros=sb("zeros", [P, MEM]))
            page_v = sb("page_v", [P, 4, FW])
            weights = sb("weights", [P, PAGES * FH])
            own = sb("own", [P, FW])
            row = sb("row", [P, FW])

            def fox_head(h):
                return group(q=scratch.proj[PAD:, ds(h * HD + QCOL, HD)], k=scratch.proj[PAD:, ds(h * HD + KCOL, HD)],
                                       v=scratch.proj[PAD:, ds(h * HD + VCOL, HD)], neg_cum=scratch.neg_cum[ds(h, 1), :])

            def mem_head(h):
                return group(q=scratch.proj[PAD:, ds(h * HD + MCOL, HD)], k=io.mem_kv[:, ds(h * HD, HD)],
                                       v=io.mem_kv[:, ds(h * HD + MW, HD)], neg_cum=None)

            def first_head(head, nk):
                with stage(nc, "loaded decay") as (block, s):

                    @block.sync
                    def _(sp):
                        load_head(sp, a, head, nk, s.loaded)
                        load_decay(sp, a, head, s.decay)
                        sp.wait_ge(s.loaded, 48)
                        if head.neg_cum is not None:
                            sp.wait_ge(s.decay, 16)

                    @block.gpsimd
                    def _(pool):
                        pool.memset(a.zeros[:], 0.0)
                        pool.wait_ge(s.loaded, 48)
                        double_head(pool, a, nk)

            first_head(fox_head(0), NT)
            with nc.Fori(0, FH) as h:
                values = group(seq=h, cache=value_pages, last_page=last_page, page_v=page_v, weights=weights, own=own, row=row,
                                         all_weights=dec.scores[:, ds(h * (PAGES * FH), PAGES * FH)], dst=scratch.samp_fox[ds(h, 1), :])
                attend(nc, c, a, NT, True, fox_head((h + 1) % FH),
                       lambda ch: scratch.fox[ch * BLK:(ch + 1) * BLK, ds(h * HD, HD)].rearrange("(r p) d -> p r d", p=P), values)
            first_head(mem_head(0), 2)
            with nc.Fori(0, MH) as h:
                attend(nc, c, a, 2, False, mem_head((h + 1) % MH),
                       lambda ch: scratch.mem[ch * BLK:(ch + 1) * BLK, ds(h * HD, HD)].rearrange("(r p) d -> p r d", p=P))

        with ExitStack() as ctx:
            sb, _ = alloc(ctx, nc)
            w = group(hi=sb("wo_hi", [P, DT, D], F32R), lo=sb("wo_lo", [P, DT, D], F32R))
            gain = sb("gain_out", [P, D])
            conv_w = sb("conv_w", [P, 3, CW])
            load(nc, [(gain[:], io.out_norm_g.to_broadcast([P, D]))] +
                 [(conv_w[:, back, :], io.conv_w[2 - back:3 - back, :].to_broadcast([P, CW])) for back in range(3)])
            with ExitStack() as inner:
                raw = inner.enter_context(nc.sbuf_tensor("wo_raw", [P, DT, D], F32))
                split_weights(nc, weight_parts(raw[:], w.hi[:], w.lo[:], io.w_out.rearrange("(d p) n -> p d n", p=P)))
            sample_outputs(nc, c, io, scratch, dec, conv_w, y_samp)
            mix(nc, c, 1, w, gain, SampleTile(scratch.samp_y), lambda k: io.x_sample, lambda k: scratch.samp_x1, rows=DB)
            with nc.Fori(0, NT // HALF) as half:
                with ExitStack() as inner:
                    tiles = PromptTiles(alloc(inner, nc)[0], conv_w, scratch, half * HALF)
                    mix(nc, c, HALF, w, gain, tiles, lambda k: io.x_prompt[ds((half * HALF + k) * P, P), :],
                        lambda k: scratch.x1[ds((half * HALF + k) * P, P), :])

        early.close()

        with ExitStack() as ctx:
            sb, psum = alloc(ctx, nc)
            T = FCH * P
            x1 = sb("x1_tiles", [P, 2, FCH, D])
            h_hi, h_lo = sb("h2_hi", [P, DT, T], F32R), sb("h2_lo", [P, DT, T], F32R)
            gain2, gain_f = sb("gain2", [P, D]), sb("gain_f", [P, D])
            w = group(raw=sb("w_items", [P, RING, D]), hi=sb("w_items_hi", [P, RING, D], F32R), lo=sb("w_items_lo", [P, RING, D], F32R))

            def chunk(ch):
                return group(n=FCH, x=x1[:, ch % 2], rows=lambda k: P,
                             src=lambda k: scratch.x1[ds((ch * FCH + k) * P, P), :], dst=lambda k: io.y_prompt[ds((ch * FCH + k) * P, P), :])

            left = NT - FULL * FCH
            last = group(n=left + 1, x=x1[:, FULL % 2], rows=lambda k: P if k < left else DB,
                         src=lambda k: scratch.x1[(FULL * FCH + k) * P:(FULL * FCH + k + 1) * P, :] if k < left else scratch.samp_x1,
                         dst=lambda k: io.y_prompt[(FULL * FCH + k) * P:(FULL * FCH + k + 1) * P, :] if k < left else io.y_sample)
            load(nc, [(gain2[:], io.norm2_g.to_broadcast([P, D])), (gain_f[:], io.final_norm_g.to_broadcast([P, D]))])
            split_weights(nc, [(w.raw[:, i, :], w.hi[:, i, :], w.lo[:, i, :], [(weight_slot(w, i), weight_source(io, i))]) for i in range(AHEAD)])
            norm_transpose(nc, c, FCH, chunk(0).src, gain2[:], h_hi, h_lo, keep=x1[:, 0])
            b = group(h_hi=h_hi, h_lo=h_lo, gain2=gain2, gain_f=gain_f, act_hi=sb("act_hi", [P, FT, T], F32R), act_lo=sb("act_lo", [P, FT, T], F32R),
                      sil=sb("silu", [P, 2, T]), prod=sb("silu_up", [P, T]), xn=sb("x_normed", [P, 2, D]), ss=sb("sum_squares", [P, FCH]),
                      rstd=sb("rstd", [P, FCH]), n_ss=sb("next_sum_squares", [P, FCH]), n_rstd=sb("next_rstd", [P, FCH]))
            ps = psum("ps_ffn", [P, 8, BLK])
            ffn(nc, c, FCH, b, w, ps, io, following=chunk(1))
            with nc.Fori(1, FULL - 1) as ch:
                ffn(nc, c, FCH, b, w, ps, io, before=chunk(ch - 1), following=chunk(ch + 1))
            ffn(nc, c, FCH, b, w, ps, io, before=chunk(FULL - 2), following=last)
            ffn(nc, c, last.n, b, w, ps, io, before=chunk(FULL - 1))
            finish(nc, c, b, ps, last)


_INS = ["x_prompt", "x_sample", "mem_prompt", "cache_k", "cache_v", "cache_logf", "state_conv", "cache_mem_k", "cache_mem_v",
        "page_table", "norm1_g", "w_in", "b_f", "conv_w", "mem_norm_g", "w_mem_kv", "out_norm_g", "w_out", "norm2_g",
        "w_gate", "w_up", "w_down", "final_norm_g"]
_OUTS = {"y_prompt": (SEQ, D), "y_sample": (DB, D), "proj": (PAD + SEQ, PW), "samp": (DB, PW), "mem_kv": (MEM, 2 * MW),
         "new_logf": (SEQ, FH), "new_logf_s": (DB, FH), "new_conv": (PAD, CW), "new_conv_s": (DB, PAD, CW)}
_FLAT = {"x_prompt": (SEQ, D), "x_sample": (DB, D), "mem_prompt": (MEM, D), "w_in": None, "conv_w": None, "w_mem_kv": None,
         "w_out": None, "w_gate": None, "w_up": None, "w_down": None, "final_norm_g": (1, D)}


def kernel(**inputs):
    import numpy as np
    import concourse.bacc as bacc
    from concourse.bass_utils import run_bass_kernel_spmd

    nc = bacc.Bacc("TRN2", target_bir_lowering=False, num_devices=1)
    arrays, io = {}, {}
    for name in _INS:
        a = np.ascontiguousarray(inputs[name])
        if name in _FLAT:
            a = a.reshape(_FLAT[name] or a.shape[1:])
        arrays[f"in_{name}"] = a
        io[name] = nc.dram_tensor(f"in_{name}", a.shape, mybir.dt.from_np(a.dtype), kind="ExternalInput").ap()
    for name, shape in _OUTS.items():
        io[name] = nc.dram_tensor(f"out_{name}", shape, F32, kind="ExternalOutput").ap()
    decoder_step(nc, group(**io))
    r = run_bass_kernel_spmd(nc, [arrays], core_ids=[0]).results[0]
    out = {name: r[f"out_{name}"] for name in _OUTS}
    proj, samp, mem_kv = out["proj"][PAD:], out["samp"], out["mem_kv"]
    heads = (1, 1, SEQ, FH, HD)
    sample_heads = (1, DB, 1, FH, HD)
    return (out["y_prompt"].reshape(1, SEQ, D), out["y_sample"].reshape(DB, 1, D),
            proj[:, KCOL:KCOL + FW].reshape(heads), proj[:, VCOL:VCOL + FW].reshape(heads),
            out["new_logf"].reshape(1, 1, SEQ, FH), out["new_conv"].reshape(1, 1, PAD, CW),
            mem_kv[:, 0:MW].reshape(1, 1, MEM, MH, HD), mem_kv[:, MW:].reshape(1, 1, MEM, MH, HD),
            samp[:, KCOL:KCOL + FW].reshape(sample_heads), samp[:, VCOL:VCOL + FW].reshape(sample_heads),
            out["new_logf_s"].reshape(1, DB, 1, FH), out["new_conv_s"].reshape(1, DB, PAD, CW))
```

```python
from collections import namedtuple
from contextlib import ExitStack, contextmanager

import concourse.bass as bass
from concourse import mybir

F32 = mybir.dt.float32
F32R = mybir.dt.float32r
I32 = mybir.dt.int32
U32 = mybir.dt.uint32
ALU = mybir.AluOpType
ACT = mybir.ActivationFunctionType
AX = mybir.AxisListType
RMAX = bass.bass_isa.ReduceOp.max
RADD = bass.bass_isa.ReduceOp.add
ds = bass.ds

P = 128
D = 1024
SEQ = 2048
HD = 64
CW = 256
FW = 512
MW = 256
FH = FW // HD
MH = MW // HD
MEM = 256
DB = 8
PAGES = 32
D_FF = 2816
DT = D // P
NT = SEQ // P
QCH = 4
FT = D_FF // P
FCH = 3
FULL = NT // FCH
RING = 3
SLOTS = 4
DOUBLE_FROM = 12
AHEAD = RING - 1
ITEMS = 3 * FT
EPS = 1e-6
SCALE = HD ** -0.5
NEG = -1.0e30
BIG = 3.0e38
BLK = 512
NBLK = 5
HALF = 8
PAD = 2
QCOL = 3 * CW
KCOL = QCOL + FW
VCOL = KCOL + FW
FCOL = VCOL + FW
MCOL = FCOL
PW = NBLK * BLK


def group(**things):
    return namedtuple("group", list(things))(**things)


class Steps:

    def __init__(self):
        self.score = self.turned = self.page = self.scored = self.joined = self.bank = 0
        self.uses = []


@contextmanager
def stage(nc, names):
    with ExitStack() as ctx:
        sems = [ctx.enter_context(nc.semaphore(n)) for n in names.split()]
        with nc.Block() as block:
            yield block, group(**dict(zip(names.split(), sems)))
        numbers = sorted(s.num for s in sems)
        starts = [n for n in numbers if n - 1 not in numbers]
        for n0 in starts:
            n1 = n0
            while n1 in numbers:
                n1 += 1
            nc.sync.sem_clear(range(n0, n1))
        nc.all_engine_barrier()


SERIAL = [0]


def alloc(ctx, nc):
    def own_name(name):
        SERIAL[0] += 1
        return f"{name}_{SERIAL[0]}"

    def sb(name, shape, dt=F32):
        return ctx.enter_context(nc.sbuf_tensor(own_name(name), shape, dt))

    def ps(name, shape, dt=F32):
        return ctx.enter_context(nc.psum_tensor(own_name(name), shape, dt))

    return sb, ps


def setup_constants(nc, c, io):
    with ExitStack() as ctx:
        sb, _ = alloc(ctx, nc)
        causal = sb("causal", [P, P])
        with stage(nc, "filled ready loaded") as (block, s):

            @block.gpsimd
            def _(pool):
                pool.memset(c.ident[:], 0.0).then_inc(s.filled, 1)
                pool.memset(causal[:], 0.0).then_inc(s.filled, 1)
                pool.memset(c.page_before[:], 1.0).then_inc(s.filled, 1)
                pool.memset(c.own_head[:], 1.0).then_inc(s.filled, 1)
                pool.memset(c.seq_of_page[:], 0.0).then_inc(s.filled, 1)
                pool.memset(c.ones[:], 1.0).then_inc(s.filled, 1)
                pool.memset(c.minus_half[:], -0.5).then_inc(s.filled, 1)
                pool.wait_ge(s.filled, 7)
                pool.affine_select(out=c.ident[:], in_=c.ident[:], compare_op=ALU.not_equal, fill=1.0, base=0,
                                   pattern=[[-1, P]], channel_multiplier=1).then_inc(s.ready, 1)
                pool.affine_select(out=causal[:], in_=causal[:], compare_op=ALU.is_ge, fill=NEG, base=0,
                                   pattern=[[-1, P]], channel_multiplier=1).then_inc(s.ready, 1)
                pool.affine_select(out=c.page_before[:], in_=c.page_before[:], compare_op=ALU.is_gt, fill=0.0,
                                   base=0, pattern=[[1, P]], channel_multiplier=-1).then_inc(s.ready, 1)
                pool.affine_select(out=c.own_head[:], in_=c.own_head[:], compare_op=ALU.is_ge, fill=0.0, base=0,
                                   pattern=[[1, FW]], channel_multiplier=-HD).then_inc(s.ready, 1)
                pool.wait_ge(s.ready, 4)
                pool.affine_select(out=c.own_head[:], in_=c.own_head[:], compare_op=ALU.is_ge, fill=0.0,
                                   base=HD - 1, pattern=[[-1, FW]], channel_multiplier=HD).then_inc(s.ready, 1)

            @block.vector
            def _(dve):
                dve.wait_ge(s.ready, 4)
                dve.tensor_copy(c.ident_r[:], c.ident[:])
                dve.tensor_copy(c.causal_r[:], causal[:])
                dve.tensor_copy(c.fold[0:HD, :], c.ident[0:HD, 0:HD])
                dve.tensor_copy(c.fold[HD:P, :], c.ident[HD:P, HD:P])
                for k in range(P // PAGES):
                    rows = slice(k * PAGES, (k + 1) * PAGES)
                    if k < P // PAGES - 1:
                        dve.memset(c.page_before[rows, (k + 1) * PAGES:], 0.0)
                    for g in range(2):
                        j = g * (P // PAGES) + k
                        dve.memset(c.seq_of_page[rows, g, j:j + 1], 1.0)

            @block.sync
            def _(sp):
                sp.dma_start(c.b_f[0:FH, :], io.b_f.rearrange("l h -> h l")).then_inc(s.loaded, 16)
                sp.dma_start(c.pages[0:1, :], io.page_table.rearrange("b n -> (b n)").unsqueeze(0)).then_inc(s.loaded, 16)
                for g in range(2):
                    half = io.page_table[4 * g:4 * g + 4, :].rearrange("b n -> (b n)").unsqueeze(1)
                    sp.dma_start(c.page_index[:, g:g + 1], half.bitcast(U32)).then_inc(s.loaded, 16)
                sp.wait_ge(s.ready, 5)
                sp.dma_start(c.own_head[FH:2 * FH, :], c.own_head[0:FH, :]).then_inc(s.loaded, 16)
                sp.wait_ge(s.loaded, 80)


def load_parts(sp, parts, loaded):
    for j, (_, _, _, src) in enumerate(parts):
        for dst, part in src:
            sp.dma_start(dst, part).then_inc(loaded[j], 16)


def split_parts_hi(act, parts, loaded, hi_done):
    for j, (raw, hi, _, src) in enumerate(parts):
        act.wait_ge(loaded[j], 16 * len(src))
        act.activation(hi, raw, ACT.Copy).then_inc(hi_done, 1)


def split_parts_lo(dve, parts, hi_done):
    for j, (raw, hi, lo, _) in enumerate(parts):
        dve.wait_ge(hi_done, j + 1)
        dve.tensor_tensor(lo, raw, hi.bitcast(F32), ALU.subtract)


def split_weights(nc, parts, also=()):
    with stage(nc, "loaded0 loaded1 loaded2 loaded3 also hi_done") as (block, s):
        loaded = (s.loaded0, s.loaded1, s.loaded2, s.loaded3)

        @block.sync
        def _(sp):
            load_parts(sp, parts, loaded)
            for dst, src in also:
                sp.dma_start(dst, src).then_inc(s.also, 16)
            if also:
                sp.wait_ge(s.also, 16 * len(also))

        @block.scalar
        def _(act):
            split_parts_hi(act, parts, loaded, s.hi_done)

        @block.vector
        def _(dve):
            split_parts_lo(dve, parts, s.hi_done)


def weight_parts(raw, hi, lo, src):
    rows = [slice(d, d + 2) for d in range(0, DT, 2)]
    return [(raw[:, r], hi[:, r], lo[:, r], [(raw[:, r], src[:, r])]) for r in rows]


def norm_transpose(nc, c, n, src, gain, hi, lo, rows=P, keep=None, gates=None):
    with ExitStack() as ctx:
        sb, psum = alloc(ctx, nc)
        x = keep if keep is not None else sb("x_in", [P, 3, D])
        slots = n if keep is not None else 3
        xn = sb("x_normed", [P, 3, D])
        ss = sb("sum_squares", [P, n])
        rstd = sb("rstd", [P, n])
        ps_t = psum("ps_transposed", [P, 2, D])
        ps_f = psum("ps_gates", [P, BLK])
        logits = sb("gate_logits", [P, n * P]) if gates else None
        with stage(nc, "zeroed load0 load1 load2 squared var rstd normed turned hi_done lo_done gate gate_out gates_stored") as (block, s):
            loads = (s.load0, s.load1, s.load2)
            gate_chunks = [(t0, min(BLK, n * P - t0)) for t0 in range(0, n * P, BLK)]

            @block.sync
            def _(sp):
                if rows < P:
                    sp.wait_ge(s.zeroed, 1)
                for k in range(n):
                    if k >= 3:
                        sp.wait_ge(s.normed, k - 2)
                    sp.dma_start(x[0:rows, k % slots, :], src(k)).then_inc(loads[k % 3], 16)
                if gates:
                    sp.wait_ge(s.gate_out, len(gate_chunks))
                    sp.dma_start(gates[2], logits[0:FH, :]).then_inc(s.gates_stored, 16)
                    sp.wait_ge(s.gates_stored, 16)

            @block.gpsimd
            def _(pool):
                if rows < P:
                    pool.memset(x[:, 0, :], 0.0).then_inc(s.zeroed, 1)
                for k in range(n):
                    pool.wait_ge(s.squared, k + 1)
                    pool.tensor_scalar(rstd[:, k:k + 1], ss[:, k:k + 1], 1.0 / D, EPS, ALU.mult, ALU.add).then_inc(s.var, 1)
                    pool.wait_ge(s.var, k + 1)
                    pool.tensor_tensor(rstd[:, k:k + 1], rstd[:, k:k + 1], c.minus_half[:], ALU.pow).then_inc(s.rstd, 1)

            @block.scalar
            def _(act):
                def square(k):
                    act.wait_ge(loads[k % 3], 16 * (k // 3 + 1))
                    if k >= 3:
                        act.wait_ge(s.turned, k - 2)
                    act.activation(xn[:, k % 3, :], x[:, k % slots, :], ACT.Square, accum_out=ss[:, k:k + 1]).then_inc(s.squared, 1)

                def gate_logits(j):
                    t0, w = gate_chunks[j]
                    act.wait_ge(s.gate, j + 1)
                    act.activation(logits[0:FH, t0:t0 + w], ps_f[0:FH, 0:w], ACT.Identity, bias=c.b_f[0:FH, :]).then_inc(s.gate_out, 1)

                for k in range(min(n, 2)):
                    square(k)
                for k in range(n):
                    if k + 2 < n:
                        square(k + 2)
                    act.wait_ge(s.turned, k + 1)
                    act.activation(hi[:, :, k * P:(k + 1) * P], ps_t[:, k % 2, :].rearrange("p (d t) -> p d t", d=DT),
                                   ACT.Copy).then_inc(s.hi_done, 1)
                    if gates and k == 6:
                        gate_logits(0)
                if gates:
                    gate_logits(len(gate_chunks) - 1)

            @block.vector
            def _(dve):
                def normalise(k):
                    dve.wait_ge(s.rstd, k + 1)
                    dve.scalar_tensor_tensor(out=xn[:, k % 3, :], in0=x[:, k % slots, :], scalar=rstd[:, k:k + 1],
                                             in1=gain, op0=ALU.mult, op1=ALU.mult).then_inc(s.normed, 1)

                normalise(0)
                for k in range(n):
                    if k + 1 < n:
                        normalise(k + 1)
                    dve.wait_ge(s.hi_done, k + 1)
                    dve.tensor_tensor(lo[:, :, k * P:(k + 1) * P], ps_t[:, k % 2, :].rearrange("p (d t) -> p d t", d=DT),
                                      hi[:, :, k * P:(k + 1) * P].bitcast(F32), ALU.subtract).then_inc(s.lo_done, 1)

            @block.tensor
            def _(pe):
                def gate_products(j):
                    t0, w = gate_chunks[j]
                    pe.wait_ge(s.lo_done, (t0 + w) // P)
                    if j >= 1:
                        pe.wait_ge(s.gate_out, j)
                    for d in range(DT):
                        for m, (a, b) in enumerate(((gates[0], hi), (gates[0], lo), (gates[1], hi))):
                            mm = pe.matmul(ps_f[:, 0:w], a[:, d, :], b[:, d, t0:t0 + w],
                                           start=(d == 0 and m == 0), stop=(d == DT - 1 and m == 2))
                    mm.then_inc(s.gate, 1)

                for k in range(n):
                    pe.wait_ge(s.normed, k + 1)
                    if k >= 2:
                        pe.wait_ge(s.lo_done, k - 1)
                    for d in range(DT):
                        turned = pe.transpose(ps_t[:, k % 2, d * P:(d + 1) * P], xn[:, k % 3, d * P:(d + 1) * P], c.ident[:])
                    turned.then_inc(s.turned, 1)
                    if gates and k == 5:
                        gate_products(0)
                if gates:
                    gate_products(len(gate_chunks) - 1)


def project(nc, c, n, h_hi, h_lo, w, buf, dst, following, rows=P, keys=None):
    nxt = 1 - buf
    groups = PAGES // 4
    pairs = DT // 2
    bufs = 3
    by_pool = (2, 5)
    with ExitStack() as ctx:
        sb, psum = alloc(ctx, nc)
        out = sb("proj_out", [P, 2, BLK])
        ps_p = psum("ps_proj", [P, 4, BLK])
        if keys:
            page_k = sb("page_k", [P, bufs, 4, FW])
            q_row = sb("q_row", [P, FW])
        with stage(nc, "w_in0 w_in1 w_in2 w_in3 w_hi made evacuated store0 store1 q_in keys0 keys1 keys2 pool_done prod_done keys_done") as (block, s):
            w_in = (s.w_in0, s.w_in1, s.w_in2, s.w_in3)
            stores = (s.store0, s.store1)
            keys_in = (s.keys0, s.keys1, s.keys2)

            def load_keys(eng, g):
                if g >= bufs:
                    eng.wait_ge(s.keys_done, g - bufs + 1)
                for j in range(4):
                    page = eng.value_load(c.pages[0:1, ds(keys.seq * PAGES + 4 * g + j, 1)], min_val=0, max_val=keys.last_page)
                    eng.dma_start(page_k[:, g % bufs, j, :], keys.cache[ds(page, 1)].rearrange("n r c -> (n r) c")).then_inc(keys_in[g % bufs], 16)

            @block.sync
            def _(sp):
                if keys:
                    sp.dma_start(q_row[:], keys.query).then_inc(s.q_in, 16)
                    load_keys(sp, 0)
                    load_keys(sp, 2)
                for j in range(pairs):
                    for to, part in following(j):
                        sp.dma_start(to, part).then_inc(w_in[j], 16)
                    if keys and j == 1:
                        load_keys(sp, 3)
                if keys:
                    for g in range(4, groups):
                        load_keys(sp, g)
                for k in range(min(n, 2)):
                    sp.wait_ge(stores[k], 16 * ((n - k + 1) // 2))

            @block.tensor
            def _(pe):
                for t in range(n):
                    if t >= 4:
                        pe.wait_ge(s.evacuated, t - 3)
                    for d in range(DT):
                        a_hi, a_lo = h_hi[:, d, t * P:(t + 1) * P], h_lo[:, d, t * P:(t + 1) * P]
                        b_hi, b_lo = w.hi[:, buf, d, :], w.lo[:, buf, d, :]
                        pe.matmul(ps_p[:, t % 4, :], a_hi, b_hi, start=(d == 0), stop=False)
                        pe.matmul(ps_p[:, t % 4, :], a_hi, b_lo, start=False, stop=False)
                        mm = pe.matmul(ps_p[:, t % 4, :], a_lo, b_hi, start=False, stop=(d == DT - 1))
                    mm.then_inc(s.made, 1)

            @block.scalar
            def _(act):
                def evacuate(t):
                    act.wait_ge(s.made, t + 1)
                    if t >= 2:
                        act.wait_ge(stores[t % 2], 16 * (t // 2))
                    act.activation(out[:, t % 2, :], ps_p[:, t % 4, :], ACT.Copy).then_inc(s.evacuated, 1)
                    act.wait_ge(s.evacuated, t + 1)
                    act.dma_start(dst(t), out[0:rows, t % 2, :]).then_inc(stores[t % 2], 16)

                def split_hi(j):
                    act.wait_ge(w_in[j], 16 * len(following(j)))
                    act.activation(w.hi[:, nxt, 2 * j:2 * j + 2, :], w.raw[:, 2 * j:2 * j + 2, :], ACT.Copy).then_inc(s.w_hi, 1)

                if keys:
                    load_keys(act, 1)
                todo = list(range(pairs))
                if n <= 2:
                    while todo:
                        split_hi(todo.pop(0))
                for t in range(n):
                    evacuate(t)
                    if t >= 1 and todo:
                        split_hi(todo.pop(0))

            def split_lo(eng, j):
                eng.wait_ge(s.w_hi, j + 1)
                eng.tensor_tensor(w.lo[:, nxt, 2 * j:2 * j + 2, :], w.raw[:, 2 * j:2 * j + 2, :],
                                  w.hi[:, nxt, 2 * j:2 * j + 2, :].bitcast(F32), ALU.subtract)

            def multiply(eng, g):
                part = page_k[:, g % bufs, :, :]
                eng.wait_ge(keys_in[g % bufs], 64 * (g // bufs + 1))
                return eng.tensor_tensor(part, part, q_row[:].unsqueeze(1).to_broadcast([P, 4, FW]), ALU.mult)

            @block.gpsimd
            def _(pool):
                if keys:
                    pool.wait_ge(s.q_in, 16)
                    for g in by_pool:
                        multiply(pool, g).then_inc(s.pool_done, 1)
                    for j in range(pairs):
                        split_lo(pool, j)

            @block.vector
            def _(dve):
                if keys:
                    dve.wait_ge(s.q_in, 16)
                    for g in range(groups):
                        if g in by_pool:
                            dve.wait_ge(s.pool_done, by_pool.index(g) + 1)
                        else:
                            multiply(dve, g).then_inc(s.prod_done, 1)
                            dve.wait_ge(s.prod_done, g + 1 - sum(p < g for p in by_pool))
                        dve.tensor_reduce(keys.scores[:, ds(keys.seq * (PAGES * FH) + g * 4 * FH, 4 * FH)],
                                          page_k[:, g % bufs, :, :].rearrange("p a (h d) -> p (a h) d", d=HD), AX.X, ALU.add).then_inc(s.keys_done, 1)
                else:
                    for j in range(pairs):
                        split_lo(dve, j)


def forget_gates(nc, c, gates, io, scratch, dec):
    T = SEQ + P
    with ExitStack() as ctx:
        sb, psum = alloc(ctx, nc)
        low = sb("low", [P, T])
        soft = sb("soft", [P, T])
        lf = sb("logf", [P, T])
        ones = sb("ones_row", [P, SEQ])
        out = sb("logf_out", [P, NT, FH])
        ps = psum("ps_logf", [P, NT + 1, FH])
        with stage(nc, "low size exp ln lf cum turned out stored") as (block, s):

            @block.vector
            def _(dve):
                dve.memset(ones[0:FH, :], 1.0)
                dve.tensor_scalar(low[0:FH, :], gates[0:FH, :], 0.0, None, ALU.min).then_inc(s.low, 1)
                dve.wait_ge(s.ln, 1)
                dve.wait_ge(s.low, 1)
                dve.tensor_tensor(lf[0:FH, :], low[0:FH, :], soft[0:FH, :], ALU.subtract).then_inc(s.lf, 1)
                dve.wait_ge(s.lf, 1)
                dve.tensor_tensor_scan(low[0:FH, 0:SEQ], ones[0:FH, :], lf[0:FH, 0:SEQ], 0.0, ALU.mult, ALU.subtract).then_inc(s.cum, 1)
                dve.wait_ge(s.turned, 1)
                dve.tensor_copy(out[:], ps[:, 0:NT, :])
                dve.tensor_copy(dec.logf_new[0:DB, :], ps[0:DB, NT, :]).then_inc(s.out, 1)

            @block.scalar
            def _(act):
                act.activation(soft[0:FH, :], gates[0:FH, :], ACT.Abs).then_inc(s.size, 1)
                act.wait_ge(s.size, 1)
                act.activation(soft[0:FH, :], soft[0:FH, :], ACT.Exp, scale=-1.0).then_inc(s.exp, 1)
                act.wait_ge(s.exp, 1)
                act.activation(soft[0:FH, :], soft[0:FH, :], ACT.Ln, bias=1.0).then_inc(s.ln, 1)

            @block.tensor
            def _(pe):
                pe.wait_ge(s.lf, 1)
                for t in range(NT + 1):
                    turned = pe.transpose(ps[:, t, :], lf[0:FH, t * P:(t + 1) * P], c.ident[0:FH, 0:FH])
                turned.then_inc(s.turned, 1)

            @block.sync
            def _(sp):
                sp.wait_ge(s.cum, 1)
                sp.dma_start(scratch.neg_cum, low[0:FH, 0:SEQ]).then_inc(s.stored, 16)
                sp.wait_ge(s.out, 1)
                sp.dma_start(io.new_logf.rearrange("(t p) h -> p t h", p=P), out[:]).then_inc(s.stored, 16)
                sp.dma_start(io.new_logf_s, dec.logf_new[0:DB, :]).then_inc(s.stored, 16)
                sp.wait_ge(s.stored, 48)


def decode_softmax(nc, c, io, scratch, dec, a, head, mem_v):
    G = 2
    NS = DB * FH
    NM = DB * MH
    with ExitStack() as ctx:
        sb, psum = alloc(ctx, nc)
        lfp = sb("page_logf", [P, G, P, FH])
        cum = sb("page_cum", [P, G, P, FH])
        ones = sb("ones_page", [P, P])
        cum_r = sb("row_cum", [P, DB, PAGES, FH])
        rows = sb("new_rows", [P, PW])
        small = sb("small", [P, 8, FH])
        wide = sb("wide", [P, DB, FH])
        mem_k = sb("mem_k", [P, DB, 2, MW])
        mem_q = sb("mem_q", [P, DB, MW])
        mx = sb("maxima", [P, NS + NM])
        top = sb("maxima_all", [P, NS + NM])
        sm = sb("sums", [P, NS + NM])
        total = sb("sums_all", [P, NS + NM])
        ps_t = psum("ps_cum", [P, 4, 4, P])
        ps_o = psum("ps_offset", [P, G, FH])
        ps_c = psum("ps_total", [P, FH])
        names = "first_loaded doubled others_loaded loaded chain scanned offsets totals summed_cum turned row_major maxed all_max shifted weighed summed all_sum"
        with stage(nc, names) as (block, s):

            @block.gpsimd
            def _(pool):
                table = io.cache_logf.rearrange("l n r h -> (l n) (r h)")
                for g in range(G):
                    pool.indirect_dma_start(lfp[:, g, :, :].rearrange("p r h -> p (r h)"), None, table,
                                            bass.IndirectOffsetOnAxis(ap=c.page_index[:, g:g + 1], axis=0)).then_inc(c.gathered, 16)
                pool.memset(a.zeros[:], 0.0)
                pool.wait_ge(s.first_loaded, 48)
                for part in double_parts(NT):
                    double(pool, a, NT, part, s.doubled)
                pool.wait_ge(s.maxed, 1)
                pool.partition_all_reduce(top[:], mx[:], P, RMAX).then_inc(s.all_max, 1)
                pool.wait_ge(s.summed, 1)
                pool.partition_all_reduce(total[:], sm[:], P, RADD).then_inc(s.all_sum, 1)

            @block.sync
            def _(sp):
                sp.dma_start(rows[0:DB, :], scratch.samp).then_inc(s.loaded, 16)
                sp.dma_start(mem_k[:], io.cache_mem_k.rearrange("l b (t p) h d -> p (l b) t (h d)", p=P)).then_inc(s.loaded, 16)
                for b in range(DB):
                    sp.dma_start(mem_q[:, b, :], scratch.samp[b:b + 1, MCOL:MCOL + MW].to_broadcast([P, MW])).then_inc(s.loaded, 16)
                load_head(sp, a, head, NT, s.first_loaded)
                load_decay(sp, a, head, s.others_loaded)
                sp.dma_start(mem_v[:], io.cache_mem_v.rearrange("l b (t p) h d -> p (l b) t (h d)", p=P)).then_inc(s.others_loaded, 16)
                sp.wait_ge(s.others_loaded, 32)

            @block.vector
            def _(dve):
                chain = [0]

                def link(ins):
                    chain[0] += 1
                    ins.then_inc(s.chain, 1)
                    dve.wait_ge(s.chain, chain[0])

                past = dec.scores[:].rearrange("p (b n h) -> p b n h", b=DB, n=PAGES)
                past_h = dec.scores[:].rearrange("p (b n h) -> p b h n", b=DB, n=PAGES)
                mem = dec.mem_scores[:].rearrange("p (b t h) -> p b t h", b=DB, t=2)
                mx_mem = mx[:, NS:].rearrange("p (b h) -> p b h", b=DB)
                own = c.ident[0:DB, 0:DB].unsqueeze(2).to_broadcast([DB, DB, FH])
                own_m = c.ident[0:DB, 0:DB].unsqueeze(2).to_broadcast([DB, DB, MH])

                def on_own(source, mask, heads, out):
                    link(dve.tensor_tensor(wide[0:DB, :, 0:heads], source.rearrange("p (b h) -> p b h", b=DB), mask, ALU.mult))
                    link(dve.tensor_reduce(out, wide[0:DB, :, 0:heads].rearrange("p b h -> p h b"), AX.X, ALU.add))

                link(dve.memset(ones[:], 1.0))
                dve.wait_ge(c.gathered, 16 * G)
                for g in range(G):
                    for h in range(FH):
                        scan = dve.tensor_tensor_scan(cum[:, g, :, h], ones[:], lfp[:, g, :, h], 0.0, ALU.mult, ALU.add)
                scan.then_inc(s.scanned, 1)
                dve.wait_ge(s.scanned, 1)
                dve.wait_ge(s.offsets, 1)
                dve.wait_ge(s.totals, 1)
                for g in range(G):
                    added = dve.tensor_tensor(cum[:, g], cum[:, g], ps_o[:, g, :].unsqueeze(1).to_broadcast([P, P, FH]), ALU.add)
                added.then_inc(s.summed_cum, 1)
                dve.wait_ge(s.loaded, 16 * (2 + DB))
                for b in range(DB):
                    last = dve.tensor_tensor(mem_k[:, b], mem_k[:, b], mem_q[:, b, :].unsqueeze(1).to_broadcast([P, 2, MW]), ALU.mult)
                link(last)
                link(dve.tensor_reduce(dec.mem_scores[:], mem_k[:].rearrange("p b t (h d) -> p (b t h) d", d=HD), AX.X, ALU.add))
                link(dve.tensor_scalar(dec.mem_scores[:], dec.mem_scores[:], SCALE, None, ALU.mult))
                dve.tensor_tensor(mx_mem, mem[:, :, 0, :], mem[:, :, 1, :], ALU.max)
                link(dve.tensor_tensor(rows[0:DB, QCOL:QCOL + FW], rows[0:DB, QCOL:QCOL + FW], rows[0:DB, KCOL:KCOL + FW], ALU.mult))
                dve.tensor_tensor(small[0:DB, 1, :], dec.logf_new[0:DB, :], ps_c[0:DB, :], ALU.add)
                link(dve.tensor_reduce(small[0:DB, 0, :], rows[0:DB, QCOL:QCOL + FW].rearrange("p (h d) -> p h d", d=HD), AX.X, ALU.add))
                dve.tensor_scalar(wide[0:DB], own, 1.0, -NEG, ALU.subtract, ALU.mult)
                link(dve.scalar_tensor_tensor(out=small[0:DB, 2, :], in0=small[0:DB, 0, :], scalar=SCALE, in1=small[0:DB, 1, :],
                                              op0=ALU.mult, op1=ALU.subtract))
                link(dve.tensor_tensor(wide[0:DB], wide[0:DB], small[0:DB, 2, :].unsqueeze(1).to_broadcast([DB, DB, FH]), ALU.add))
                dve.wait_ge(s.row_major, 4)
                link(dve.scalar_tensor_tensor(out=dec.scores[:], in0=dec.scores[:], scalar=SCALE,
                                              in1=cum_r[:].rearrange("p b n h -> p (b n h)"), op0=ALU.mult, op1=ALU.subtract))
                link(dve.tensor_reduce(mx[:, 0:NS], past_h, AX.X, ALU.max))
                dve.tensor_tensor(mx[0:DB, 0:NS], mx[0:DB, 0:NS], wide[0:DB].rearrange("p b h -> p (b h)"), ALU.max).then_inc(s.maxed, 1)
                dve.wait_ge(s.all_max, 1)
                for b in range(DB):
                    dve.tensor_tensor(past[:, b], past[:, b], top[:, b * FH:(b + 1) * FH].unsqueeze(1).to_broadcast([P, PAGES, FH]), ALU.subtract)
                    dve.tensor_tensor(mem[:, b], mem[:, b], top[:, NS + b * MH:NS + (b + 1) * MH].unsqueeze(1).to_broadcast([P, 2, MH]), ALU.subtract)
                on_own(top[0:DB, 0:NS], own, FH, small[0:DB, 3, :])
                dve.tensor_tensor(small[0:DB, 4, :], small[0:DB, 2, :], small[0:DB, 3, :], ALU.subtract).then_inc(s.shifted, 1)
                dve.wait_ge(s.weighed, 3)
                dve.tensor_reduce(sm[:, 0:NS], past_h, AX.X, ALU.add)
                dve.tensor_tensor(sm[:, NS:].rearrange("p (b h) -> p b h", b=DB), mem[:, :, 0, :], mem[:, :, 1, :], ALU.add).then_inc(s.summed, 1)
                dve.wait_ge(s.all_sum, 1)
                on_own(total[0:DB, 0:NS], own, FH, small[0:DB, 6, :])
                link(dve.tensor_tensor(small[0:DB, 6, :], small[0:DB, 6, :], dec.w_new[0:DB, :], ALU.add))
                dve.reciprocal(dec.r_fox[0:DB, :], small[0:DB, 6, :])
                on_own(total[0:DB, NS:], own_m, MH, small[0:DB, 7, 0:MH])
                dve.reciprocal(dec.r_mem[0:DB, :], small[0:DB, 7, 0:MH])

            @block.tensor
            def _(pe):
                pe.wait_ge(s.scanned, 1)
                for g in range(G):
                    mm = pe.matmul(ps_o[:, g, :], c.page_before[:], cum[:, g, P - 1, :], start=True, stop=True)
                mm.then_inc(s.offsets, 1)
                for g in range(G):
                    mm = pe.matmul(ps_c[0:DB, :], c.seq_of_page[:, g, :], cum[:, g, P - 1, :], start=(g == 0), stop=(g == 1))
                mm.then_inc(s.totals, 1)
                pe.wait_ge(s.summed_cum, 1)
                for k in range(4):
                    for j in range(4):
                        turned = pe.transpose(ps_t[:, k, j, :], cum[:, k // 2, :, 4 * (k % 2) + j], c.ident[:])
                    turned.then_inc(s.turned, 1)

            @block.scalar
            def _(act):
                for k in range(4):
                    act.wait_ge(s.turned, k + 1)
                    b0, h0 = 4 * (k // 2), 4 * (k % 2)
                    act.activation(cum_r[:, b0:b0 + 4, :, h0:h0 + 4].rearrange("p b n h -> p (b n) h"),
                                   ps_t[:, k, :, :].rearrange("p h m -> p m h"), ACT.Copy).then_inc(s.row_major, 1)
                act.wait_ge(s.shifted, 1)
                act.activation(dec.scores[:], dec.scores[:], ACT.Exp).then_inc(s.weighed, 1)
                act.activation(dec.mem_scores[:], dec.mem_scores[:], ACT.Exp).then_inc(s.weighed, 1)
                act.activation(dec.w_new[0:DB, :], small[0:DB, 4, :], ACT.Exp).then_inc(s.weighed, 1)


def decode_memory_values(nc, c, dec, mem_v, out):
    with ExitStack() as ctx:
        sb, psum = alloc(ctx, nc)
        own = sb("own_rows", [P, DB, MW])
        pick = sb("pick", [P, DB, DB])
        ps_m = psum("ps_m", [P, DB, MW])
        ps_s = psum("ps_s", [P, MW])
        with stage(nc, "picked zeroed made masked summed") as (block, s):

            @block.gpsimd
            def _(pool):
                pool.memset(pick[0:MH], 0.0).then_inc(s.zeroed, 1)
                pool.wait_ge(s.zeroed, 1)
                for b in range(DB):
                    pool.memset(pick[0:MH, b, b:b + 1], 1.0).then_inc(s.picked, 1)

            @block.tensor
            def _(pe):
                for b in range(DB):
                    for t in range(2):
                        mm = pe.matmul(ps_m[0:MH, b, :], dec.mem_scores[:, (2 * b + t) * MH:(2 * b + t + 1) * MH], mem_v[:, b, t, :],
                                       start=(t == 0), stop=(t == 1))
                mm.then_inc(s.made, 1)
                pe.wait_ge(s.picked, DB)
                pe.wait_ge(s.masked, 1)
                for b in range(DB):
                    mm = pe.matmul(ps_s[0:DB, :], pick[0:MH, b, :], own[0:MH, b, :], start=(b == 0), stop=(b == DB - 1))
                mm.then_inc(s.summed, 1)

            @block.vector
            def _(dve):
                dve.wait_ge(s.made, 1)
                dve.tensor_tensor(own[0:MH], ps_m[0:MH], c.own_head[0:MH, 0:MW].unsqueeze(1).to_broadcast([MH, DB, MW]), ALU.mult).then_inc(s.masked, 1)
                dve.wait_ge(s.summed, 1)
                dve.tensor_tensor(out[0:DB, :].rearrange("p (h d) -> p h d", d=HD), ps_s[0:DB, :].rearrange("p (h d) -> p h d", d=HD),
                                  dec.r_mem[0:DB, :].unsqueeze(2).to_broadcast([DB, MH, HD]), ALU.mult)


def load_head(eng, a, head, nk, sem):
    eng.dma_start(a.q[:, :, 0, :], head.q.rearrange("(t p) d -> p t d", p=P)).then_inc(sem, 16)
    eng.dma_start(a.k[:, 0:nk, 0, :], head.k.rearrange("(t p) d -> p t d", p=P)).then_inc(sem, 16)
    eng.dma_start(a.v[:, 0:nk, :], head.v.rearrange("(t p) d -> p t d", p=P)).then_inc(sem, 16)


def load_decay(eng, a, head, sem):
    if head.neg_cum is not None:
        eng.dma_start(a.neg_cum[:], head.neg_cum.to_broadcast([P, SEQ])).then_inc(sem, 16)


def double_parts(nk):
    return [(what, j) for j in range(NT // 4) for what in "kq" if what == "q" or 4 * j < nk]


def double(pool, a, nk, part, doubled):
    what, j = part
    raw, end = (a.k, min(4 * j + 4, nk)) if what == "k" else (a.q, 4 * j + 4)
    pool.tensor_copy(raw[:, 4 * j:end, 1, :], raw[:, 4 * j:end, 0, :]).then_inc(doubled, 1)


def attention_order(nk, causal, pages, opening):
    chunks = NT // QCH
    n_k = (nk + 3) // 4
    steps = [(ch, j) for ch in range(chunks) for j in range(QCH * (ch + 1) if causal else nk)]
    ins = [(what, j) for j in range(NT // 4) for what in "kq" if what == "q" or j < n_k]
    n_lead = 4 if causal else 3
    order, pending = [], []
    left = [pages]

    def score(following, i):
        w = (i + 1) * P if causal else nk * P
        return [("score", following, i, m, p0, min(w, p0 + 1024), p0 + 1024 >= w) for m, p0 in enumerate(range(0, w, 1024))]

    def past(count):
        for _ in range(min(count, left[0])):
            left[0] -= 1
            order.append(("page",))

    def slot(items, page=False, value=()):
        order.extend(items)
        past(1 if page else 0)
        order.extend(value)
        order.extend(("exp", i) for i in pending)
        pending[:] = [e[2] for e in items if e[0] == "score" and e[6]]

    lead = [[("in", True) + one] for one in ins[:n_lead]]
    lead += [score(True, i) + score(True, i + 1) for i in range(0, QCH, 2)]
    if opening:
        for items in lead + [[]]:
            slot(items)
        return order
    ins = [("in", False) + one for one in ins[n_lead:]]
    rows = [score(False, i) for i in range(NT)]

    def turn(n):
        ch, j = steps[n]
        if j == 0:
            order.extend(("exp", i) for i in pending if i < QCH * (ch + 1))
            pending[:] = [i for i in pending if i >= QCH * (ch + 1)]
        return ("turn", n, ch, j)

    slot([turn(0), ("split_v",)] + rows[QCH])
    slot(rows[QCH + 1], page=True)
    done = QCH + 2
    folding = None
    for ch in range(chunks):
        own = [n for n, (c, _) in enumerate(steps) if c == ch]
        ahead = min(NT, QCH * (ch + (2 if causal else 3)))
        todo = [piece for row in rows[done:ahead] for piece in row]
        total, done = len(todo), max(done, ahead)
        span = max(2, len(own) // 2) if causal else len(own)
        for j, n in enumerate(own):
            items = []
            if n + 1 < len(steps):
                items.append(turn(n + 1))
            if ins:
                items.append(ins.pop(0))
            while todo and total - len(todo) < -(-total * (j + 1) // span):
                items.append(todo.pop(0))
            if ch == chunks - 1 and lead and (not causal or (j >= 2 and j % 2 == 0)):
                items.extend(lead.pop(0))
            slot(items, page=ch in (0, chunks - 1) or j % 2 == 0 or (ch, j) in ((1, 7), (2, 11)), value=[("value", n, ch, j)])
            if j == 0 and folding is not None:
                order.append(("fold", folding))
            if j == 1 and folding is not None:
                order.append(("store", folding))
            if ch == 1 and j == 0:
                order.append(("load_head",))
            if ch == chunks - 1 and j == 0:
                order.append(("load_decay",))
        order.append(("copy", ch))
        folding = ch
    if pages:
        past(left[0])
        order.append(("row",))
    for items in lead:
        slot(items)
    order.append(("fold", folding))
    slot([])
    order.append(("store", folding))
    return order


def attend(nc, c, a, nk, causal, following, dst, values=None, opening=False):
    chunks = NT // QCH
    n_k = (nk + 3) // 4
    order = attention_order(nk, causal, PAGES if values else 0, opening)
    own_turns = sum(e[0] == "in" and not e[1] for e in order)

    def first_row(ch, j):
        return max(0, j - QCH * ch) if causal else 0

    def last_key(ch):
        return (QCH * (ch + 1) if causal else nk) - 1

    def probs(ch, r, p0, p1):
        at = 0 if causal else (ch // 2) * nk * P
        return a.probs[:, ch % 2, r, at + p0:at + p1]

    def turned_in(following, i):
        turns = [e[1:] for e in order if e[0] == "in"]
        groups = [("q", i // 4)] + [("k", j) for j in range(min(n_k, i // 4 + 1))]
        return max([u + 1 for u, turn in enumerate(turns) if turn in [(following,) + g for g in groups]] or [0])

    def steps_through(ch):
        return sum(last_key(k) + 1 for k in range(ch + 1))

    with ExitStack() as ctx:
        sb, psum = alloc(ctx, nc)
        ps_s = psum("ps_scores", [P, 2, 1024])
        ps_t = psum("ps_turned", [P, 2, BLK])
        ps_o = psum("ps_out", [P, BLK])
        if values:
            ps_v = psum("ps_values", [P, FW])
        names = ("doubled turned hi lo v_hi v_lo scored min1 min2 probs t_turned t_hi t_split pv o_copied o_ready inverted o_out "
                 "stored loaded decay w_hi w_lo v0 v1 v2 v3 page_hi page_lo v_used v_masked v_row v_row_out")
        with stage(nc, names) as (block, s):
            v_in = (s.v0, s.v1, s.v2, s.v3)
            if values:
                w_pages = a.w_st[:, 0:PAGES * 2 * FH].rearrange("p (n h) -> p n h", n=PAGES)
                all_weights = values.all_weights.rearrange("p (n h) -> p n h", n=PAGES)

            @block.sync
            def _(sp):
                if values:
                    for n in range(PAGES):
                        if n >= 4:
                            sp.wait_ge(s.page_lo, n - 3)
                        page = sp.value_load(c.pages[0:1, ds(values.seq * PAGES + n, 1)], min_val=0, max_val=values.last_page)
                        sp.dma_start(values.page_v[:, n % 4, :], values.cache[ds(page, 1)].rearrange("n r c -> (n r) c")).then_inc(v_in[n % 4], 16)
                    sp.wait_ge(s.v_row_out, 1)
                    sp.dma_start(values.dst, values.row[0:1, :]).then_inc(s.stored, 16)
                if not opening:
                    sp.wait_ge(s.stored, 16 * (chunks + (1 if values else 0)))

            @block.gpsimd
            def _(pool):
                if opening:
                    pool.memset(a.w_st[:, PAGES * 2 * FH:].bitcast(F32), 0.0)
                parts = [] if opening else double_parts(nk)
                for n in range(PAGES if values else 0):
                    if n == DOUBLE_FROM:
                        pool.wait_ge(s.loaded, 48)
                    if n >= DOUBLE_FROM and parts:
                        double(pool, a, nk, parts.pop(0), s.doubled)
                    pool.wait_ge(s.page_hi, n + 1)
                    pool.tensor_tensor(values.page_lo[:, n % 3, :], values.page_v[:, n % 4, :], values.page_hi[:, n % 3, :].bitcast(F32),
                                       ALU.subtract).then_inc(s.page_lo, 1)
                if parts:
                    pool.wait_ge(s.loaded, 48)
                for part in parts:
                    double(pool, a, nk, part, s.doubled)

            @block.tensor
            def _(pe):
                st = Steps()

                def take_bank():
                    if len(st.uses) >= 2:
                        pe.wait_ge(*st.uses[-2])
                    return ps_t[:, len(st.uses) % 2, :]

                for what, *at in order:
                    if what == "in":
                        ahead, side, j = at
                        bank = take_bank()
                        raw = a.k if side == "k" else a.q
                        if ahead and not opening:
                            pe.wait_ge(s.doubled, double_parts(nk).index((side, j)) + 1)
                        for t in range(4 * j, min(4 * j + 4, nk if side == "k" else NT)):
                            turned = pe.transpose(bank[:, (t - 4 * j) * P:(t - 4 * j + 1) * P],
                                                  raw[:, t, :, :].rearrange("p a d -> p (a d)"), c.ident[:])
                        turned.then_inc(s.turned, 1)
                        st.turned += 1
                        st.uses.append((s.lo, st.turned))
                    elif what == "score":
                        ahead, i, m, p0, p1, _ = at
                        if m == 0 and turned_in(ahead, i):
                            pe.wait_ge(s.lo, turned_in(ahead, i))
                        if st.score >= 2:
                            pe.wait_ge(s.min1, st.score - 1)
                        bank = ps_s[:, st.score % 2, :]
                        for b0 in range(p0, p1, BLK):
                            b1 = min(b0 + BLK, p1)
                            out = bank[:, b0 - p0:b1 - p0]
                            diag = causal and b1 == (i + 1) * P
                            pe.matmul(out, a.q_hi[:, i * P:(i + 1) * P], a.k_st[:, b0:b1], start=True, stop=False)
                            mm = pe.matmul(out, a.q_lo[:, i * P:(i + 1) * P], a.k_st[:, b0:b1], start=False, stop=not diag)
                            if diag:
                                mm = pe.matmul(bank[:, b1 - P - p0:b1 - p0], c.ident_r[:], c.causal_r[:], start=False, stop=True)
                        mm.then_inc(s.scored, 1)
                        st.score += 1
                    elif what == "turn":
                        n, ch, j = at
                        if j == 0 and ch >= 1:
                            pe.wait_ge(s.probs, QCH * ch)
                        bank = take_bank()
                        for r in range(first_row(ch, j), QCH):
                            turned = pe.transpose(bank[:, r * P:(r + 1) * P], probs(ch, r, j * P, (j + 1) * P), c.ident[:])
                        turned.then_inc(s.t_turned, 1)
                        st.uses.append((s.t_split, n + 1))
                    elif what == "value":
                        n, ch, j = at
                        r0 = first_row(ch, j)
                        if n == 0:
                            pe.wait_ge(s.v_lo, 1)
                        if j == 0 and ch >= 1:
                            pe.wait_ge(s.o_copied, ch)
                        out = ps_o[:, r0 * P:]
                        pe.wait_ge(s.t_split, n + 1)
                        pe.matmul(out, a.v_st[:, j, :], a.p_hi[:, n % 2, r0 * P:], start=(j == 0), stop=False)
                        pe.matmul(out, a.v_st[:, j, :], a.p_lo[:, n % 2, r0 * P:], start=False, stop=(j == last_key(ch))).then_inc(s.pv, 1)
                    elif what == "fold":
                        ch, = at
                        pe.wait_ge(s.o_copied, ch + 1)
                        bank = take_bank()
                        for r in range(QCH):
                            mm = pe.matmul(bank[:, r * HD:(r + 1) * HD], a.o_t[:, ch % 2, r * P:(r + 1) * P], c.fold[:], start=True, stop=True)
                        mm.then_inc(s.o_ready, 1)
                        st.uses.append((s.o_out, ch + 1))
                    elif what == "page":
                        n = st.page
                        if n == 0:
                            pe.wait_ge(s.w_lo, 1)
                        pe.wait_ge(s.page_lo, n + 1)
                        page_w = a.w_st[:, n * 2 * FH:n * 2 * FH + P]
                        pe.matmul(ps_v[:], page_w, values.page_hi[:, n % 3, :], start=(n == 0), stop=False)
                        pe.matmul(ps_v[:], page_w, values.page_lo[:, n % 3, :], start=False, stop=(n == PAGES - 1)).then_inc(s.v_used, 1)
                        st.page += 1
                    elif what == "row":
                        bank = take_bank()
                        pe.wait_ge(s.v_masked, 1)
                        pe.matmul(bank[0:1, :], c.ones[0:2 * FH, :], values.own[0:2 * FH, :], start=True, stop=True).then_inc(s.v_row, 1)
                        st.uses.append((s.v_row_out, 1))

            @block.scalar
            def _(act):
                st = Steps()

                def page_hi(n):
                    if n < PAGES:
                        act.wait_ge(v_in[n % 4], 16 * (n // 4 + 1))
                        if n >= 3:
                            act.wait_ge(s.v_used, n - 2)
                        act.activation(values.page_hi[:, n % 3, :], values.page_v[:, n % 4, :], ACT.Copy).then_inc(s.page_hi, 1)

                if values:
                    act.activation(w_pages[:, :, 0:FH], all_weights, ACT.Copy).then_inc(s.w_hi, 1)
                    page_hi(0)
                    page_hi(1)
                for what, *at in order:
                    if what == "page":
                        page_hi(st.page + 2)
                        st.page += 1
                    elif what == "in":
                        _, side, j = at
                        act.wait_ge(s.turned, st.turned + 1)
                        if side == "k":
                            w = min(BLK, nk * P - j * BLK)
                            act.activation(a.k_st[:, j * BLK:j * BLK + w], ps_t[:, st.bank % 2, 0:w], ACT.Copy).then_inc(s.hi, 1)
                        else:
                            act.activation(a.q_hi[:, j * BLK:(j + 1) * BLK], ps_t[:, st.bank % 2, :], ACT.Copy, scale=SCALE).then_inc(s.hi, 1)
                        st.turned += 1
                        st.bank += 1
                    elif what == "split_v":
                        act.activation(a.v_st[:, 0:nk, 0:HD], a.v[:, 0:nk, :], ACT.Copy).then_inc(s.v_hi, 1)
                    elif what == "exp":
                        i, = at
                        w = (i + 1) * P if causal else nk * P
                        n_pieces = -(-w // 1024)
                        st.scored += n_pieces
                        if n_pieces == 1:
                            act.wait_ge(s.min1, st.scored)
                        else:
                            st.joined += 1
                            act.wait_ge(s.min2, st.joined)
                        part = probs(i // QCH, i % QCH, 0, w)
                        act.activation(part, part, ACT.Exp, scale=-1.0, bias=a.low[:, i:i + 1], accum_out=a.sums[:, i:i + 1]).then_inc(s.probs, 1)
                    elif what == "turn":
                        n, ch, j = at
                        r0 = first_row(ch, j)
                        act.wait_ge(s.t_turned, n + 1)
                        if n >= 2:
                            act.wait_ge(s.pv, n - 1)
                        act.activation(a.p_hi[:, n % 2, r0 * P:], ps_t[:, st.bank % 2, r0 * P:], ACT.Copy).then_inc(s.t_hi, 1)
                        st.bank += 1
                    elif what == "copy":
                        ch, = at
                        act.wait_ge(s.pv, steps_through(ch))
                        if ch >= 2:
                            act.wait_ge(s.o_ready, ch - 1)
                        act.activation(a.o_t[:, ch % 2, :], ps_o[:], ACT.Copy).then_inc(s.o_copied, 1)
                    elif what == "fold":
                        st.bank += 1
                    elif what == "store":
                        ch, = at
                        act.wait_ge(s.o_out, ch + 1)
                        act.dma_start(dst(ch), a.o_out[:, ch, :, :]).then_inc(s.stored, 16)
                    elif what == "load_head":
                        act.wait_ge(s.turned, own_turns)
                        act.wait_ge(s.v_lo, 1)
                        load_head(act, a, following, nk, s.loaded)
                    elif what == "load_decay":
                        load_decay(act, a, following, s.decay)
                    elif what == "row":
                        act.wait_ge(s.v_row, 1)
                        act.activation(values.row[0:1, :], ps_t[0:1, st.bank % 2, :], ACT.Copy).then_inc(s.v_row_out, 1)
                        st.bank += 1

            @block.vector
            def _(dve):
                st = Steps()

                if values:
                    dve.wait_ge(s.w_hi, 1)
                    dve.tensor_tensor(w_pages[:, :, FH:], all_weights, w_pages[:, :, 0:FH].bitcast(F32), ALU.subtract).then_inc(s.w_lo, 1)
                for what, *at in order:
                    if what == "in":
                        _, side, j = at
                        dve.wait_ge(s.hi, st.turned + 1)
                        if side == "k":
                            w = min(BLK, nk * P - j * BLK)
                            upper = a.k_st[HD:P, j * BLK:j * BLK + w]
                            dve.tensor_tensor(upper, ps_t[HD:P, st.bank % 2, 0:w], upper.bitcast(F32), ALU.subtract).then_inc(s.lo, 1)
                        else:
                            cols = slice(j * BLK, (j + 1) * BLK)
                            dve.scalar_tensor_tensor(out=a.q_lo[:, cols], in0=ps_t[:, st.bank % 2, :], scalar=SCALE, in1=a.q_hi[:, cols].bitcast(F32),
                                                     op0=ALU.mult, op1=ALU.subtract).then_inc(s.lo, 1)
                        st.turned += 1
                        st.bank += 1
                    elif what == "split_v":
                        dve.wait_ge(s.v_hi, 1)
                        dve.tensor_tensor(a.v_st[:, 0:nk, HD:P], a.v[:, 0:nk, :], a.v_st[:, 0:nk, 0:HD].bitcast(F32), ALU.subtract).then_inc(s.v_lo, 1)
                    elif what == "score":
                        ahead, i, m, p0, p1, complete = at
                        ch, r = i // QCH, i % QCH
                        if ahead and i == 0 and not opening:
                            dve.wait_ge(s.t_turned, steps_through(chunks - 2 if causal else 0))
                            if causal:
                                dve.wait_ge(s.decay, 16)
                        if causal and not ahead and r == 0 and m == 0 and ch >= 2:
                            dve.wait_ge(s.t_turned, steps_through(ch - 2))
                        dve.wait_ge(s.scored, st.score + 1)
                        part = a.low[:, i:i + 1] if complete and m == 0 else a.low2[:, m, i:i + 1]
                        bias = a.neg_cum[:, p0:p1] if causal else a.zeros[:, 0:p1 - p0]
                        dve.tensor_tensor_reduce(probs(ch, r, p0, p1), ps_s[:, st.score % 2, 0:p1 - p0], bias, -1.0, BIG, ALU.add, ALU.min,
                                                 part).then_inc(s.min1, 1)
                        st.score += 1
                        if complete and m == 1:
                            dve.wait_ge(s.min1, st.score)
                            dve.tensor_tensor(a.low[:, i:i + 1], a.low2[:, 0, i:i + 1], a.low2[:, 1, i:i + 1], ALU.min).then_inc(s.min2, 1)
                    elif what == "turn":
                        n, ch, j = at
                        r0 = first_row(ch, j)
                        dve.wait_ge(s.t_hi, n + 1)
                        dve.tensor_tensor(a.p_lo[:, n % 2, r0 * P:], ps_t[:, st.bank % 2, r0 * P:], a.p_hi[:, n % 2, r0 * P:].bitcast(F32),
                                          ALU.subtract).then_inc(s.t_split, 1)
                        st.bank += 1
                    elif what == "fold":
                        ch, = at
                        part = slice(QCH * ch, QCH * ch + QCH)
                        dve.reciprocal(a.inv[:, part], a.sums[:, part]).then_inc(s.inverted, 1)
                        dve.wait_ge(s.inverted, ch + 1)
                        dve.wait_ge(s.o_ready, ch + 1)
                        dve.tensor_tensor(a.o_out[:, ch, :, :], ps_t[:, st.bank % 2, 0:QCH * HD].rearrange("p (r d) -> p r d", d=HD),
                                          a.inv[:, part].unsqueeze(2).to_broadcast([P, QCH, HD]), ALU.mult).then_inc(s.o_out, 1)
                        st.bank += 1
                    elif what == "row":
                        dve.wait_ge(s.v_used, PAGES)
                        dve.tensor_tensor(values.own[0:2 * FH, :], ps_v[0:2 * FH, :], c.own_head[0:2 * FH, :], ALU.mult).then_inc(s.v_masked, 1)
                        st.bank += 1


def mix(nc, c, n, w, gain, assemble, x_src, dst, rows=P):
    with ExitStack() as ctx:
        sb, psum = alloc(ctx, nc)
        y = sb("y", [P, min(n, SLOTS), D])
        yn = sb("y_normed", [P, D])
        y_hi = sb("y_hi", [P, 2, DT, P], F32R)
        y_lo = sb("y_lo", [P, 2, DT, P], F32R)
        x = sb("x_res", [P, min(n, SLOTS), D])
        junk = sb("squares", [P, D])
        ss = sb("sum_squares", [P, n, 3])
        rstd = sb("rstd", [P, n, 3])
        ps_t = psum("ps_transposed", [P, 2, BLK])
        ps_y = psum("ps_y", [P, 2, D])
        groups = [(0, CW), (CW, FW), (CW + FW, MW)]
        with stage(nc, "fox0 fox1 fox2 fox3 parts0 parts1 parts2 parts3 xin0 xin1 xin2 xin3 conv conv_step squared var rstd normed turned hi_done lo_done made res store0 store1 store2 store3") as (block, s):
            parts = (s.parts0, s.parts1, s.parts2, s.parts3)
            fox = (s.fox0, s.fox1, s.fox2, s.fox3)
            xin = (s.xin0, s.xin1, s.xin2, s.xin3)
            stores = (s.store0, s.store1, s.store2, s.store3)

            @block.sync
            def _(sp):
                for k in range(n + SLOTS - 1):
                    if k < n:
                        assemble.load(sp, s, k, y, parts[k % SLOTS], fox[k % SLOTS])
                        if k >= SLOTS:
                            sp.wait_ge(stores[k % SLOTS], 16 * (k // SLOTS))
                        sp.dma_start(x[0:rows, k % SLOTS, :], x_src(k)).then_inc(xin[k % SLOTS], 16)
                    done = k - (SLOTS - 1)
                    if done >= 0:
                        sp.wait_ge(s.res, done + 1)
                        sp.dma_start(dst(done), x[0:rows, done % SLOTS, :]).then_inc(stores[done % SLOTS], 16)
                for k in range(min(n, SLOTS)):
                    sp.wait_ge(stores[k], 16 * ((n - k + SLOTS - 1) // SLOTS))

            @block.gpsimd
            def _(pool):
                for k in range(n):
                    assemble.conv(pool, s, k, y, parts[k % SLOTS])
                    pool.wait_ge(s.squared, k + 1)
                    for m, (g0, gw) in enumerate(groups):
                        scaled = pool.tensor_scalar(rstd[:, k, m:m + 1], ss[:, k, m:m + 1], 1.0 / gw, EPS, ALU.mult, ALU.add)
                    scaled.then_inc(s.var, 1)
                    pool.wait_ge(s.var, k + 1)
                    pool.tensor_tensor(rstd[:, k, :], rstd[:, k, :], c.minus_half[:].to_broadcast([P, 3]), ALU.pow).then_inc(s.rstd, 1)

            @block.scalar
            def _(act):
                def square(k):
                    act.wait_ge(s.conv, k + 1)
                    assemble.ready(act, s, k, fox[k % SLOTS])
                    if k >= 1:
                        act.wait_ge(s.squared, k)
                    for m, (g0, gw) in enumerate(groups):
                        done = act.activation(junk[:, g0:g0 + gw], y[:, k % SLOTS, g0:g0 + gw], ACT.Square, accum_out=ss[:, k, m:m + 1])
                    done.then_inc(s.squared, 1)

                square(0)
                for k in range(n):
                    for j in range(2):
                        u = 2 * k + j
                        act.wait_ge(s.turned, u + 1)
                        if k >= 2:
                            act.wait_ge(s.made, k - 1)
                        act.activation(y_hi[:, k % 2, 4 * j:4 * j + 4, :], ps_t[:, j, :].rearrange("p (d t) -> p d t", d=4), ACT.Copy).then_inc(s.hi_done, 1)
                    if k + 1 < n:
                        square(k + 1)

            @block.vector
            def _(dve):
                def normalise(k):
                    dve.wait_ge(s.rstd, k + 1)
                    if k >= 1:
                        dve.wait_ge(s.turned, 2 * k)
                    for m, (g0, gw) in enumerate(groups):
                        done = dve.scalar_tensor_tensor(out=yn[:, g0:g0 + gw], in0=y[:, k % SLOTS, g0:g0 + gw], scalar=rstd[:, k, m:m + 1],
                                                        in1=gain[:, g0:g0 + gw], op0=ALU.mult, op1=ALU.mult)
                    done.then_inc(s.normed, 1)

                def split(k):
                    for j in range(2):
                        u = 2 * k + j
                        dve.wait_ge(s.hi_done, u + 1)
                        dve.tensor_tensor(y_lo[:, k % 2, 4 * j:4 * j + 4, :], ps_t[:, j, :].rearrange("p (d t) -> p d t", d=4),
                                          y_hi[:, k % 2, 4 * j:4 * j + 4, :].bitcast(F32), ALU.subtract).then_inc(s.lo_done, 1)

                def residual(k):
                    dve.wait_ge(s.made, k + 1)
                    dve.wait_ge(xin[k % SLOTS], 16 * (k // SLOTS + 1))
                    dve.tensor_tensor(x[0:rows, k % SLOTS, :], ps_y[0:rows, k % 2, :], x[0:rows, k % SLOTS, :], ALU.add).then_inc(s.res, 1)

                normalise(0)
                for k in range(n):
                    split(k)
                    if k + 1 < n:
                        normalise(k + 1)
                    if k >= 1:
                        residual(k - 1)
                residual(n - 1)

            @block.tensor
            def _(pe):
                def turn(k):
                    pe.wait_ge(s.normed, k + 1)
                    for j in range(2):
                        if k >= 1:
                            pe.wait_ge(s.lo_done, 2 * k - 1 + j)
                        for d in range(4):
                            turned = pe.transpose(ps_t[:, j, d * P:(d + 1) * P], yn[:, (4 * j + d) * P:(4 * j + d + 1) * P], c.ident[:])
                        turned.then_inc(s.turned, 1)

                turn(0)
                for k in range(n):
                    pe.wait_ge(s.lo_done, 2 * k + 2)
                    if k >= 2:
                        pe.wait_ge(s.res, k - 1)
                    for e in range(2):
                        if e == 1 and k + 1 < n:
                            turn(k + 1)
                        for d in range(DT):
                            out = ps_y[:, k % 2, e * BLK:(e + 1) * BLK]
                            cols = slice(e * BLK, (e + 1) * BLK)
                            pe.matmul(out, y_hi[:, k % 2, d, :], w.hi[:, d, cols], start=(d == 0), stop=False)
                            pe.matmul(out, y_hi[:, k % 2, d, :], w.lo[:, d, cols], start=False, stop=False)
                            mm = pe.matmul(out, y_lo[:, k % 2, d, :], w.hi[:, d, cols], start=False, stop=(d == DT - 1))
                    mm.then_inc(s.made, 1)


def weight_source(io, i):
    if i >= 2 * FT:
        return io.w_down[(i - 2 * FT) * P:(i - 2 * FT + 1) * P, :]
    table = io.w_up if i % 2 else io.w_gate
    return table.rearrange("(d p) n -> p d n", p=P)[:, :, (i // 2) * P:(i // 2 + 1) * P]


def weight_slot(w, i):
    slot = w.raw[:, i % RING, :]
    return slot if i >= 2 * FT else slot.rearrange("p (d n) -> p d n", d=DT)


def ffn(nc, c, n, b, w, ps, io, before=None, following=None):
    T = n * P
    splits = ITEMS if following else ITEMS - AHEAD
    def squared_at(k):
        return 3 + 5 * k

    def turned_at(k, j):
        return squared_at(k) + 2 + j

    names = ("w_in0 w_in1 w_in2 w_hi w_lo w_used silu_done prod_done a_hi a_lo res squared var rstd normed stored "
             "n_loaded0 n_loaded1 n_loaded2 n_squared n_var n_rstd n_normed n_turned n_hi n_lo")
    with stage(nc, names) as (block, s):
        w_in = (s.w_in0, s.w_in1, s.w_in2)
        n_loaded = (s.n_loaded0, s.n_loaded1, s.n_loaded2)

        @block.sync
        def _(sp):
            for k in range(splits):
                i = (k + AHEAD) % ITEMS
                if before and k == 12:
                    for t in range(before.n):
                        sp.wait_ge(s.normed, t + 1)
                        sp.dma_start(before.dst(t), before.x[:, t, :]).then_inc(s.stored, 16)
                if following and k == 2 * FT:
                    if before:
                        sp.wait_ge(s.stored, 16 * before.n)
                    for t in range(following.n):
                        sp.dma_start(following.x[0:following.rows(t), t, :], following.src(t)).then_inc(n_loaded[t], 16)
                if k >= RING:
                    sp.wait_ge(s.w_lo, k - RING + 1)
                sp.dma_start(weight_slot(w, i), weight_source(io, i)).then_inc(w_in[(k + AHEAD) % RING], 16)
            if before and not following:
                sp.wait_ge(s.stored, 16 * before.n)

        @block.gpsimd
        def _(pool):
            if before:
                for k in range(before.n):
                    pool.wait_ge(s.squared, k + 1)
                    pool.tensor_scalar(b.rstd[:, k:k + 1], b.ss[:, k:k + 1], 1.0 / D, EPS, ALU.mult, ALU.add).then_inc(s.var, 1)
                    pool.wait_ge(s.var, k + 1)
                    pool.tensor_tensor(b.rstd[:, k:k + 1], b.rstd[:, k:k + 1], c.minus_half[:], ALU.pow).then_inc(s.rstd, 1)
            if following:
                for k in range(following.n):
                    pool.wait_ge(s.n_squared, k + 1)
                    pool.tensor_scalar(b.n_rstd[:, k:k + 1], b.n_ss[:, k:k + 1], 1.0 / D, EPS, ALU.mult, ALU.add).then_inc(s.n_var, 1)
                    pool.wait_ge(s.n_var, k + 1)
                    pool.tensor_tensor(b.n_rstd[:, k:k + 1], b.n_rstd[:, k:k + 1], c.minus_half[:], ALU.pow).then_inc(s.n_rstd, 1)

        @block.scalar
        def _(act):
            def split_hi(k):
                if k >= splits:
                    return
                i = k + AHEAD
                act.wait_ge(w_in[i % RING], 16 * (k // RING + 1))
                if i >= RING:
                    act.wait_ge(s.w_used, i - RING + 1)
                act.activation(w.hi[:, i % RING, :], w.raw[:, i % RING, :], ACT.Copy).then_inc(s.w_hi, 1)

            for f in range(FT):
                split_hi(2 * f)
                act.wait_ge(s.w_used, 2 * f + 1)
                if f >= 2:
                    act.wait_ge(s.prod_done, f - 1)
                act.activation(b.sil[:, f % 2, 0:T], ps[:, gate_bank(f), 0:T], ACT.Silu).then_inc(s.silu_done, 1)
                split_hi(2 * f + 1)
                act.wait_ge(s.prod_done, f + 1)
                act.activation(b.act_hi[:, f, 0:T], b.prod[:, 0:T], ACT.Copy).then_inc(s.a_hi, 1)
                if before and 1 <= f <= before.n:
                    act.wait_ge(s.res, before.n)
                    if f > 1:
                        act.wait_ge(s.squared, f - 1)
                    act.activation(b.xn[:, 0, :], before.x[:, f - 1, :], ACT.Square, accum_out=b.ss[:, f - 1:f]).then_inc(s.squared, 1)
            for f in range(FT):
                split_hi(2 * FT + f)
                if following:
                    for k in range(following.n):
                        if f == squared_at(k):
                            act.wait_ge(n_loaded[k], 16)
                            if k >= 2:
                                act.wait_ge(s.n_turned, 2 * (k - 1))
                            act.activation(b.xn[:, k % 2, :], following.x[:, k, :], ACT.Square, accum_out=b.n_ss[:, k:k + 1]).then_inc(s.n_squared, 1)
                        for j in range(2):
                            if f == turned_at(k, j):
                                act.wait_ge(s.n_turned, 2 * k + j + 1)
                                act.activation(b.h_hi[:, 4 * j:4 * j + 4, k * P:(k + 1) * P], ps[:, 6 + j, :].rearrange("p (d t) -> p d t", d=4),
                                               ACT.Copy).then_inc(s.n_hi, 1)

        @block.vector
        def _(dve):
            def split_lo(k):
                if k >= splits:
                    return
                i = k + AHEAD
                dve.wait_ge(s.w_hi, k + 1)
                dve.tensor_tensor(w.lo[:, i % RING, :], w.raw[:, i % RING, :], w.hi[:, i % RING, :].bitcast(F32), ALU.subtract).then_inc(s.w_lo, 1)

            if before:
                for k in (2, 0, 1):
                    dve.tensor_tensor(before.x[:, k, :], ps[:, 2 * k:2 * k + 2, :].rearrange("p a n -> p (a n)"), before.x[:, k, :],
                                      ALU.add).then_inc(s.res, 1)
            for f in range(FT):
                split_lo(2 * f)
                split_lo(2 * f + 1)
                dve.wait_ge(s.silu_done, f + 1)
                dve.wait_ge(s.w_used, 2 * f + 2)
                if f >= 1:
                    dve.wait_ge(s.a_lo, f)
                dve.tensor_tensor(b.prod[:, 0:T], ps[:, gate_bank(f) + 1, 0:T], b.sil[:, f % 2, 0:T], ALU.mult).then_inc(s.prod_done, 1)
                dve.wait_ge(s.a_hi, f + 1)
                dve.tensor_tensor(b.act_lo[:, f, 0:T], b.prod[:, 0:T], b.act_hi[:, f, 0:T].bitcast(F32), ALU.subtract).then_inc(s.a_lo, 1)
                if before and 2 <= f < 2 + before.n:
                    k = f - 2
                    dve.wait_ge(s.rstd, k + 1)
                    dve.scalar_tensor_tensor(out=before.x[:, k, :], in0=before.x[:, k, :], scalar=b.rstd[:, k:k + 1], in1=b.gain_f[:],
                                             op0=ALU.mult, op1=ALU.mult).then_inc(s.normed, 1)
            for f in range(FT):
                split_lo(2 * FT + f)
                if following:
                    for k in range(following.n):
                        if f == squared_at(k) + 1:
                            dve.wait_ge(s.n_rstd, k + 1)
                            dve.scalar_tensor_tensor(out=b.xn[:, k % 2, :], in0=following.x[:, k, :], scalar=b.n_rstd[:, k:k + 1], in1=b.gain2[:],
                                                     op0=ALU.mult, op1=ALU.mult).then_inc(s.n_normed, 1)
                        for j in range(2):
                            if f == turned_at(k, j):
                                dve.wait_ge(s.n_hi, 2 * k + j + 1)
                                part = b.h_hi[:, 4 * j:4 * j + 4, k * P:(k + 1) * P]
                                dve.tensor_tensor(b.h_lo[:, 4 * j:4 * j + 4, k * P:(k + 1) * P], ps[:, 6 + j, :].rearrange("p (d t) -> p d t", d=4),
                                                  part.bitcast(F32), ALU.subtract).then_inc(s.n_lo, 1)

        @block.tensor
        def _(pe):
            def item(i):
                if i >= AHEAD:
                    pe.wait_ge(s.w_lo, i - AHEAD + 1)
                return w.hi[:, i % RING, :], w.lo[:, i % RING, :]

            for f in range(FT):
                if f == 1 and before:
                    pe.wait_ge(s.res, 1)
                if f >= 2:
                    pe.wait_ge(s.prod_done, f - 1)
                for u in range(2):
                    hi, lo = item(2 * f + u)
                    out = ps[:, gate_bank(f) + u, 0:T]
                    for d in range(DT):
                        a_hi, a_lo = hi[:, d * P:(d + 1) * P], lo[:, d * P:(d + 1) * P]
                        pe.matmul(out, a_hi, b.h_hi[:, d, 0:T], start=(d == 0), stop=False)
                        pe.matmul(out, a_hi, b.h_lo[:, d, 0:T], start=False, stop=False)
                        mm = pe.matmul(out, a_lo, b.h_hi[:, d, 0:T], start=False, stop=(d == DT - 1))
                    mm.then_inc(s.w_used, 1)
            for f in range(FT):
                if following:
                    for k in range(following.n):
                        for j in range(2):
                            if f == turned_at(k, j):
                                pe.wait_ge(s.n_normed, k + 1)
                                if k >= 1:
                                    pe.wait_ge(s.n_lo, 2 * (k - 1) + j + 1)
                                for d in range(4):
                                    turned = pe.transpose(ps[:, 6 + j, d * P:(d + 1) * P], b.xn[:, k % 2, (4 * j + d) * P:(4 * j + d + 1) * P], c.ident[:])
                                turned.then_inc(s.n_turned, 1)
                if f == 0 and before:
                    pe.wait_ge(s.res, before.n)
                hi, lo = item(2 * FT + f)
                pe.wait_ge(s.a_lo, f + 1)
                for k in range(n):
                    if f == 0 and k == 2:
                        pe.wait_ge(s.prod_done, FT)
                    for e in range(2):
                        out = ps[:, 2 * k + e, :]
                        cols = slice(e * BLK, (e + 1) * BLK)
                        a_hi, a_lo = b.act_hi[:, f, k * P:(k + 1) * P], b.act_lo[:, f, k * P:(k + 1) * P]
                        pe.matmul(out, a_hi, hi[:, cols], start=(f == 0), stop=False)
                        pe.matmul(out, a_hi, lo[:, cols], start=False, stop=False)
                        mm = pe.matmul(out, a_lo, hi[:, cols], start=False, stop=(f == FT - 1))
                mm.then_inc(s.w_used, 1)


def gate_bank(f):
    return 6 if f % 2 == 0 else 4


def finish(nc, c, b, ps, last):
    with stage(nc, "res squared var rstd normed stored") as (block, s):

        @block.vector
        def _(dve):
            for k in range(last.n):
                dve.tensor_tensor(last.x[:, k, :], ps[:, 2 * k:2 * k + 2, :].rearrange("p a n -> p (a n)"), last.x[:, k, :],
                                  ALU.add).then_inc(s.res, 1)
            for k in range(last.n):
                dve.wait_ge(s.rstd, k + 1)
                dve.scalar_tensor_tensor(out=last.x[:, k, :], in0=last.x[:, k, :], scalar=b.rstd[:, k:k + 1], in1=b.gain_f[:],
                                         op0=ALU.mult, op1=ALU.mult).then_inc(s.normed, 1)

        @block.scalar
        def _(act):
            for k in range(last.n):
                act.wait_ge(s.res, k + 1)
                act.activation(b.xn[:, k, :], last.x[:, k, :], ACT.Square, accum_out=b.ss[:, k:k + 1]).then_inc(s.squared, 1)

        @block.gpsimd
        def _(pool):
            for k in range(last.n):
                pool.wait_ge(s.squared, k + 1)
                pool.tensor_scalar(b.rstd[:, k:k + 1], b.ss[:, k:k + 1], 1.0 / D, EPS, ALU.mult, ALU.add).then_inc(s.var, 1)
                pool.wait_ge(s.var, k + 1)
                pool.tensor_tensor(b.rstd[:, k:k + 1], b.rstd[:, k:k + 1], c.minus_half[:], ALU.pow).then_inc(s.rstd, 1)

        @block.sync
        def _(sp):
            for k in range(last.n):
                sp.wait_ge(s.normed, k + 1)
                sp.dma_start(last.dst(k), last.x[0:last.rows(k), k, :]).then_inc(s.stored, 16)
            sp.wait_ge(s.stored, 16 * last.n)


class PromptTiles:

    def __init__(self, sb, conv_w, scratch, first):
        self.gate = sb("conv_gate", [P, SLOTS, CW])
        self.ch = sb("conv_c_h", [P, SLOTS, 3, 2 * CW])
        self.u = sb("conv_u", [P, 3, CW])
        self.sum = sb("conv_sum", [P, CW])
        self.w, self.scratch, self.first = conv_w, scratch, first

    def load(self, sp, s, k, y, parts, fox):
        row = (self.first + k) * P
        proj = self.scratch.proj
        if k >= SLOTS:
            sp.wait_ge(s.normed, k - SLOTS + 1)
        sp.dma_start(self.gate[:, k % SLOTS, :], proj[ds(row + PAD, P), 0:CW]).then_inc(parts, 16)
        for back in range(3):
            sp.dma_start(self.ch[:, k % SLOTS, back, :], proj[ds(row + PAD - back, P), CW:3 * CW]).then_inc(parts, 16)
        sp.dma_start(y[:, k % SLOTS, CW:CW + FW], self.scratch.fox[ds(row, P), :]).then_inc(fox, 16)
        sp.dma_start(y[:, k % SLOTS, CW + FW:D], self.scratch.mem[ds(row, P), :]).then_inc(fox, 16)

    def ready(self, act, s, k, fox):
        act.wait_ge(fox, 32 * (k // SLOTS + 1))

    def conv(self, pool, s, k, y, parts):
        steps = 4 * k
        pool.wait_ge(parts, 64 * (k // SLOTS + 1))
        pool.tensor_tensor(self.u[:], self.ch[:, k % SLOTS, :, 0:CW], self.ch[:, k % SLOTS, :, CW:2 * CW], ALU.mult).then_inc(s.conv_step, 1)
        pool.wait_ge(s.conv_step, steps + 1)
        pool.tensor_tensor(self.u[:], self.u[:], self.w[:], ALU.mult).then_inc(s.conv_step, 1)
        pool.wait_ge(s.conv_step, steps + 2)
        pool.tensor_tensor(self.sum[:], self.u[:, 2, :], self.u[:, 1, :], ALU.add).then_inc(s.conv_step, 1)
        pool.wait_ge(s.conv_step, steps + 3)
        pool.tensor_tensor(self.sum[:], self.sum[:], self.u[:, 0, :], ALU.add).then_inc(s.conv_step, 1)
        pool.wait_ge(s.conv_step, steps + 4)
        pool.tensor_tensor(y[:, k % SLOTS, 0:CW], self.sum[:], self.gate[:, k % SLOTS, :], ALU.mult).then_inc(s.conv, 1)


class SampleTile:

    def __init__(self, src):
        self.src = src

    def load(self, sp, s, k, y, parts, fox):
        sp.wait_ge(s.conv, 1)
        sp.dma_start(y[0:DB, 0, :], self.src).then_inc(fox, 16)

    def ready(self, act, s, k, fox):
        act.wait_ge(fox, 16)

    def conv(self, pool, s, k, y, parts):
        pool.memset(y[:, 0, :], 0.0).then_inc(s.conv, 1)


def sample_outputs(nc, io, scratch, dec, conv_w, y, parts, also):
    with ExitStack() as ctx:
        sb, _ = alloc(ctx, nc)
        rows = sb("rows", [P, PW])
        fox = sb("fox_rows", [P, FW])
        state = sb("state", [P, 3, CW])
        u = sb("weighted", [P, 3, CW])
        new = sb("new_value", [P, FW])
        last = sb("last_c_h", [P, 2 * CW])
        last_u = sb("last_u", [P, CW])
        with stage(nc, "w_in0 w_in1 w_in2 w_in3 hi_done also loaded chain stored") as (block, s):
            w_in = (s.w_in0, s.w_in1, s.w_in2, s.w_in3)

            @block.sync
            def _(sp):
                sp.dma_start(rows[0:DB, :], scratch.samp).then_inc(s.loaded, 16)
                sp.dma_start(fox[0:DB, :], scratch.samp_fox).then_inc(s.loaded, 16)
                sp.dma_start(state[0:DB, 0:2, :], io.state_conv.rearrange("l b k c -> (l b) k c")).then_inc(s.loaded, 16)
                sp.dma_start(last[0:PAD, :], scratch.proj[SEQ:SEQ + PAD, CW:3 * CW]).then_inc(s.loaded, 16)
                for dst, src in also:
                    sp.dma_start(dst, src).then_inc(s.also, 16)
                load_parts(sp, parts, w_in)
                sp.wait_ge(s.chain, 8)
                sp.dma_start(io.new_conv_s.rearrange("b k c -> b k c"), state[0:DB, 1:3, :]).then_inc(s.stored, 16)
                sp.dma_start(io.new_conv, last_u[0:PAD, :]).then_inc(s.stored, 16)
                sp.dma_start(scratch.samp_y, y[0:DB, :]).then_inc(s.stored, 16)
                sp.wait_ge(s.stored, 48)

            @block.scalar
            def _(act):
                split_parts_hi(act, parts, w_in, s.hi_done)

            @block.vector
            def _(dve):
                chain = [0]

                def link(ins):
                    chain[0] += 1
                    ins.then_inc(s.chain, 1)
                    dve.wait_ge(s.chain, chain[0])

                heads = [DB, FH, HD]
                dve.wait_ge(s.loaded, 64)
                dve.wait_ge(s.also, 16 * len(also))
                dve.tensor_tensor(last_u[0:PAD, :], last[0:PAD, 0:CW], last[0:PAD, CW:], ALU.mult)
                link(dve.tensor_tensor(state[0:DB, 2, :], rows[0:DB, CW:2 * CW], rows[0:DB, 2 * CW:3 * CW], ALU.mult))
                for back in range(3):
                    done = dve.tensor_tensor(u[0:DB, back, :], state[0:DB, 2 - back, :], conv_w[0:DB, back, :], ALU.mult)
                link(done)
                link(dve.tensor_tensor(u[0:DB, 2, :], u[0:DB, 2, :], u[0:DB, 1, :], ALU.add))
                link(dve.tensor_tensor(u[0:DB, 2, :], u[0:DB, 2, :], u[0:DB, 0, :], ALU.add))
                link(dve.tensor_tensor(y[0:DB, 0:CW], u[0:DB, 2, :], rows[0:DB, 0:CW], ALU.mult))
                link(dve.tensor_tensor(new[0:DB, :].rearrange("p (h d) -> p h d", d=HD), rows[0:DB, VCOL:VCOL + FW].rearrange("p (h d) -> p h d", d=HD),
                                       dec.w_new[0:DB, :].unsqueeze(2).to_broadcast(heads), ALU.mult))
                link(dve.tensor_tensor(new[0:DB, :], new[0:DB, :], fox[0:DB, :], ALU.add))
                link(dve.tensor_tensor(y[0:DB, CW:CW + FW].rearrange("p (h d) -> p h d", d=HD), new[0:DB, :].rearrange("p (h d) -> p h d", d=HD),
                                       dec.r_fox[0:DB, :].unsqueeze(2).to_broadcast(heads), ALU.mult))
                split_parts_lo(dve, parts, s.hi_done)


def load(nc, pairs):
    with stage(nc, "loaded") as (block, s):

        @block.sync
        def _(sp):
            for dst, src in pairs:
                sp.dma_start(dst, src).then_inc(s.loaded, 16)
            sp.wait_ge(s.loaded, 16 * len(pairs))


def decoder_step(nc, io):
    def dram(name, shape):
        return nc.dram_tensor(name, shape, F32, kind="Internal").ap()

    scratch = group(proj=io.proj, samp=io.samp, gates=dram("gate_logits", (FH, SEQ + P)), neg_cum=dram("neg_cum", (FH, SEQ)), fox=dram("fox", (SEQ, FW)),
                              mem=dram("mem", (SEQ, MW)), x1=dram("x1", (SEQ, D)), samp_fox=dram("samp_fox", (DB, FW)),
                              samp_y=dram("samp_y", (DB, D)), samp_x1=dram("samp_x1", (DB, D)))
    w_in = io.w_in.rearrange("(d p) n -> p d n", p=P)
    w_mem = io.w_mem_kv.rearrange("(d p) n -> p d n", p=P)
    last_page = io.cache_k.shape[1] - 1
    key_pages = io.cache_k.rearrange("l n r h d -> (l n) r (h d)")
    value_pages = io.cache_v.rearrange("l n r h d -> (l n) r (h d)")

    with ExitStack() as whole:
        sb, _ = alloc(whole, nc)
        c = group(ident=sb("ident", [P, P]), ident_r=sb("ident_r", [P, P], F32R), causal_r=sb("causal_r", [P, P], F32R),
                            page_before=sb("page_before", [P, P]), seq_of_page=sb("seq_of_page", [P, 2, DB]),
                            own_head=sb("own_head", [P, FW]), fold=sb("fold", [P, HD]), ones=sb("ones", [P, 1]),
                            minus_half=sb("minus_half", [P, 1]), b_f=sb("b_f", [P, 1]), pages=sb("pages", [1, DB * PAGES], I32),
                            page_index=sb("page_index", [P, 2], U32),
                  gathered=whole.enter_context(nc.semaphore("gathered")))
        early = whole.enter_context(ExitStack())
        early_sb, _ = alloc(early, nc)
        y_samp = early_sb("y_samp", [P, D])
        dec = group(scores=early_sb("scores", [P, DB * PAGES * FH]), mem_scores=early_sb("mem_scores", [P, DB * 2 * MH]),
                              logf_new=early_sb("logf_new", [P, FH]), w_new=early_sb("w_new", [P, FH]), r_fox=early_sb("r_fox", [P, FH]), r_mem=early_sb("r_mem", [P, MH]))
        setup_constants(nc, c, io)

        with ExitStack() as ctx:
            sb, _ = alloc(ctx, nc)
            h_hi = sb("h_hi", [P, DT, HALF * P], F32R)
            h_lo = sb("h_lo", [P, DT, HALF * P], F32R)
            w = group(raw=sb("w_raw", [P, DT, BLK]), hi=sb("w_hi", [P, 2, DT, BLK], F32R), lo=sb("w_lo", [P, 2, DT, BLK], F32R))
            wf_hi = sb("wf_hi", [P, DT, P], F32R)
            wf_lo = sb("wf_lo", [P, DT, P], F32R)
            with ExitStack() as inner:
                gain = inner.enter_context(nc.sbuf_tensor("gain_mem", [P, D], F32))
                zero = inner.enter_context(nc.sbuf_tensor("zero_rows", [PAD, 2 * CW], F32))
                with stage(nc, "zeroed stored") as (block, s):

                    @block.gpsimd
                    def _(pool):
                        pool.memset(zero[:], 0.0).then_inc(s.zeroed, 1)

                    @block.sync
                    def _(sp):
                        sp.wait_ge(s.zeroed, 1)
                        sp.dma_start(scratch.proj[0:PAD, CW:3 * CW], zero[:]).then_inc(s.stored, 16)
                        sp.wait_ge(s.stored, 16)
                split_weights(nc, weight_parts(w.raw[:], w.hi[:, 1], w.lo[:, 1], w_mem), also=[(gain[:], io.mem_norm_g.to_broadcast([P, D]))])
                norm_transpose(nc, c, 2, lambda k: io.mem_prompt[k * P:(k + 1) * P, :], gain[:], h_hi, h_lo)

            def block_columns(n):
                return lambda j: [(w.raw[:, 2 * j:2 * j + 2, 0:CW], w_in[:, 2 * j:2 * j + 2, ds(n * BLK, CW)]),
                                  (w.raw[:, 2 * j:2 * j + 2, CW:BLK], w_in[:, 2 * j:2 * j + 2, ds(n * BLK + CW + (n // (NBLK - 1)) * FH, CW)])]

            project(nc, c, 2, h_hi, h_lo, w, 1, lambda t: io.mem_kv[t * P:(t + 1) * P, :], block_columns(0))
            gain = sb("gain1", [P, D])
            split_weights(nc, weight_parts(w.raw[:, :, 0:P], wf_hi[:], wf_lo[:], w_in[:, :, FCOL:FCOL + P]),
                          also=[(gain[:], io.norm1_g.to_broadcast([P, D]))])
            norm_transpose(nc, c, 1, lambda k: io.x_sample[:, :], gain[:], h_hi, h_lo, rows=DB, gates=(wf_hi, wf_lo, scratch.gates[:, SEQ:]))
            with nc.Fori(0, NBLK) as n:
                project(nc, c, 1, h_hi, h_lo, w, n % 2, lambda t: scratch.samp[:, ds(n * BLK, BLK)],
                        block_columns((n + 1) % NBLK), rows=DB)
            for half in range(2):
                first = half * HALF
                norm_transpose(nc, c, HALF, lambda k: io.x_prompt[(first + k) * P:(first + k + 1) * P, :], gain[:], h_hi, h_lo,
                               gates=(wf_hi, wf_lo, scratch.gates[:, first * P:(first + HALF) * P]))
                for n0, n1 in ((0, NBLK),) if half == 0 else ((0, DB - NBLK), (DB - NBLK, NBLK)):
                    with nc.Fori(n0, n1) as n:
                        seq = n + half * NBLK
                        keys = None
                        if n0 == 0:
                            keys = group(seq=seq, scores=dec.scores, cache=key_pages, last_page=last_page,
                                                   query=scratch.samp[ds(seq, 1), QCOL:QCOL + FW].to_broadcast([P, FW]))
                        project(nc, c, HALF, h_hi, h_lo, w, (n + half + 1) % 2,
                                lambda t: scratch.proj[PAD + (first + t) * P:PAD + (first + t + 1) * P, ds(n * BLK, BLK)],
                                block_columns((n + 1) % NBLK), keys=keys)
        with ExitStack() as ctx:
            sb, _ = alloc(ctx, nc)
            gates = sb("gates2", [P, SEQ + P])
            load(nc, [(gates[0:FH, :], scratch.gates)])
            forget_gates(nc, c, gates, io, scratch, dec)

        def fox_head(h):
            return group(q=scratch.proj[PAD:, ds(h * HD + QCOL, HD)], k=scratch.proj[PAD:, ds(h * HD + KCOL, HD)],
                         v=scratch.proj[PAD:, ds(h * HD + VCOL, HD)], neg_cum=scratch.neg_cum[ds(h, 1), :])

        def mem_head(h):
            return group(q=scratch.proj[PAD:, ds(h * HD + MCOL, HD)], k=io.mem_kv[:, ds(h * HD, HD)],
                         v=io.mem_kv[:, ds(h * HD + MW, HD)], neg_cum=None)

        with ExitStack() as ctx:
            sb, _ = alloc(ctx, nc)
            raw = group(q=sb("q_raw", [P, NT, 2, HD]), k=sb("k_raw", [P, NT, 2, HD]), v=sb("v_raw", [P, NT, HD]),
                        neg_cum=sb("neg_cum_all", [P, SEQ]), zeros=sb("zeros", [P, MEM]))
            with ExitStack() as inner:
                mem_v = inner.enter_context(nc.sbuf_tensor("mem_v", [P, DB, 2, MW], F32))
                decode_softmax(nc, c, io, scratch, dec, raw, fox_head(0), mem_v)
                decode_memory_values(nc, c, dec, mem_v, y_samp[:, CW + FW:D])
            a = group(q=raw.q, k=raw.k, v=raw.v, neg_cum=raw.neg_cum, zeros=raw.zeros, k_st=sb("k_stacked", [P, SEQ], F32R),
                      q_hi=sb("q_hi", [P, SEQ], F32R), q_lo=sb("q_lo", [P, SEQ], F32R), v_st=sb("v_stacked", [P, NT, P], F32R),
                      probs=sb("probs", [P, 2, QCH, SEQ]), p_hi=sb("p_hi", [P, 2, BLK], F32R), p_lo=sb("p_lo", [P, 2, BLK], F32R),
                      o_t=sb("o_turned", [P, 2, BLK]), o_out=sb("o_out", [P, QCH, QCH, HD]), low=sb("low", [P, NT]),
                      low2=sb("low2", [P, 2, NT]), sums=sb("row_sums", [P, NT]), inv=sb("inverse", [P, NT]),
                      w_st=sb("page_weights", [P, PAGES * 2 * FH + P - 2 * FH], F32R))
            page_v = sb("page_v", [P, 4, FW])
            page_hi = sb("page_hi", [P, 3, FW], F32R)
            page_lo = sb("page_lo", [P, 3, FW], F32R)
            own = sb("own", [P, FW])
            row = sb("row", [P, FW])

            attend(nc, c, a, NT, True, None, None, opening=True)
            with nc.Fori(0, FH) as h:
                values = group(seq=h, cache=value_pages, last_page=last_page, page_v=page_v, page_hi=page_hi, page_lo=page_lo, own=own, row=row,
                                         all_weights=dec.scores[:, ds(h * (PAGES * FH), PAGES * FH)], dst=scratch.samp_fox[ds(h, 1), :])
                attend(nc, c, a, NT, True, fox_head((h + 1) % FH),
                       lambda ch: scratch.fox[ch * BLK:(ch + 1) * BLK, ds(h * HD, HD)].rearrange("(r p) d -> p r d", p=P), values)
            with stage(nc, "loaded doubled") as (block, s):

                @block.sync
                def _(sp):
                    load_head(sp, a, mem_head(0), 2, s.loaded)

                @block.gpsimd
                def _(pool):
                    pool.wait_ge(s.loaded, 48)
                    for part in double_parts(2):
                        double(pool, a, 2, part, s.doubled)
            attend(nc, c, a, 2, False, None, None, opening=True)
            with nc.Fori(0, MH) as h:
                attend(nc, c, a, 2, False, mem_head((h + 1) % MH),
                       lambda ch: scratch.mem[ch * BLK:(ch + 1) * BLK, ds(h * HD, HD)].rearrange("(r p) d -> p r d", p=P))

        with ExitStack() as ctx:
            sb, _ = alloc(ctx, nc)
            w = group(hi=sb("wo_hi", [P, DT, D], F32R), lo=sb("wo_lo", [P, DT, D], F32R))
            gain = sb("gain_out", [P, D])
            conv_w = sb("conv_w", [P, 3, CW])
            with ExitStack() as inner:
                raw = inner.enter_context(nc.sbuf_tensor("wo_raw", [P, DT, D], F32))
                sample_outputs(nc, io, scratch, dec, conv_w, y_samp,
                               weight_parts(raw[:], w.hi[:], w.lo[:], io.w_out.rearrange("(d p) n -> p d n", p=P)),
                               [(gain[:], io.out_norm_g.to_broadcast([P, D]))] +
                               [(conv_w[:, back, :], io.conv_w[2 - back:3 - back, :].to_broadcast([P, CW])) for back in range(3)])
            mix(nc, c, 1, w, gain, SampleTile(scratch.samp_y), lambda k: io.x_sample, lambda k: scratch.samp_x1, rows=DB)
            with nc.Fori(0, NT // HALF) as half:
                with ExitStack() as inner:
                    tiles = PromptTiles(alloc(inner, nc)[0], conv_w, scratch, half * HALF)
                    mix(nc, c, HALF, w, gain, tiles, lambda k: io.x_prompt[ds((half * HALF + k) * P, P), :],
                        lambda k: scratch.x1[ds((half * HALF + k) * P, P), :])

        early.close()

        with ExitStack() as ctx:
            sb, psum = alloc(ctx, nc)
            T = FCH * P
            x1 = sb("x1_tiles", [P, 2, FCH, D])
            h_hi, h_lo = sb("h2_hi", [P, DT, T], F32R), sb("h2_lo", [P, DT, T], F32R)
            gain2, gain_f = sb("gain2", [P, D]), sb("gain_f", [P, D])
            w = group(raw=sb("w_items", [P, RING, D]), hi=sb("w_items_hi", [P, RING, D], F32R), lo=sb("w_items_lo", [P, RING, D], F32R))

            def chunk(ch):
                return group(n=FCH, x=x1[:, ch % 2], rows=lambda k: P,
                             src=lambda k: scratch.x1[ds((ch * FCH + k) * P, P), :], dst=lambda k: io.y_prompt[ds((ch * FCH + k) * P, P), :])

            left = NT - FULL * FCH
            last = group(n=left + 1, x=x1[:, FULL % 2], rows=lambda k: P if k < left else DB,
                         src=lambda k: scratch.x1[(FULL * FCH + k) * P:(FULL * FCH + k + 1) * P, :] if k < left else scratch.samp_x1,
                         dst=lambda k: io.y_prompt[(FULL * FCH + k) * P:(FULL * FCH + k + 1) * P, :] if k < left else io.y_sample)
            split_weights(nc, [(w.raw[:, i, :], w.hi[:, i, :], w.lo[:, i, :], [(weight_slot(w, i), weight_source(io, i))]) for i in range(AHEAD)],
                          also=[(gain2[:], io.norm2_g.to_broadcast([P, D])), (gain_f[:], io.final_norm_g.to_broadcast([P, D]))])
            norm_transpose(nc, c, FCH, chunk(0).src, gain2[:], h_hi, h_lo, keep=x1[:, 0])
            b = group(h_hi=h_hi, h_lo=h_lo, gain2=gain2, gain_f=gain_f, act_hi=sb("act_hi", [P, FT, T], F32R), act_lo=sb("act_lo", [P, FT, T], F32R),
                      sil=sb("silu", [P, 2, T]), prod=sb("silu_up", [P, T]), xn=sb("x_normed", [P, 2, D]), ss=sb("sum_squares", [P, FCH]),
                      rstd=sb("rstd", [P, FCH]), n_ss=sb("next_sum_squares", [P, FCH]), n_rstd=sb("next_rstd", [P, FCH]))
            ps = psum("ps_ffn", [P, 8, BLK])
            ffn(nc, c, FCH, b, w, ps, io, following=chunk(1))
            with nc.Fori(1, FULL - 1) as ch:
                ffn(nc, c, FCH, b, w, ps, io, before=chunk(ch - 1), following=chunk(ch + 1))
            ffn(nc, c, FCH, b, w, ps, io, before=chunk(FULL - 2), following=last)
            ffn(nc, c, last.n, b, w, ps, io, before=chunk(FULL - 1))
            finish(nc, c, b, ps, last)


_INS = ["x_prompt", "x_sample", "mem_prompt", "cache_k", "cache_v", "cache_logf", "state_conv", "cache_mem_k", "cache_mem_v",
        "page_table", "norm1_g", "w_in", "b_f", "conv_w", "mem_norm_g", "w_mem_kv", "out_norm_g", "w_out", "norm2_g",
        "w_gate", "w_up", "w_down", "final_norm_g"]
_OUTS = {"y_prompt": (SEQ, D), "y_sample": (DB, D), "proj": (PAD + SEQ, PW), "samp": (DB, PW), "mem_kv": (MEM, 2 * MW),
         "new_logf": (SEQ, FH), "new_logf_s": (DB, FH), "new_conv": (PAD, CW), "new_conv_s": (DB, PAD, CW)}
_FLAT = {"x_prompt": (SEQ, D), "x_sample": (DB, D), "mem_prompt": (MEM, D), "w_in": None, "conv_w": None, "w_mem_kv": None,
         "w_out": None, "w_gate": None, "w_up": None, "w_down": None, "final_norm_g": (1, D)}


def kernel(**inputs):
    import numpy as np
    import concourse.bacc as bacc
    from concourse.bass_utils import run_bass_kernel_spmd

    nc = bacc.Bacc("TRN2", target_bir_lowering=False, num_devices=1)
    arrays, io = {}, {}
    for name in _INS:
        a = np.ascontiguousarray(inputs[name])
        if name in _FLAT:
            a = a.reshape(_FLAT[name] or a.shape[1:])
        arrays[f"in_{name}"] = a
        io[name] = nc.dram_tensor(f"in_{name}", a.shape, mybir.dt.from_np(a.dtype), kind="ExternalInput").ap()
    for name, shape in _OUTS.items():
        io[name] = nc.dram_tensor(f"out_{name}", shape, F32, kind="ExternalOutput").ap()
    decoder_step(nc, group(**io))
    r = run_bass_kernel_spmd(nc, [arrays], core_ids=[0]).results[0]
    out = {name: r[f"out_{name}"] for name in _OUTS}
    proj, samp, mem_kv = out["proj"][PAD:], out["samp"], out["mem_kv"]
    heads = (1, 1, SEQ, FH, HD)
    sample_heads = (1, DB, 1, FH, HD)
    return (out["y_prompt"].reshape(1, SEQ, D), out["y_sample"].reshape(DB, 1, D),
            proj[:, KCOL:KCOL + FW].reshape(heads), proj[:, VCOL:VCOL + FW].reshape(heads),
            out["new_logf"].reshape(1, 1, SEQ, FH), out["new_conv"].reshape(1, 1, PAD, CW),
            mem_kv[:, 0:MW].reshape(1, 1, MEM, MH, HD), mem_kv[:, MW:].reshape(1, 1, MEM, MH, HD),
            samp[:, KCOL:KCOL + FW].reshape(sample_heads), samp[:, VCOL:VCOL + FW].reshape(sample_heads),
            out["new_logf_s"].reshape(1, DB, 1, FH), out["new_conv_s"].reshape(1, DB, PAD, CW))
```
